# Optimizing a Trainium2 kernel written in Bass

```python
import math
import jax, jax.numpy as jnp
from jax import lax
import numpy as np

D_MODEL = 1024
BATCH = 1
SEQ = 512
DEPTH = 2

D_MIX = D_MODEL
W_CONV = D_MIX // 4
W_GLA = D_MIX // 4
W_MLA = D_MIX // 4
W_CFM = D_MIX // 4
SC_WIDTH = 3
GLA_HEADS = 4
GLA_DV = W_GLA // GLA_HEADS
GLA_DK = GLA_DV // 2
GLA_LOWRANK = 16
GLA_TAU = 16.0
GLA_CHUNK = 64
MLA_HEADS = 4
MLA_V_DIM = W_MLA // MLA_HEADS
MLA_NOPE = 64
MLA_ROPE = 32
MLA_Q_RANK = 256
MLA_KV_RANK = 128
ROPE_BASE = 10000.0
Q_BLOCK = 128
CFM_WIDTH = 31
D_FF = 2816
FFN_CONV_WIDTH = 3
DN_ALPHA = (2.0 * DEPTH) ** 0.25
DN_BETA = (8.0 * DEPTH) ** -0.25
EPS = 1e-5

SPLIT_SIZES = (
    W_CONV, W_CONV, W_CONV,
    GLA_HEADS * GLA_DK, GLA_HEADS * GLA_DK, W_GLA, W_GLA,
    GLA_LOWRANK, GLA_LOWRANK,
    MLA_Q_RANK, MLA_KV_RANK, MLA_ROPE,
    2 * W_CFM,
)
D_IN = sum(SPLIT_SIZES)


def _split_points():
    pts, acc = [], 0
    for s in SPLIT_SIZES[:-1]:
        acc += s
        pts.append(acc)
    return pts

def layer_norm(x, g, b):
    xf = x.astype(jnp.float32)
    mu = jnp.mean(xf, axis=-1, keepdims=True)
    var = jnp.mean(jnp.square(xf - mu), axis=-1, keepdims=True)
    return ((xf - mu) * lax.rsqrt(var + EPS) * g.astype(jnp.float32) + b.astype(jnp.float32)).astype(x.dtype)

def rms_norm(x, g):
    xf = x.astype(jnp.float32)
    return (xf * lax.rsqrt(jnp.mean(xf * xf, axis=-1, keepdims=True) + EPS) * g.astype(jnp.float32)).astype(x.dtype)

def depthwise_conv(x, w):
    k, c = w.shape
    return lax.conv_general_dilated(
        x, w[:, None, :].astype(x.dtype), window_strides=(1,), padding=[(k // 2, k // 2)],
        dimension_numbers=('NWC', 'WIO', 'NWC'), feature_group_count=c)

def rope_tables(positions):
    inv = ROPE_BASE ** (-jnp.arange(0, MLA_ROPE, 2, dtype=jnp.float32) / MLA_ROPE)
    ang = positions.astype(jnp.float32)[..., None] * inv
    return jnp.cos(ang), jnp.sin(ang)

def apply_rope(x, cos, sin):
    half = MLA_ROPE // 2
    xf = x.astype(jnp.float32)
    x1, x2 = xf[..., :half], xf[..., half:]
    c, s = cos[:, :, None, :], sin[:, :, None, :]
    return jnp.concatenate([x1 * c - x2 * s, x1 * s + x2 * c], axis=-1).astype(x.dtype)

def gla_scan(q, k, v, log_a, include_diag):
    bsz, nh, s, dk = q.shape
    dv = v.shape[-1]
    n = s // GLA_CHUNK

    def chunks(t):
        return t.astype(jnp.float32).reshape(bsz, nh, n, GLA_CHUNK, t.shape[-1]).transpose(2, 0, 1, 3, 4)

    idx = jnp.arange(GLA_CHUNK)
    mask = (idx[:, None] >= idx[None, :]) if include_diag else (idx[:, None] > idx[None, :])
    mask5 = mask[None, None, :, :, None]

    def step(state, inp):
        qc, kc, vc, ac = inp
        b = jnp.cumsum(ac, axis=2)
        o_inter = jnp.einsum('bhtk,bhkv->bhtv', qc * jnp.exp(b), state)
        rel = b[:, :, :, None, :] - b[:, :, None, :, :]
        decay = jnp.where(mask5, jnp.exp(jnp.where(mask5, rel, 0.0)), 0.0)
        scores = jnp.einsum('bhtk,bhsk,bhtsk->bhts', qc, kc, decay)
        o = o_inter + jnp.einsum('bhts,bhsv->bhtv', scores, vc)
        b_last = b[:, :, -1:, :]
        state = jnp.exp(b_last[:, :, 0, :])[..., None] * state + \
            jnp.einsum('bhsk,bhsv->bhkv', kc * jnp.exp(b_last - b), vc)
        return state, o

    init = jnp.zeros((bsz, nh, dk, dv), jnp.float32)
    _, o = lax.scan(step, init, (chunks(q), chunks(k), chunks(v), chunks(log_a)))
    return o.transpose(1, 2, 0, 3, 4).reshape(bsz, nh, s, dv)

def blocked_attention(q, k, v, scale):
    bsz, s, nh, d = q.shape
    nb = s // Q_BLOCK
    qb = q.reshape(bsz, nb, Q_BLOCK, nh, d).transpose(1, 0, 2, 3, 4)

    def blk(qi):
        sc = jnp.einsum('bqhd,bkhd->bhqk', qi, k).astype(jnp.float32) * scale
        p = jax.nn.softmax(sc, axis=-1)
        return jnp.einsum('bhqk,bkhd->bqhd', p.astype(v.dtype), v)

    o = lax.map(blk, qb)
    return o.transpose(1, 0, 2, 3, 4).reshape(bsz, s, nh, v.shape[-1])

def token_mixers(h, cos, sin, w_in, w_sc_conv, w_gla_a_up, b_gla_a, g_gla_head, g_mla_q, w_mla_uq,
                 g_mla_kv, w_mla_ukv, w_cfm_dw, g_cfm_ln, b_cfm_ln, g_branch, w_out):
    bsz, s, _ = h.shape
    proj = h @ w_in
    (sc_b, sc_c, sc_h, gq, gk, gv, gg, ga_f, ga_b, cq, ckv, kr, cfm_in) = jnp.split(proj, _split_points(), axis=-1)

    y_a = sc_b * depthwise_conv(sc_c * sc_h, w_sc_conv)

    def heads(t, d):
        return t.reshape(bsz, s, GLA_HEADS, d).transpose(0, 2, 1, 3)

    q = heads(gq, GLA_DK) * (GLA_DK ** -0.5)
    k = heads(gk, GLA_DK)
    v = heads(gv, GLA_DV)
    la_f = heads(jax.nn.log_sigmoid((ga_f @ w_gla_a_up[0] + b_gla_a[0]).astype(jnp.float32)) / GLA_TAU, GLA_DK)
    la_b = heads(jax.nn.log_sigmoid((ga_b @ w_gla_a_up[1] + b_gla_a[1]).astype(jnp.float32)) / GLA_TAU, GLA_DK)
    flip = lambda t: jnp.flip(t, axis=2)
    o_f = gla_scan(q, k, v, la_f, True)
    o_b = flip(gla_scan(flip(q), flip(k), flip(v), flip(la_b), False))
    o = (o_f + o_b).transpose(0, 2, 1, 3)
    o = rms_norm(o, g_gla_head.reshape(GLA_HEADS, GLA_DV)).reshape(bsz, s, W_GLA)
    y_b = o.astype(h.dtype) * jax.nn.silu(gg)

    qm = (rms_norm(cq, g_mla_q) @ w_mla_uq).reshape(bsz, s, MLA_HEADS, MLA_NOPE + MLA_ROPE)
    q_c = jnp.concatenate([qm[..., :MLA_NOPE], apply_rope(qm[..., MLA_NOPE:], cos, sin)], axis=-1)
    kvm = (rms_norm(ckv, g_mla_kv) @ w_mla_ukv).reshape(bsz, s, MLA_HEADS, MLA_NOPE + MLA_V_DIM)
    k_rope = jnp.broadcast_to(apply_rope(kr[:, :, None, :], cos, sin), (bsz, s, MLA_HEADS, MLA_ROPE))
    k_c = jnp.concatenate([kvm[..., :MLA_NOPE], k_rope], axis=-1)
    v_c = kvm[..., MLA_NOPE:]
    y_c = blocked_attention(q_c, k_c, v_c, (MLA_NOPE + MLA_ROPE) ** -0.5).reshape(bsz, s, W_MLA)

    a, gate = jnp.split(cfm_in, 2, axis=-1)
    u = depthwise_conv(a * jax.nn.sigmoid(gate), w_cfm_dw)
    y_d = jax.nn.silu(layer_norm(u, g_cfm_ln, b_cfm_ln))

    gains = jnp.split(g_branch, [W_CONV, W_CONV + W_GLA, W_CONV + W_GLA + W_MLA])
    y = jnp.concatenate([rms_norm(yb, gb) for yb, gb in zip((y_a, y_b, y_c, y_d), gains)], axis=-1)
    return y @ w_out

def conv_ffn(h, w_up, w_dw, w_down):
    u = depthwise_conv(h @ w_up, w_dw)
    g, val = jnp.split(u, 2, axis=-1)
    return (jax.nn.silu(g) * val) @ w_down

def first_inputs(seed: int = 0) -> dict:
    key = jax.random.key(seed)
    ks = jax.random.split(key, 32)
    L = DEPTH
    nrm = lambda k, shape, scale: jax.random.normal(k, shape, jnp.float32) * scale
    gain = lambda k, shape: 1.0 + 0.02 * jax.random.normal(k, shape, jnp.float32)
    offsets = jax.random.randint(ks[1], (BATCH, 1), 0, SEQ, dtype=jnp.int32)
    positions = jnp.arange(SEQ, dtype=jnp.int32)[None, :] + offsets
    return {
        'x': jax.random.normal(ks[0], (BATCH, SEQ, D_MODEL), jnp.float32),
        'positions': positions,
        'ln_in_g': gain(ks[2], (D_MODEL,)),
        'ln_in_b': nrm(ks[3], (D_MODEL,), 0.02),
        'w_in': nrm(ks[4], (L, D_MODEL, D_IN), D_MODEL ** -0.5),
        'w_sc_conv': nrm(ks[5], (L, SC_WIDTH, W_CONV), SC_WIDTH ** -0.5),
        'w_gla_a_up': nrm(ks[6], (L, 2, GLA_LOWRANK, GLA_HEADS * GLA_DK), GLA_LOWRANK ** -0.5),
        'b_gla_a': nrm(ks[7], (L, 2, GLA_HEADS * GLA_DK), 0.02),
        'g_gla_head': gain(ks[8], (L, W_GLA)),
        'g_mla_q': gain(ks[9], (L, MLA_Q_RANK)),
        'w_mla_uq': nrm(ks[10], (L, MLA_Q_RANK, MLA_HEADS * (MLA_NOPE + MLA_ROPE)), MLA_Q_RANK ** -0.5),
        'g_mla_kv': gain(ks[11], (L, MLA_KV_RANK)),
        'w_mla_ukv': nrm(ks[12], (L, MLA_KV_RANK, MLA_HEADS * (MLA_NOPE + MLA_V_DIM)), MLA_KV_RANK ** -0.5),
        'w_cfm_dw': nrm(ks[13], (L, CFM_WIDTH, W_CFM), CFM_WIDTH ** -0.5),
        'g_cfm_ln': gain(ks[14], (L, W_CFM)),
        'b_cfm_ln': nrm(ks[15], (L, W_CFM), 0.02),
        'g_branch': gain(ks[16], (L, D_MIX)),
        'w_out': nrm(ks[17], (L, D_MIX, D_MODEL), DN_BETA * D_MIX ** -0.5),
        'ln1_g': gain(ks[18], (L, D_MODEL)),
        'ln1_b': nrm(ks[19], (L, D_MODEL), 0.02),
        'w_ffn_up': nrm(ks[20], (L, D_MODEL, 2 * D_FF), D_MODEL ** -0.5),
        'w_ffn_dw': nrm(ks[21], (L, FFN_CONV_WIDTH, 2 * D_FF), FFN_CONV_WIDTH ** -0.5),
        'w_ffn_down': nrm(ks[22], (L, D_FF, D_MODEL), DN_BETA * D_FF ** -0.5),
        'ln2_g': gain(ks[23], (L, D_MODEL)),
        'ln2_b': nrm(ks[24], (L, D_MODEL), 0.02),
    }

def first_block(x, positions, ln_in_g, ln_in_b, w_in, w_sc_conv, w_gla_a_up, b_gla_a, g_gla_head, g_mla_q,
              w_mla_uq, g_mla_kv, w_mla_ukv, w_cfm_dw, g_cfm_ln, b_cfm_ln, g_branch, w_out, ln1_g, ln1_b,
              w_ffn_up, w_ffn_dw, w_ffn_down, ln2_g, ln2_b):
    cos, sin = rope_tables(positions)
    h = layer_norm(x, ln_in_g, ln_in_b)
    for l in range(DEPTH):
        mix = token_mixers(h, cos, sin, w_in[l], w_sc_conv[l], w_gla_a_up[l], b_gla_a[l], g_gla_head[l],
                           g_mla_q[l], w_mla_uq[l], g_mla_kv[l], w_mla_ukv[l], w_cfm_dw[l], g_cfm_ln[l],
                           b_cfm_ln[l], g_branch[l], w_out[l])
        h = layer_norm(DN_ALPHA * h + mix, ln1_g[l], ln1_b[l])
        h = layer_norm(DN_ALPHA * h + conv_ffn(h, w_ffn_up[l], w_ffn_dw[l], w_ffn_down[l]), ln2_g[l], ln2_b[l])
    return h


CHUNK = 64
N_MEM = 256
ROPE_THETA = 10000.0
LN_EPS = 1e-5

POOL_GROUPS = 4
POOL_GROUP_DIM = 128
POOL_WINDOWS = (2, 4, 8, 16)
POOL_WIDTH = POOL_GROUPS * POOL_GROUP_DIM
ATT_HEADS = 8
ATT_HEAD_DIM = 64
ATT_WIDTH = ATT_HEADS * ATT_HEAD_DIM
IDX_HEADS = 8
IDX_HEAD_DIM = 64
TOPK_MAX = 256
MEM_HEADS = 4
MEM_HEAD_DIM = 128
MEM_WIDTH = MEM_HEADS * MEM_HEAD_DIM
N_BRANCH = 3
BRANCH_WIDTH = 512
IN_WIDTHS = (POOL_WIDTH, ATT_WIDTH, ATT_WIDTH, ATT_WIDTH, IDX_HEADS * IDX_HEAD_DIM,
             IDX_HEAD_DIM, IDX_HEADS, MEM_WIDTH, N_BRANCH * D_MODEL)
D_IN_2 = sum(IN_WIDTHS)
N_EXPERTS = 16
N_GROUPS = 4
EXPERTS_PER_GROUP = N_EXPERTS // N_GROUPS
TOP_K_EXPERTS = 2
GROUP_SCORE_TOPK = 2
D_EXPERT = 512
MOE_BLOCK = 128
DN_ALPHA_2 = (2 * DEPTH) ** 0.25
DN_BETA_2 = (8 * DEPTH) ** -0.25


def layer_norm_2(x, g, b):
    xf = x.astype(jnp.float32)
    mu = jnp.mean(xf, axis=-1, keepdims=True)
    var = jnp.mean(jnp.square(xf - mu), axis=-1, keepdims=True)
    y = (xf - mu) * lax.rsqrt(var + LN_EPS) * g.astype(jnp.float32) + b.astype(jnp.float32)
    return y.astype(x.dtype)

def rotary(x, positions):
    half = x.shape[-1] // 2
    inv_freq = ROPE_THETA ** (-jnp.arange(half, dtype=jnp.float32) / half)
    ang = positions.astype(jnp.float32)[..., None] * inv_freq
    cos = jnp.cos(ang)[:, :, None, :]
    sin = jnp.sin(ang)[:, :, None, :]
    xf = x.astype(jnp.float32)
    x1, x2 = xf[..., :half], xf[..., half:]
    out = jnp.concatenate([x1 * cos - x2 * sin, x2 * cos + x1 * sin], axis=-1)
    return out.astype(x.dtype)

def pool_branch(u, pool_w, pool_scale):
    B, S, _ = u.shape
    u = u.reshape(B, S, POOL_GROUPS, POOL_GROUP_DIM)
    t = jnp.arange(S)
    outs = []
    for g, w in enumerate(POOL_WINDOWS):
        ug = u[:, :, g].astype(jnp.float32)
        cs = jnp.cumsum(ug, axis=1)
        lagged = jnp.pad(cs, ((0, 0), (w, 0), (0, 0)))[:, :S]
        cnt = jnp.minimum(t + 1, w).astype(jnp.float32)[None, :, None]
        outs.append((cs - lagged) / cnt - ug)
    d = jnp.stack(outs, axis=2).astype(u.dtype)
    mixed = jnp.einsum('bsgc,gce->bsge', d, pool_w).reshape(B, S, POOL_WIDTH)
    return mixed * pool_scale

def dsa_branch(q, k, v, iq, ik, iw, positions):
    B, S, _ = q.shape
    q = rotary(q.reshape(B, S, ATT_HEADS, ATT_HEAD_DIM), positions)
    k = rotary(k.reshape(B, S, ATT_HEADS, ATT_HEAD_DIM), positions)
    v = v.reshape(B, S, ATT_HEADS, ATT_HEAD_DIM)
    iq = rotary(iq.reshape(B, S, IDX_HEADS, IDX_HEAD_DIM), positions)
    ik = rotary(ik[:, :, None, :], positions)[:, :, 0]
    iw = iw * (IDX_HEADS ** -0.5)
    n_sel = min(TOPK_MAX, S // 4)
    nb = S // Q_BLOCK
    key_chunk = jnp.arange(S) // CHUNK

    def to_blocks(a):
        return a.reshape(B, nb, Q_BLOCK, *a.shape[2:]).swapaxes(0, 1)

    def attend_block(args):
        blk, qb, iqb, iwb = args
        t = blk * Q_BLOCK + jnp.arange(Q_BLOCK)
        q_chunk = t // CHUNK
        admissible = key_chunk[None, :] <= q_chunk[:, None]
        rel = jax.nn.relu(jnp.einsum('bqhd,bsd->bqhs', iqb, ik) * (IDX_HEAD_DIM ** -0.5))
        score = jnp.einsum('bqhs,bqh->bqs', rel, iwb).astype(jnp.float32)
        score = jnp.where(admissible[None], score, -jnp.inf)
        _, sel = lax.top_k(score, n_sel)
        valid = (sel // CHUNK) <= q_chunk[None, :, None]
        kg = jax.vmap(lambda kk, ii: kk[ii])(k, sel)
        vg = jax.vmap(lambda vv, ii: vv[ii])(v, sel)
        s = jnp.einsum('bqhd,bqkhd->bqhk', qb, kg).astype(jnp.float32) * (ATT_HEAD_DIM ** -0.5)
        s = jnp.where(valid[:, :, None, :], s, -jnp.inf)
        p = jax.nn.softmax(s, axis=-1).astype(vg.dtype)
        return jnp.einsum('bqhk,bqkhd->bqhd', p, vg)

    out = lax.map(attend_block, (jnp.arange(nb), to_blocks(q), to_blocks(iq), to_blocks(iw)))
    return out.swapaxes(0, 1).reshape(B, S, ATT_WIDTH)

def memory_branch(mq, mem, w_mem_kv):
    B, S, _ = mq.shape
    M = mem.shape[1]
    kv = jnp.einsum('bmd,de->bme', mem, w_mem_kv)
    mk, mv = jnp.split(kv, 2, axis=-1)
    mk = mk.reshape(B, M, MEM_HEADS, MEM_HEAD_DIM)
    mv = mv.reshape(B, M, MEM_HEADS, MEM_HEAD_DIM)
    q = mq.reshape(B, S, MEM_HEADS, MEM_HEAD_DIM)
    s = jnp.einsum('bshd,bmhd->bhsm', q, mk).astype(jnp.float32) * (MEM_HEAD_DIM ** -0.5)
    p = jax.nn.softmax(s, axis=-1).astype(mv.dtype)
    return jnp.einsum('bhsm,bmhd->bshd', p, mv).reshape(B, S, MEM_WIDTH)

def token_mixing(x, mem, positions, w_in, b_in, pool_w, pool_scale, w_mem_kv, w_br, w_out):
    B, S, D = x.shape
    proj = jnp.einsum('bsd,de->bse', x, w_in) + b_in
    split_points = np.cumsum(IN_WIDTHS)[:-1].tolist()
    u_pool, q, k, v, iq, ik, iw, mq, gate_logits = jnp.split(proj, split_points, axis=-1)
    gates = jax.nn.sigmoid(gate_logits.astype(jnp.float32)).astype(x.dtype).reshape(B, S, N_BRANCH, D)
    branches = (pool_branch(u_pool, pool_w, pool_scale),
                dsa_branch(q, k, v, iq, ik, iw, positions),
                memory_branch(mq, mem, w_mem_kv))
    merged = jnp.zeros_like(x)
    for n in range(N_BRANCH):
        merged = merged + gates[:, :, n] * jnp.einsum('bsc,cd->bsd', branches[n], w_br[n])
    return jnp.einsum('bsd,de->bse', merged, w_out)

def route(x2, w_router, router_bias):
    scores = jax.nn.sigmoid(jnp.einsum('nd,de->ne', x2, w_router).astype(jnp.float32))
    biased = scores + router_bias.astype(jnp.float32)
    grouped = biased.reshape(-1, N_GROUPS, EXPERTS_PER_GROUP)
    group_score = lax.top_k(grouped, GROUP_SCORE_TOPK)[0].sum(-1)
    best = jnp.argmax(group_score, axis=-1).astype(jnp.int32)
    within = jnp.take_along_axis(grouped, best[:, None, None], axis=1)[:, 0]
    _, local = lax.top_k(within, TOP_K_EXPERTS)
    expert_idx = (best[:, None] * EXPERTS_PER_GROUP + local).astype(jnp.int32)
    w = jnp.take_along_axis(scores, expert_idx, axis=1)
    w = w / jnp.sum(w, axis=-1, keepdims=True)
    return expert_idx, w

def moe(x2, w_router, router_bias, w1, w3, w2):
    N, D = x2.shape
    expert_idx, gate_w = route(x2, w_router, router_bias)
    n_assign = N * TOP_K_EXPERTS
    n_blk = -(-n_assign // MOE_BLOCK) + N_EXPERTS
    flat_e = expert_idx.reshape(-1)
    flat_tok = jnp.repeat(jnp.arange(N, dtype=jnp.int32), TOP_K_EXPERTS)
    flat_g = gate_w.reshape(-1).astype(x2.dtype)
    order = jnp.argsort(flat_e)
    e_sorted = flat_e[order]
    counts = jax.ops.segment_sum(jnp.ones_like(flat_e), flat_e, num_segments=N_EXPERTS)
    padded = ((counts + MOE_BLOCK - 1) // MOE_BLOCK) * MOE_BLOCK
    pad_end = jnp.cumsum(padded)
    pad_start = pad_end - padded
    start = jnp.cumsum(counts) - counts
    rank = jnp.arange(n_assign, dtype=jnp.int32) - start[e_sorted]
    dest = pad_start[e_sorted] + rank
    slot_tok = jnp.full((n_blk * MOE_BLOCK,), N, jnp.int32).at[dest].set(flat_tok[order])
    slot_gate = jnp.zeros((n_blk * MOE_BLOCK,), x2.dtype).at[dest].set(flat_g[order])
    blk_e = jnp.minimum(jnp.searchsorted(pad_end, jnp.arange(n_blk) * MOE_BLOCK, side='right'),
                        N_EXPERTS - 1).astype(jnp.int32)
    x_pad = jnp.concatenate([x2, jnp.zeros((1, D), x2.dtype)], axis=0)

    def run_block(args):
        e, toks = args
        xb = x_pad[toks]
        h = jax.nn.silu(xb @ w1[e]) * (xb @ w3[e])
        return h @ w2[e]

    yb = lax.map(run_block, (blk_e, slot_tok.reshape(n_blk, MOE_BLOCK)))
    y = yb.reshape(-1, D) * slot_gate[:, None]
    return jnp.zeros((N + 1, D), x2.dtype).at[slot_tok].add(y)[:N]

def second_inputs(seed: int = 0) -> dict:
    key = jax.random.key(seed)
    ks = jax.random.split(key, 20)
    f32 = jnp.float32
    nrm = lambda k, shape, scale: jax.random.normal(k, shape, f32) * scale
    return {
        'x': nrm(ks[0], (BATCH, SEQ, D_MODEL), 1.0),
        'mem': nrm(ks[1], (BATCH, N_MEM, D_MODEL), 1.0),
        'positions': jnp.broadcast_to(jnp.arange(SEQ, dtype=jnp.int32)[None], (BATCH, SEQ)),
        'w_in': nrm(ks[2], (DEPTH, D_MODEL, D_IN_2), D_MODEL ** -0.5),
        'b_in': nrm(ks[3], (DEPTH, D_IN_2), 0.02),
        'pool_w': nrm(ks[4], (DEPTH, POOL_GROUPS, POOL_GROUP_DIM, POOL_GROUP_DIM), POOL_GROUP_DIM ** -0.5),
        'pool_scale': 1.0 + nrm(ks[5], (DEPTH, POOL_WIDTH), 0.02),
        'w_mem_kv': nrm(ks[6], (DEPTH, D_MODEL, 2 * MEM_WIDTH), D_MODEL ** -0.5),
        'w_br': nrm(ks[7], (DEPTH, N_BRANCH, BRANCH_WIDTH, D_MODEL), DN_BETA_2 * BRANCH_WIDTH ** -0.5),
        'w_out': nrm(ks[8], (DEPTH, D_MODEL, D_MODEL), DN_BETA_2 * D_MODEL ** -0.5),
        'ln1_g': 1.0 + nrm(ks[9], (DEPTH, D_MODEL), 0.02),
        'ln1_b': nrm(ks[10], (DEPTH, D_MODEL), 0.02),
        'w_router': nrm(ks[11], (D_MODEL, N_EXPERTS), D_MODEL ** -0.5),
        'router_bias': nrm(ks[12], (N_EXPERTS,), 0.01),
        'w1': nrm(ks[13], (DEPTH, N_EXPERTS, D_MODEL, D_EXPERT), D_MODEL ** -0.5),
        'w3': nrm(ks[14], (DEPTH, N_EXPERTS, D_MODEL, D_EXPERT), D_MODEL ** -0.5),
        'w2': nrm(ks[15], (DEPTH, N_EXPERTS, D_EXPERT, D_MODEL), DN_BETA_2 * D_EXPERT ** -0.5),
        'ln2_g': 1.0 + nrm(ks[16], (DEPTH, D_MODEL), 0.02),
        'ln2_b': nrm(ks[17], (DEPTH, D_MODEL), 0.02),
    }

def second_block(x, mem, positions, w_in, b_in, pool_w, pool_scale, w_mem_kv, w_br, w_out,
              ln1_g, ln1_b, w_router, router_bias, w1, w3, w2, ln2_g, ln2_b):
    B, S, D = x.shape
    for l in range(DEPTH):
        mix = token_mixing(x, mem, positions, w_in[l], b_in[l], pool_w[l], pool_scale[l],
                           w_mem_kv[l], w_br[l], w_out[l])
        x = layer_norm_2(DN_ALPHA_2 * x + mix, ln1_g[l], ln1_b[l])
        ffn = moe(x.reshape(B * S, D), w_router, router_bias, w1[l], w3[l], w2[l]).reshape(B, S, D)
        x = layer_norm_2(DN_ALPHA_2 * x + ffn, ln2_g[l], ln2_b[l])
    return x


def setup_inputs(seed=0):
    out = dict(first_inputs(seed))
    for name, value in second_inputs(seed + 1).items():
        if name != "x":
            out[name + "_2"] = value
    return out


def reference(
    x, positions, ln_in_g, ln_in_b, w_in, w_sc_conv, w_gla_a_up, b_gla_a, g_gla_head, g_mla_q,
    w_mla_uq, g_mla_kv, w_mla_ukv, w_cfm_dw, g_cfm_ln, b_cfm_ln, g_branch, w_out, ln1_g, ln1_b,
    w_ffn_up, w_ffn_dw, w_ffn_down, ln2_g, ln2_b, mem_2, positions_2, w_in_2, b_in_2, pool_w_2,
    pool_scale_2, w_mem_kv_2, w_br_2, w_out_2, ln1_g_2, ln1_b_2, w_router_2, router_bias_2,
    w1_2, w3_2, w2_2, ln2_g_2, ln2_b_2,
):
    x = first_block(
        x, positions, ln_in_g, ln_in_b, w_in, w_sc_conv, w_gla_a_up, b_gla_a, g_gla_head,
        g_mla_q, w_mla_uq, g_mla_kv, w_mla_ukv, w_cfm_dw, g_cfm_ln, b_cfm_ln, g_branch, w_out,
        ln1_g, ln1_b, w_ffn_up, w_ffn_dw, w_ffn_down, ln2_g, ln2_b,
    )
    return second_block(
        x, mem_2, positions_2, w_in_2, b_in_2, pool_w_2, pool_scale_2, w_mem_kv_2, w_br_2,
        w_out_2, ln1_g_2, ln1_b_2, w_router_2, router_bias_2, w1_2, w3_2, w2_2, ln2_g_2,
        ln2_b_2,
    )


_drawn_inputs = setup_inputs


def setup_inputs(seed=0):
    import zlib

    import numpy as np

    out = dict(_drawn_inputs(seed))
    spreads = {}
    factors = {'b_gla_a': 5.862,
     'g_gla_head': 10.802,
     'g_mla_q': 5.06,
     'g_cfm_ln': 16.157,
     'b_cfm_ln': 11.242,
     'b_in_2': 6.198,
     'pool_scale_2': 8.989}
    for name, (base, spread) in spreads.items():
        noise = np.random.default_rng([zlib.crc32(name.encode()), seed]).standard_normal(out[name].shape)
        drawn = base * np.exp(spread * noise) if base else spread * noise
        out[name] = __import__('jax').numpy.asarray(drawn.astype(out[name].dtype))
    for name, factor in factors.items():
        out[name] = (out[name] * factor).astype(out[name].dtype)
    return out
```

```python
from contextlib import ExitStack

import concourse.bass as bass
from concourse import mybir

P = 128
S = 512
NT = S // P
D = 1024
KC = D // P
L = 2
F32 = mybir.dt.float32
F32R = mybir.dt.float32r
I32 = mybir.dt.int32
U32 = mybir.dt.uint32
ALU = mybir.AluOpType
ACT = mybir.ActivationFunctionType
AX = mybir.AxisListType
ADD, SUB, MUL, MAX, MIN = ALU.add, ALU.subtract, ALU.mult, ALU.max, ALU.min
EPS = 1e-5
ALPHA = (2.0 * L) ** 0.25

C_SCB, C_SCC, C_SCH, C_GQ, C_GK, C_GV, C_GA, C_CQ, C_CKV, C_KR, C_A, C_GATE = (
    0, 256, 512, 768, 896, 1024, 1536, 1568, 1824, 1952, 1984, 2240)
W = 256
D_FF = 2816
FC = D_FF // P
TAPS = 31
HALO = TAPS // 2
GH, GK, GVD, TAU = 4, 32, 64, 16.0
MH, NOPE, ROPE, MD = 4, 64, 32, 96
R0 = NOPE
MLA_SCALE = MD ** -0.5

RAW, SPLIT = 4, 2

K_ID, K_SWA, K_SWB, K_TRF, K_TRB, K_HEAD, K_BLK, K_FREQ, K_CNT, K_E16, K_G16, K_BNO, K_END = (
    0, 128, 256, 384, 512, 640, 644, 900, 904, 968, 984, 1000, 1028)


def shape_constants():
    import numpy as np

    c = np.zeros((P, K_END), np.float32)
    i = np.arange(P)
    c[i, K_ID + i] = 1.0
    for r in range(ROPE):
        c[R0 + (r ^ 16), K_SWA + R0 + r] = 1.0
    c[i ^ 32, K_SWB + i] = 1.0
    s, t = i[:, None], i[None, :]
    c[:, K_TRF:K_TRF + P] = s <= t
    c[:, K_TRB:K_TRB + P] = s > t
    c[i, K_HEAD + i // GK] = 1.0
    c[:, K_BLK:K_BLK + W] = (s // GK) == (np.arange(W)[None, :] // GVD)
    c[:, K_FREQ] = np.float32(10000.0) ** (-(i % 16).astype(np.float32) / np.float32(16))
    c[:, K_FREQ + 1] = np.where(i % 32 < 16, -1.0, 1.0)
    c[:, K_FREQ + 2] = np.float32(10000.0) ** (-(i % 32).astype(np.float32) / np.float32(32))
    c[:, K_FREQ + 3] = np.where(i % 64 < 32, -1.0, 1.0)
    for g, w in enumerate((2, 4, 8, 16)):
        c[:, K_CNT + 16 * g:K_CNT + 16 * g + 16] = 1.0 / np.minimum(np.arange(16) + 1, w).astype(np.float32)
    c[:, K_E16:K_E16 + 16] = np.arange(16)
    c[:, K_G16:K_G16 + 16] = np.arange(16) // 4
    c[:, K_BNO:K_END] = np.arange(K_END - K_BNO)
    return c


COUNTS = {
    "ld_start": (7, 0, 0),
    "h_st": (0, 0, 4),
    "wt_ld0": (0, 0, 24),
    "wt_ld1": (0, 0, 24),
    "wt_ld2": (0, 0, 24),
    "wt_ld3": (0, 0, 24),
    "wt_ld4": (0, 0, 24),
    "wt_ld5": (0, 0, 24),
    "set_up": (5, 0, 0),
    "y_st0": (1, 0, 12),
    "y_st1": (1, 0, 12),
    "bidx": (0, 0, 2),
    "slot_zero": (0, 0, 1),
    "slot_st": (0, 0, 8),
    "slot_ld": (0, 0, 1),
    "sid_ok": (0, 0, 25),
    "xb_ld0": (0, 0, 13),
    "xb_ld1": (0, 0, 12),
    "yg_ld0": (0, 0, 2),
    "yg_ld1": (0, 0, 2),
    "yg_ld2": (0, 0, 2),
    "yg_ld3": (0, 0, 2),
    "wt_done": (6, 0, 144),
    "x_tr": (1, 0, 50),
    "h_tr": (1, 0, 24),
    "norm_tr": (8, 16, 16),
    "par_tr": (0, 1, 1),
    "ga_mm": (0, 2, 0),
    "rms_mm": (0, 5, 0),
    "cfm_mm": (0, 1, 0),
    "kd_tr": (0, 2, 0),
    "gla_scores": (0, 8, 0),
    "gla_kv": (0, 6, 0),
    "gla_out": (0, 8, 0),
    "tok_tr": (0, 4, 0),
    "head_sw": (0, 5, 13),
    "at_scores": (0, 16, 32),
    "at_tr": (0, 16, 32),
    "at_out": (0, 16, 32),
    "mem_tr": (0, 0, 4),
    "m_s": (0, 0, 16),
    "m_t": (0, 0, 16),
    "m_o": (0, 0, 16),
    "m_ot": (0, 0, 4),
    "a_ot": (0, 0, 4),
    "ix_s": (0, 0, 24),
    "rt_rank": (0, 0, 1),
    "gb_ld": (2, 4, 4),
    "norm_sd": (4, 8, 8),
    "norm_hi": (8, 16, 16),
    "tab_sin": (4, 0, 0),
    "par_ld": (0, 13, 11),
    "proj_ev": (0, 16, 21),
    "la_part": (0, 4, 0),
    "a_step": (0, 11, 0),
    "gv_ev": (0, 8, 0),
    "gexp": (0, 5, 0),
    "rms_sq": (0, 9, 0),
    "rms_rs": (0, 5, 0),
    "y_hi": (0, 4, 0),
    "kd_ev": (0, 2, 0),
    "tok_sd": (0, 3, 0),
    "tok_hi": (0, 4, 0),
    "c_h": (0, 3, 0),
    "head_ev": (0, 4, 0),
    "k_cp": (0, 7, 0),
    "at_p": (0, 16, 32),
    "up_ev": (0, 44, 0),
    "up_silu": (0, 22, 0),
    "up_hi": (0, 22, 0),
    "mem_hi": (0, 0, 4),
    "v2_ev": (0, 0, 4),
    "pool_dh": (0, 0, 4),
    "pool_hi": (0, 0, 4),
    "mk_ev": (0, 0, 4),
    "mv_ev": (0, 0, 2),
    "m_p": (0, 0, 16),
    "m_oh": (0, 0, 4),
    "a_te": (0, 0, 32),
    "a_oh": (0, 0, 4),
    "ix_rel": (0, 0, 24),
    "gt_sig": (0, 0, 24),
    "mg_hi": (0, 0, 8),
    "rb_ld": (0, 0, 1),
    "rt_sc": (0, 0, 1),
    "x_ev": (0, 0, 50),
    "act_h": (0, 0, 24),
    "h_ev": (0, 0, 24),
    "y_ev": (1, 0, 48),
    "gt_use": (2, 0, 24),
    "v_step": (46, 284, 355),
    "norm_var": (4, 8, 8),
    "norm_z": (4, 8, 8),
    "norm_lo": (8, 16, 16),
    "tab_arg": (4, 0, 0),
    "par_col": (0, 1, 1),
    "rms_in": (0, 2, 0),
    "la_x": (0, 1, 0),
    "y_val": (0, 4, 0),
    "y_lo": (0, 4, 0),
    "cfm_ln": (0, 2, 0),
    "kd_val": (0, 2, 0),
    "gla_q": (0, 8, 0),
    "gla_state": (0, 8, 0),
    "gla_masked": (0, 8, 0),
    "gla_out_read": (0, 8, 0),
    "tok_ms": (0, 3, 0),
    "tok_y": (0, 2, 0),
    "tok_lo": (0, 4, 0),
    "c_val": (0, 3, 0),
    "c_l": (0, 3, 0),
    "head_rope": (0, 5, 13),
    "v_ev": (0, 1, 0),
    "at_max": (0, 16, 32),
    "at_pT": (0, 16, 0),
    "up_conv": (0, 44, 0),
    "up_val": (0, 22, 0),
    "up_lo": (0, 22, 0),
    "mem_lo": (0, 0, 4),
    "pool_d": (0, 0, 4),
    "iw_ev": (0, 0, 1),
    "pool_dl": (0, 0, 4),
    "pool_lo": (0, 0, 4),
    "m_mx": (0, 0, 16),
    "m_te": (0, 0, 16),
    "m_or": (0, 0, 4),
    "m_ol": (0, 0, 4),
    "a_sc": (0, 0, 32),
    "a_or": (0, 0, 4),
    "a_ol": (0, 0, 4),
    "ix_use": (0, 0, 24),
    "mg_lo": (0, 0, 8),
    "rt_oh": (0, 0, 1),
    "be_ok": (0, 0, 1),
    "rt_dest": (0, 0, 1),
    "h_val": (0, 0, 24),
    "yg_use": (0, 0, 8),
    "y_free": (2, 0, 24),
    "y_st": (0, 0, 24),
}
TURNS = {
    "sp_moe": {"wt_ld0": 2, "wt_ld1": 2, "wt_ld2": 2, "wt_ld3": 2, "wt_ld4": 2, "wt_ld5": 2},
    "g_moe": {"sid_ok": 2, "xb_ld0": 1, "xb_ld1": 1, "y_st0": 1, "y_st1": 1, "y_st": 2, "y_free": 2},
    "t_moe": {"x_tr": 4, "wt_done": 12, "h_tr": 2},
    "a_up": {"up_ev": 4, "up_silu": 2, "up_hi": 2},
    "a_gates": {"gt_sig": 6},
    "a_moe": {"x_ev": 4, "act_h": 2, "h_ev": 2},
    "v_up": {"v_step": 8, "up_conv": 4, "up_val": 2, "up_lo": 2},
    "v_gates": {"v_step": 4, "gt_use": 6},
    "v_moe": {"h_val": 2, "y_ev": 4},
}


class Signal:

    def __init__(self, name, sem, step=1):
        self.name, self.sem, self.step = name, sem, step
        self.counts = COUNTS.get(name, (0, 0, 0))
        self.first = (0, self.counts[0], self.counts[0] + L * self.counts[1])

    def at(self, lane, k):
        return lane.layer * (self.counts[lane.block] * self.step) + (self.first[lane.block] + k) * self.step

    def up(self, lane):
        lane.raised[self] = lane.raised.get(self, 0) + 1
        return self.step

    def last(self, lane):
        k = lane.raised[self]
        if lane.turn is not None:
            k = lane.turn[1] * TURNS.get(lane.turn[0], {}).get(self.name, 0) + k
        return self.at(lane, k)


class Lane:

    def __init__(self, eng, began):
        self.eng, self.began = eng, began
        self.enter(0, 0)

    def enter(self, block, layer):
        self.block, self.layer, self.raised, self.turn = block, layer, {}, None

    def leave(self):
        for s, n in self.raised.items():
            if n != s.counts[self.block]:
                raise ValueError(s.name, self.block, n)

    def loop(self, name, reg):
        self.turn, self.begun = (name, reg), dict(self.raised)

    def loop_end(self, count):
        name, _ = self.turn
        for s in list(self.raised):
            got = self.raised[s] - self.begun.get(s, 0)
            if got != TURNS.get(name, {}).get(s.name, 0):
                raise ValueError(s.name, name, got)
            self.raised[s] = self.begun.get(s, 0) + got * count
        self.turn = None

    def alone(self, value):
        value = self.eng.to_reg(value) if self.block else value
        self.eng.wait_ge(self.began, 1)
        return value


class Stream:

    PER = (0, 96, 92)

    def __init__(self, sb, sem):
        self.raw = [sb(f"unit_raw{i}", [P, 1024], F32) for i in range(RAW)]
        self.hi = [sb(f"unit_hi{i}", [P, 1024], F32R) for i in range(SPLIT)]
        self.lo = [sb(f"unit_lo{i}", [P, 1024], F32R) for i in range(SPLIT)]
        self.loaded = [sem(f"unit_loaded{i}") for i in range(RAW)]
        self.hi_made = sem("unit_hi_made")
        self.split = sem("unit_split")
        self.done = sem("unit_done")
        self.base = (0, 0, L * self.PER[1])

    def number(self, lane, j, turn=0, size=RAW):
        return lane.layer * self.PER[lane.block] + turn * size + (self.base[lane.block] + j)

    def prime(self, pool, pe):
        if pool is not None:
            for _ in range(RAW):
                pool.nop().then_inc(self.split, 1)
        if pe is not None:
            for _ in range(SPLIT):
                pe.nop().then_inc(self.done, 1)

    def load(self, sp, j, parts, turn=0, size=RAW):
        assert len(parts) == 2
        sp.eng.wait_ge(self.split, sp.alone(self.number(sp, j, turn, size) + 1))
        for dst, src in parts:
            sp.eng.dma_start(dst, src).then_inc(self.loaded[j % RAW], 16)

    def part(self, pool, j, turn=0, size=RAW, width=1024):
        n = self.number(pool, j, turn, size)
        laps = pool.layer * (self.PER[pool.block] // RAW) + turn * (size // RAW) + (self.base[pool.block] + j) // RAW
        raw, hi, lo = self.raw[j % RAW][:, 0:width], self.hi[j % SPLIT][:, 0:width], self.lo[j % SPLIT][:, 0:width]
        pool.eng.wait_ge(self.loaded[j % RAW], laps * 32 + 32)
        pool.eng.wait_ge(self.done, pool.alone(n + 1))
        pool.eng.tensor_scalar(hi, raw, 1.0, 0.0, MUL, ADD).then_inc(self.hi_made, 1)
        pool.eng.wait_ge(self.hi_made, n + 1)
        pool.eng.tensor_tensor(lo, raw, hi.bitcast(F32), SUB).then_inc(self.split, 1)

    def weights(self, pe, j, turn=0, size=RAW):
        pe.eng.wait_ge(self.split, self.number(pe, j, turn, size) + 1 + RAW)
        return self.hi[j % SPLIT], self.lo[j % SPLIT]

    def products(self, lane, j, turn=0, size=RAW):
        return self.number(lane, j, turn, size) + 1 + SPLIT


def triple(pe, out, wh, wl, xh, xl, first, last):
    pe.matmul(out, wh, xh, start=first, stop=False)
    pe.matmul(out, wh, xl, start=False, stop=False)
    return pe.matmul(out, wl, xh, start=False, stop=last)


def flat(ap):
    return ap.rearrange("p a b -> p (a b)")


def over(ap, shape):
    return ap.broadcast_to(shape)


def build(nc, t, out, debug=None):
    ctx = ExitStack()
    with ctx:
        def sb(name, shape, dt=F32, to=ctx):
            return to.enter_context(nc.sbuf_tensor(name, shape, dt))

        def sem(name):
            return ctx.enter_context(nc.semaphore(name))

        def signal(name, step=1):
            return Signal(name, sem(name), step)

        h = sb("h", [P, NT, D])
        xT_hi = sb("xT_hi", [P, KC, S], F32R)
        xT_lo = sb("xT_lo", [P, KC, S], F32R)
        ring = Stream(sb, sem)
        konst = sb("konst", [P, K_END])
        gb = sb("gb", [P, 2, D])
        cosA, sinA = sb("cosA", [P, S]), sb("sinA", [P, S])
        cosB, sinB = sb("cosB", [P, S]), sb("sinB", [P, S])
        small = sb("small", [P, 4])
        mean_of = sb("mean_of", [P, P])
        ones = sb("ones", [P, P])
        stats = sb("stats", [P, NT, 2, 6])
        mv = sb("mv", [P, NT, 2])
        sd = sb("sd", [P, NT])
        rs = sb("rs", [P, NT])
        pcol = sb("pcol", [P, 224])
        gaup = sb("gaup", [32, 2, P])
        eps, unit1 = small[:, 0:1], small[:, 1:2]
        ident = konst[:, K_ID:K_ID + P]
        bank = [ctx.enter_context(nc.psum_tensor(f"bank{i}", [P, S], F32)) for i in range(8)]

        one = ExitStack()
        s1 = lambda name, shape, dt=F32: sb(name, shape, dt, one)
        proj = s1("proj", [P, 16, S])
        glu = s1("glu", [P, 2, S + 2 * HALO])
        u = s1("u", [P, 2, S])
        scp = s1("scp", [P, 2, S + 2])
        ya = s1("ya", [P, 2, S])
        sq = s1("sq", [P, 2, S])
        rstd = s1("rstd", [P, S])
        gvgg = s1("gvgg", [P, NT, S])
        prow = s1("prow", [96, P])
        prow2 = s1("prow2", [66, 2, P])
        ghead = s1("ghead", [P, W])
        og = s1("og", [P, NT, W])
        gst = s1("gst", [P, 3 * 16])
        attn = ExitStack()
        s2 = lambda name, shape, dt=F32: sb(name, shape, dt, attn)
        lax = s2("lax", [P, 2, S])
        eqk = s2("eqk", [P, 2, 2, S])
        qikd = s2("qikd", [P, 2, 2, S])
        gsm = s2("gsm", [P, 2, 3, NT])
        gse = s2("gse", [P, 2, 3, NT])
        kdT = s2("kdT", [P, 8, P])
        qbd = [s2(f"qbd{i}", [P, GH, P]) for i in range(2)]
        sT = [s2(f"sT{i}", [P, GH, P]) for i in range(2)]
        state, stnew = s2("state", [P, W]), s2("stnew", [P, W])
        attn.close()
        attn = ExitStack()
        c_hi, c_lo = s2("c_hi", [P, 3, S], F32R), s2("c_lo", [P, 3, S], F32R)
        vml = s2("vml", [P, NT, W])
        pm = [s2(f"pm{i}", [P, S]) for i in range(2)]
        pT = [s2(f"pT{i}", [P, NT, P]) for i in range(2)]
        msum, mmx, mrs = s2("msum", [P, 16]), s2("mmx", [P, 16]), s2("mrs", [P, 16])
        attn.close()
        one.close()
        qh, kh = proj[:, 4:8, :], proj[:, 0:4, :]

        ffn = ExitStack()
        s4 = lambda name, shape, dt=F32: sb(name, shape, dt, ffn)
        g_hi, g_lo = s4("g_hi", [P, FC, S], F32R), s4("g_lo", [P, FC, S], F32R)
        ubuf = s4("ubuf", [P, 4, S + 2])
        cv = [s4(f"cv{i}", [P, S]) for i in range(2)]
        ffn.close()

        ld = signal("ld_start", 16)
        v_step, a_step = signal("v_step"), signal("a_step")
        set_up = signal("set_up")
        tab_arg, tab_sin = signal("tab_arg"), signal("tab_sin")
        gb_ld = signal("gb_ld", 16)
        norm_var, norm_sd, norm_z = signal("norm_var"), signal("norm_sd"), signal("norm_z")
        norm_tr, norm_hi, norm_lo = signal("norm_tr"), signal("norm_hi"), signal("norm_lo")
        par_ld = signal("par_ld", 16)
        par_tr, par_col = signal("par_tr"), signal("par_col")
        proj_ev = signal("proj_ev")
        ga_mm, la_part, la_x, gexp = signal("ga_mm"), signal("la_part"), signal("la_x"), signal("gexp")
        gv_ev = signal("gv_ev")
        rms_in, rms_sq, rms_mm, rms_rs = signal("rms_in"), signal("rms_sq"), signal("rms_mm"), signal("rms_rs")
        y_val, y_hi, y_lo = signal("y_val"), signal("y_hi"), signal("y_lo")
        cfm_mm, cfm_dev, cfm_ln = signal("cfm_mm"), signal("cfm_dev"), signal("cfm_ln")
        kd_val, kd_tr, kd_ev = signal("kd_val"), signal("kd_tr"), signal("kd_ev")
        g_q, g_s, g_m, g_o, g_st, g_state, g_oev = (signal(n) for n in (
            "gla_q", "gla_scores", "gla_masked", "gla_out", "gla_kv", "gla_state", "gla_out_read"))
        tok_ms, tok_sd, tok_y, tok_tr, tok_hi, tok_lo = (signal(n) for n in (
            "tok_ms", "tok_sd", "tok_y", "tok_tr", "tok_hi", "tok_lo"))
        c_val, c_h, c_l = signal("c_val"), signal("c_h"), signal("c_l")
        head_ev, head_sw, head_rope, k_cp, v_ev = (signal(n) for n in (
            "head_ev", "head_sw", "head_rope", "k_cp", "v_ev"))
        at_s, at_mx, at_p, at_t, at_te, at_o = (signal(n) for n in (
            "at_scores", "at_max", "at_p", "at_tr", "at_pT", "at_out"))
        up_ev, up_cv, up_act, up_val, up_hi, up_lo = (signal(n) for n in (
            "up_ev", "up_conv", "up_silu", "up_val", "up_hi", "up_lo"))
        stored, began = sem("stored"), sem("began")

        block = ctx.enter_context(nc.Block())

        def norm_v(V, n, last_unit):
            if last_unit is not None:
                V.eng.wait_ge(ring.done, ring.products(V, last_unit))
            for i in range(NT):
                if last_unit is not None:
                    for x in range(2):
                        c = slice(x * S, x * S + S)
                        V.eng.scalar_tensor_tensor(h[:, i, c], h[:, i, c], ALPHA, bank[2 * i + x][:], MUL, ADD).then_inc(v_step.sem, v_step.up(V))
                    V.eng.wait_ge(v_step.sem, v_step.last(V))
                for x in range(2):
                    V.eng.bn_stats(stats[:, i, x, :], h[:, i, x * S:x * S + S]).then_inc(v_step.sem, v_step.up(V))
                V.eng.wait_ge(v_step.sem, V.alone(v_step.last(V)))
                V.eng.bn_aggr(mv[:, i, :], flat(stats[:, i, :, :])).then_inc(norm_var.sem, norm_var.up(V))
                V.eng.wait_ge(norm_var.sem, norm_var.last(V))
            V.eng.wait_ge(gb_ld.sem, gb_ld.at(V, 2 * n + 2))
            for i in range(NT):
                V.eng.wait_ge(norm_sd.sem, norm_sd.at(V, NT * n + i + 1))
                V.eng.reciprocal(rs[:, i:i + 1], sd[:, i:i + 1]).then_inc(v_step.sem, v_step.up(V))
                V.eng.wait_ge(v_step.sem, v_step.last(V))
                V.eng.scalar_tensor_tensor(h[:, i, :], h[:, i, :], mv[:, i, 0:1], gb[:, 0, :], SUB, MUL).then_inc(v_step.sem, v_step.up(V))
                V.eng.wait_ge(v_step.sem, v_step.last(V))
                V.eng.scalar_tensor_tensor(h[:, i, :], h[:, i, :], rs[:, i:i + 1], gb[:, 1, :], MUL, ADD).then_inc(norm_z.sem, norm_z.up(V))
                V.eng.wait_ge(norm_z.sem, norm_z.last(V))
            for i in range(NT):
                for x in range(2):
                    V.eng.wait_ge(norm_hi.sem, norm_hi.at(V, 2 * (NT * n + i) + x + 1))
                    V.eng.tensor_tensor(
                        xT_lo[:, 4 * x:4 * x + 4, i * P:i * P + P], bank[2 * i + x][:].rearrange("p (k t) -> p k t", k=4),
                        xT_hi[:, 4 * x:4 * x + 4, i * P:i * P + P].bitcast(F32), SUB).then_inc(norm_lo.sem, norm_lo.up(V))

        def norm_a(A, n):
            for i in range(NT):
                A.eng.wait_ge(norm_var.sem, norm_var.at(A, NT * n + i + 1))
                A.eng.activation(sd[:, i:i + 1], mv[:, i, 1:2], ACT.Sqrt, bias=eps).then_inc(norm_sd.sem, norm_sd.up(A))
            for i in range(NT):
                for x in range(2):
                    A.eng.wait_ge(norm_tr.sem, norm_tr.at(A, 2 * (NT * n + i) + x + 1))
                    A.eng.activation(xT_hi[:, 4 * x:4 * x + 4, i * P:i * P + P],
                                            bank[2 * i + x][:].rearrange("p (k t) -> p k t", k=4), ACT.Copy).then_inc(norm_hi.sem, norm_hi.up(A))

        def norm_pe(T, n):
            for i in range(NT):
                T.eng.wait_ge(norm_z.sem, norm_z.at(T, NT * n + i + 1))
                for x in range(2):
                    for k in range(4):
                        last = T.eng.transpose(bank[2 * i + x][:, k * P:k * P + P],
                                               h[:, i, (4 * x + k) * P:(4 * x + k + 1) * P], ident)
                    last.then_inc(norm_tr.sem, norm_tr.up(T))

        def load_gb(A, g_row, b_row):
            A.eng.dma_start(gb[:, 0, :], over(g_row, [P, D])).then_inc(gb_ld.sem, gb_ld.up(A))
            A.eng.dma_start(gb[:, 1, :], over(b_row, [P, D])).then_inc(gb_ld.sem, gb_ld.up(A))

        def row(name, layer):
            return t[name][bass.ds(layer, 1), :]

        def chunk(T, units, j, out_bank, cols=slice(0, P), turn=0, size=RAW, kc=KC, n=S, src=None):
            wh, wl = units.weights(T, j, turn, size)
            xh, xl = src or (xT_hi, xT_lo)
            wh, wl = (w[:, 0:kc * P].rearrange("p (k c) -> p k c", c=P) for w in (wh, wl))
            for k in range(kc):
                last = triple(T.eng, out_bank[:, 0:n], wh[:, k, :], wl[:, k, :], xh[:, k, 0:n], xl[:, k, 0:n],
                              k == 0, k == kc - 1)
            last.then_inc(units.done, 1)

        CHUNKS = [C_A, C_GATE, C_A + P, C_GATE + P, C_SCB, C_SCB + P, C_SCC, C_SCC + P, C_SCH, C_SCH + P,
                  C_GQ, C_GK, None, C_CQ, C_CQ + P, C_CKV]
        U_GV, U_UQ, U_UKV, U_OUT, U_UP, U_DOWN = 16, 20, 21, 22, 30, 74
        GA, KR, CQ, CKV = 12, 12, 13, 15
        Q_G, B_GA, G_Q, G_KV, W_CF, G_CF, B_CF, G_BR, W_UP = 0, 6, 8, 10, 11, 73, 75, 77, 85

        def col(k):
            return pcol[:, k:k + 1]

        def cols3(j):
            return ring.raw[j % RAW][:, :].rearrange("p (k c) -> p k c", c=P)

        def loads1(E):
            l = E.layer
            w = t["w_in"][bass.ds(l, 1)].rearrange("o (k p) n -> (o p) k n", p=P)
            for j, c in enumerate(CHUNKS):
                dst = cols3(j)
                if c is None:
                    parts = [(dst[:, :, 0:64], w[:, :, C_GA:C_GA + 64]), (dst[:, :, 64:P], w[:, :, C_KR:C_KR + 64])]
                else:
                    parts = [(dst[:, 0:4, :], w[:, 0:4, c:c + P]), (dst[:, 4:8, :], w[:, 4:8, c:c + P])]
                ring.load(E, j, parts)
            for j in range(4):
                dst = ring.raw[(U_GV + j) % RAW][:, :].rearrange("p (k n) -> p k n", k=2)
                ring.load(E, U_GV + j, [(dst[:, k:k + 1, :], w[:, 2 * j + k:2 * j + k + 1, C_GV:C_GV + S]) for k in range(2)])
            uq = t["w_mla_uq"][bass.ds(l, 1)].rearrange("o (k p) n -> (o p) k n", p=P)
            dst = ring.raw[U_UQ % RAW][:, 0:768].rearrange("p (k n) -> p k n", k=2)
            ring.load(E, U_UQ, [(dst[:, k:k + 1, :], uq[:, k:k + 1, :]) for k in range(2)])
            ukv = t["w_mla_ukv"][bass.ds(l, 1)].rearrange("o p n -> (o p) n")
            dst = ring.raw[U_UKV % RAW]
            ring.load(E, U_UKV, [(dst[:, x:x + W], ukv[:, x:x + W]) for x in (0, W)])
            rows_unit(E, U_OUT, KC, t["w_out"], l)
            up = t["w_ffn_up"][bass.ds(l, 1)].rearrange("o (k p) n -> (o p) k n", p=P)
            with E.eng.Fori(0, FC // 2) as i:
                for s in range(4):
                    dst, j = cols3(U_UP + s), i * 2 + s // 2 + FC * (s % 2)
                    ring.load(E, U_UP + s, [(dst[:, x:x + 4, :], up[:, x:x + 4, bass.ds(j * P, P)]) for x in (0, 4)], turn=i)
            rows_unit(E, U_DOWN, FC, t["w_ffn_down"], l)

        def rows_unit(E, first, count, w, l):
            w = w[bass.ds(l, 1)].rearrange("o (k p) n -> (o p) k n", p=P)
            for k in range(count):
                dst = ring.raw[(first + k) % RAW]
                ring.load(E, first + k, [(dst[:, x:x + S], w[:, k, x:x + S]) for x in (0, S)])

        def splits1(G):
            for j in range(U_UP):
                ring.part(G, j, width=768 if j == U_UQ else 512 if j == U_UKV else 1024)
            with G.eng.Fori(0, FC // 2) as i:
                for s in range(4):
                    ring.part(G, U_UP + s, turn=i)
            for j in range(U_DOWN, U_DOWN + FC):
                ring.part(G, j)

        def rows_products(T, first, count, x_hi, x_lo):
            for k in range(count):
                wh, wl = ring.weights(T, first + k)
                for i in range(NT):
                    for x in range(2):
                        c, n = slice(i * P, i * P + P), slice(x * S, x * S + S)
                        last = triple(T.eng, bank[2 * i + x][:], x_hi[:, k, c], x_lo[:, k, c], wh[:, n], wl[:, n],
                                      k == 0, k == count - 1)
                last.then_inc(ring.done, 1)

        def rms_t(T, r, first, n, b):
            for i in range(n):
                T.eng.wait_ge(rms_sq.sem, rms_sq.at(T, first + i + 1))
                last = T.eng.matmul(bank[b][:], mean_of[:], sq[:, i, :], start=i == 0, stop=i == n - 1)
            last.then_inc(rms_mm.sem, rms_mm.up(T))

        def tok_t(T, n, src):
            T.eng.wait_ge(tok_y.sem, tok_y.at(T, n + 1))
            for x in range(2):
                for i in range(NT):
                    last = T.eng.transpose(bank[6 + x][:, i * P:i * P + P], src[:, i, x * P:x * P + P], ident)
                last.then_inc(tok_tr.sem, tok_tr.up(T))

        def tensor1(T):
            pe = T.eng
            T.eng.wait_ge(par_ld.sem, par_ld.at(T, 13))
            T.eng.wait_ge(norm_lo.sem, norm_lo.at(T, 0))
            pe.transpose(bank[7][:, 0:W_UP], prow[0:W_UP, :], ident[0:W_UP, 0:W_UP])
            pe.transpose(bank[7][:, W_UP:W_UP + 66], prow2[:, 0, :], ident[0:66, 0:66])
            pe.transpose(bank[7][:, W_UP + 66:W_UP + 132], prow2[:, 1, :], ident[0:66, 0:66]).then_inc(par_tr.sem, par_tr.up(T))
            for c in range(16):
                if c >= 4:
                    T.eng.wait_ge(proj_ev.sem, proj_ev.at(T, c - 3))
                chunk(T, ring, c, bank[c % 4])
                if c == GA:
                    T.eng.wait_ge(proj_ev.sem, proj_ev.at(T, GA + 1))
                    for d in range(2):
                        pe.matmul(bank[4 + d][:], gaup[:, d, :], proj[0:32, GA, :], start=True, stop=True).then_inc(ga_mm.sem, ga_mm.up(T))
            T.eng.wait_ge(la_part.sem, la_part.at(T, 4))
            T.eng.wait_ge(par_col.sem, par_col.at(T, 1))
            for j in range(4):
                wh, wl = ring.weights(T, U_GV + j)
                for kk in range(2):
                    for i in range(NT):
                        k, c, n = 2 * j + kk, slice(i * P, i * P + P), slice(kk * S, kk * S + S)
                        last = triple(pe, bank[4 + i][:], xT_hi[:, k, c], xT_lo[:, k, c], wh[:, n], wl[:, n], k == 0, k == 7)
                last.then_inc(ring.done, 1)
            T.eng.wait_ge(proj_ev.sem, proj_ev.at(T, 16))
            rms_t(T, 0, 0, 2, 0)
            for i in range(2):
                last = pe.matmul(bank[2][:], mean_of[:], u[:, i, :], start=i == 0, stop=i == 1)
            last.then_inc(cfm_mm.sem, cfm_mm.up(T))
            rms_t(T, 1, 2, 2, 1)
            rms_t(T, 2, 4, 2, 0)
            T.eng.wait_ge(gv_ev.sem, gv_ev.at(T, 8))
            for d in range(2):
                T.eng.wait_ge(kd_val.sem, kd_val.at(T, d + 1))
                for c in range(NT):
                    last = pe.transpose(bank[6 + d][:, c * P:c * P + P], qikd[:, d, 1, c * P:c * P + P], ident)
                last.then_inc(kd_tr.sem, kd_tr.up(T))
            for n in range(8):
                d, c = n // 4, n % 4 if n < 4 else 7 - n
                cs = slice(c * P, c * P + P)
                T.eng.wait_ge(g_q.sem, g_q.at(T, n + 1))
                pe.matmul(bank[n % 2][:], eqk[:, d, 1, cs], flat(qbd[n % 2][:]), start=True, stop=True).then_inc(g_s.sem, g_s.up(T))
                if n == 0:
                    T.eng.wait_ge(kd_ev.sem, kd_ev.at(T, 2))
                if n % 4 != 3:
                    pe.matmul(bank[4 + n % 2][:, 0:W], kdT[:, 4 * d + c, :], gvgg[:, c, 0:W], start=True, stop=True).then_inc(g_st.sem, g_st.up(T))
                T.eng.wait_ge(g_m.sem, g_m.at(T, n + 1))
                T.eng.wait_ge(g_state.sem, g_state.at(T, n + 1 if n < 4 else n + 1))
                if n >= 2:
                    T.eng.wait_ge(g_oev.sem, g_oev.at(T, n - 1))
                pe.matmul(bank[2 + n % 2][:, 0:W], qikd[:, d, 0, cs], state[:], start=True, stop=False)
                for hh in range(GH):
                    v = slice(hh * GVD, hh * GVD + GVD)
                    last = pe.matmul(bank[2 + n % 2][:, v], sT[n % 2][:, hh, :], gvgg[:, c, v], start=False, stop=hh == GH - 1)
                last.then_inc(g_o.sem, g_o.up(T))
            tok_t(T, 0, og)
            rms_t(T, 3, 6, 2, 1)
            rms_t(T, 4, 8, 1, 0)
            T.eng.wait_ge(c_l.sem, c_l.at(T, 2))
            wh, wl = ring.weights(T, U_UQ)
            wh, wl = (w[:, 0:768].rearrange("p (k n) -> p k n", k=2) for w in (wh, wl))
            T.eng.wait_ge(rms_rs.sem, rms_rs.at(T, 5))
            for hh in range(MH):
                for k in range(2):
                    n = slice(hh * MD, hh * MD + MD)
                    last = triple(pe, bank[hh][0:MD, :], wh[:, k, n], wl[:, k, n], c_hi[:, k, :], c_lo[:, k, :], k == 0, k == 1)
            last.then_inc(ring.done, 1)
            T.eng.wait_ge(tok_lo.sem, tok_lo.at(T, 2))
            for hh in range(MH):
                T.eng.wait_ge(head_ev.sem, head_ev.at(T, hh + 1))
                pe.matmul(bank[4 + hh][0:MD, :], konst[0:MD, K_SWA:K_SWA + MD], qh[0:MD, hh, :], start=True, stop=True).then_inc(head_sw.sem, head_sw.up(T))
            pe.matmul(bank[0][0:MD, :], konst[0:MD, K_SWA:K_SWA + MD], proj[0:MD, KR, :], start=True, stop=True).then_inc(head_sw.sem, head_sw.up(T))
            T.eng.wait_ge(c_l.sem, c_l.at(T, 3))
            wh, wl = ring.weights(T, U_UKV)
            T.eng.wait_ge(head_rope.sem, head_rope.at(T, 5))
            for hh in range(MH):
                n = slice(hh * P, hh * P + P)
                triple(pe, bank[hh][:], wh[:, n], wl[:, n], c_hi[:, 2, :], c_lo[:, 2, :], True, True)
            wh, wl = (w[:, 0:S].rearrange("p (h n) -> p h n", h=MH)[:, :, NOPE:P] for w in (wh, wl))
            for i in range(NT):
                c = slice(i * P, i * P + P)
                last = triple(pe, bank[4 + i // 2][:, (i % 2) * W:(i % 2) * W + W], c_hi[:, 2, c], c_lo[:, 2, c], wh, wl, True, True)
            last.then_inc(ring.done, 1)
            T.eng.wait_ge(v_ev.sem, v_ev.at(T, 1))
            T.eng.wait_ge(k_cp.sem, k_cp.at(T, 7))
            for n in range(18):
                if n < 16:
                    hh, i = n // 4, n % 4
                    if n >= 2:
                        T.eng.wait_ge(at_p.sem, at_p.at(T, n - 1))
                    pe.matmul(bank[n % 2][:], qh[0:MD, hh, i * P:i * P + P], kh[0:MD, hh, :], start=True, stop=True).then_inc(at_s.sem, at_s.up(T))
                if 0 < n < 17:
                    m = n - 1
                    T.eng.wait_ge(at_p.sem, at_p.at(T, m + 1))
                    if m >= 2:
                        T.eng.wait_ge(at_te.sem, at_te.at(T, m - 1))
                    for k in range(NT):
                        last = pe.transpose(bank[2 + m % 2][:, k * P:k * P + P], pm[m % 2][:, k * P:k * P + P], ident)
                    last.then_inc(at_t.sem, at_t.up(T))
                if n > 1:
                    m = n - 2
                    hh, i = m // 4, m % 4
                    T.eng.wait_ge(at_te.sem, at_te.at(T, m + 1))
                    for k in range(NT):
                        last = pe.matmul(bank[4 + i][:, hh * NOPE:hh * NOPE + NOPE], pT[m % 2][:, k, :],
                                         vml[:, k, hh * NOPE:hh * NOPE + NOPE], start=k == 0, stop=k == NT - 1)
                    last.then_inc(at_o.sem, at_o.up(T))
            tok_t(T, 1, og)
            T.eng.wait_ge(y_lo.sem, y_lo.at(T, 4))
            T.eng.wait_ge(tok_lo.sem, tok_lo.at(T, 4))
            rows_products(T, U_OUT, KC, xT_hi, xT_lo)
            norm_pe(T, 0)
            T.eng.wait_ge(norm_lo.sem, T.alone(norm_lo.at(T, 8)))
            with pe.Fori(0, FC // 2) as i:
                for s in range(4):
                    if s == 3:
                        T.eng.wait_ge(up_ev.sem, up_ev.at(T, i * 4 + 1))
                    chunk(T, ring, U_UP + s, bank[s], turn=i)
                T.eng.wait_ge(up_ev.sem, up_ev.at(T, i * 4 + 3))
            T.eng.wait_ge(up_lo.sem, up_lo.at(T, FC))
            T.eng.wait_ge(up_ev.sem, up_ev.at(T, 2 * FC))
            rows_products(T, U_DOWN, FC, g_hi, g_lo)
            norm_pe(T, 1)

        def rms_a(A, r, first, srcs, scale=1.0):
            for i, src in enumerate(srcs):
                A.eng.activation(sq[:, i, :], src, ACT.Square).then_inc(rms_sq.sem, rms_sq.up(A))
            A.eng.wait_ge(rms_mm.sem, rms_mm.at(A, r + 1))
            A.eng.activation(rstd[:], bank[r % 2][:], ACT.Ln, bias=eps, scale=scale).then_inc(a_step.sem, a_step.up(A))
            A.eng.wait_ge(a_step.sem, a_step.last(A))
            A.eng.activation(rstd[:], rstd[:], ACT.Exp, scale=-0.5).then_inc(rms_rs.sem, rms_rs.up(A))
            A.eng.wait_ge(rms_rs.sem, rms_rs.last(A))

        def gain_a(A, first, dst, src):
            for i in range(2):
                A.eng.wait_ge(y_val.sem, y_val.at(A, first + i + 1))
                A.eng.activation(xT_hi[:, dst + i, :], src[:, i, :], ACT.Copy, scale=col(G_BR + dst + i)).then_inc(y_hi.sem, y_hi.up(A))

        def tok_sd_a(A, k, cnt, scale):
            A.eng.wait_ge(tok_ms.sem, tok_ms.at(A, k))
            A.eng.activation(gst[:, 16:16 + cnt], gst[:, 0:cnt], ACT.Sqrt, bias=eps, scale=scale).then_inc(tok_sd.sem, tok_sd.up(A))

        def tok_hi_a(A, n, dst):
            for x in range(2):
                A.eng.wait_ge(tok_tr.sem, tok_tr.at(A, 2 * n + x + 1))
                A.eng.activation(xT_hi[:, dst + x, :], bank[6 + x][:], ACT.Copy, scale=col(G_BR + dst + x)).then_inc(tok_hi.sem, tok_hi.up(A))

        def scalar1(A):
            act, l = A.eng, A.layer
            act.dma_start(prow[0:6, :], t["w_sc_conv"][bass.ds(l, 1)].rearrange("o t (c p) -> (o t c) p", p=P)).then_inc(par_ld.sem, par_ld.up(A))
            act.dma_start(prow[6:8, :], t["b_gla_a"][bass.ds(l, 1)].rearrange("o d p -> (o d) p")).then_inc(par_ld.sem, par_ld.up(A))
            act.dma_start(prow[8:10, :], t["g_mla_q"][bass.ds(l, 1)].rearrange("o (c p) -> (o c) p", p=P)).then_inc(par_ld.sem, par_ld.up(A))
            act.dma_start(prow[10:11, :], t["g_mla_kv"][bass.ds(l, 1)]).then_inc(par_ld.sem, par_ld.up(A))
            act.dma_start(prow[11:73, :], t["w_cfm_dw"][bass.ds(l, 1)].rearrange("o t (c p) -> (o t c) p", p=P)).then_inc(par_ld.sem, par_ld.up(A))
            act.dma_start(prow[73:75, :], t["g_cfm_ln"][bass.ds(l, 1)].rearrange("o (c p) -> (o c) p", p=P)).then_inc(par_ld.sem, par_ld.up(A))
            act.dma_start(prow[75:77, :], t["b_cfm_ln"][bass.ds(l, 1)].rearrange("o (c p) -> (o c) p", p=P)).then_inc(par_ld.sem, par_ld.up(A))
            act.dma_start(prow[77:85, :], t["g_branch"][bass.ds(l, 1)].rearrange("o (c p) -> (o c) p", p=P)).then_inc(par_ld.sem, par_ld.up(A))
            dw = t["w_ffn_dw"][bass.ds(l, 1)].rearrange("o t (c p) -> (o t c) p", p=P)
            for x in range(2):
                act.dma_start(prow2[:, x, :], dw[x * 66:x * 66 + 66, :]).then_inc(par_ld.sem, par_ld.up(A))
                act.dma_start(gaup[16 * x:16 * x + 16, x, :], t["w_gla_a_up"][bass.ds(l, 1), x, :, :].rearrange("o r n -> (o r) n")).then_inc(par_ld.sem, par_ld.up(A))
            act.dma_start(ghead[:], over(t["g_gla_head"][bass.ds(l, 1), :], [P, W])).then_inc(par_ld.sem, par_ld.up(A))
            load_gb(A, t["ln1_g"][bass.ds(l, 1), :], t["ln1_b"][bass.ds(l, 1), :])
            for c in range(16):
                A.eng.wait_ge(ring.done, ring.products(A, c))
                act.activation(proj[:, c, :], bank[c % 4][:], ACT.Sigmoid if c in (1, 3) else ACT.Copy).then_inc(proj_ev.sem, proj_ev.up(A))
                if c == GA:
                    A.eng.wait_ge(proj_ev.sem, proj_ev.last(A))
                    A.eng.wait_ge(par_col.sem, par_col.at(A, 1))
                    for d in range(2):
                        A.eng.wait_ge(ga_mm.sem, ga_mm.at(A, d + 1))
                        act.activation(lax[:, d, :], bank[4 + d][:], ACT.Identity, bias=col(B_GA + d)).then_inc(la_part.sem, la_part.up(A))
                        act.activation(qikd[:, d, 0, :], bank[4 + d][:], ACT.Abs, bias=col(B_GA + d)).then_inc(a_step.sem, a_step.up(A))
                        A.eng.wait_ge(a_step.sem, a_step.last(A))
                        act.activation(qikd[:, d, 0, :], qikd[:, d, 0, :], ACT.Exp, scale=-1.0).then_inc(a_step.sem, a_step.up(A))
                        A.eng.wait_ge(a_step.sem, a_step.last(A))
                        act.activation(qikd[:, d, 0, :], qikd[:, d, 0, :], ACT.Ln, bias=unit1).then_inc(la_part.sem, la_part.up(A))
            A.eng.wait_ge(ring.done, ring.products(A, U_GV + 3))
            for i in range(NT):
                act.activation(gvgg[:, i, 0:W], bank[4 + i][:, 0:W], ACT.Copy).then_inc(gv_ev.sem, gv_ev.up(A))
                act.activation(gvgg[:, i, W:S], bank[4 + i][:, W:S], ACT.Silu).then_inc(gv_ev.sem, gv_ev.up(A))
            A.eng.wait_ge(la_x.sem, la_x.at(A, 1))
            for d in range(2):
                act.activation(eqk[:, d, 0, :], lax[:, d, :], ACT.Exp, scale=1.0 / TAU).then_inc(gexp.sem, gexp.up(A))
                act.activation(eqk[:, d, 1, :], lax[:, d, :], ACT.Exp, scale=-1.0 / TAU).then_inc(gexp.sem, gexp.up(A))
            act.activation(gse[:], gsm[:], ACT.Exp, scale=1.0 / TAU).then_inc(gexp.sem, gexp.up(A))
            A.eng.wait_ge(rms_in.sem, rms_in.at(A, 1))
            rms_a(A, 0, 0, [ya[:, i, :] for i in range(2)])
            gain_a(A, 0, 0, ya)
            A.eng.wait_ge(rms_in.sem, rms_in.at(A, 2))
            rms_a(A, 1, 2, [u[:, i, :] for i in range(2)])
            for i in range(2):
                A.eng.wait_ge(cfm_ln.sem, cfm_ln.at(A, i + 1))
                act.activation(u[:, i, :], u[:, i, :], ACT.Silu, bias=col(B_CF + i)).then_inc(a_step.sem, a_step.up(A))
            A.eng.wait_ge(a_step.sem, a_step.last(A))
            rms_a(A, 2, 4, [u[:, i, :] for i in range(2)])
            gain_a(A, 2, 6, u)
            for d in range(2):
                A.eng.wait_ge(kd_tr.sem, kd_tr.at(A, d + 1))
                act.activation(kdT[:, 4 * d:4 * d + 4, :], bank[6 + d][:].rearrange("p (c n) -> p c n", c=4), ACT.Copy).then_inc(kd_ev.sem, kd_ev.up(A))
            tok_sd_a(A, 1, 16, 1.0 / GVD)
            tok_sd_a(A, 2, 4, 1.0 / W)
            tok_hi_a(A, 0, 2)
            rms_a(A, 3, 6, [proj[:, CQ + i, :] for i in range(2)])
            A.eng.wait_ge(c_val.sem, c_val.at(A, 2))
            rms_a(A, 4, 8, [proj[:, CKV, :]], scale=2.0)
            for i in range(3):
                A.eng.wait_ge(c_val.sem, c_val.at(A, i + 1))
                act.activation(c_hi[:, i, :], proj[:, CQ + i, :], ACT.Copy).then_inc(c_h.sem, c_h.up(A))
            A.eng.wait_ge(ring.done, ring.products(A, U_UQ))
            for hh in range(MH):
                act.activation(qh[0:MD, hh, :], bank[hh][0:MD, :], ACT.Copy).then_inc(head_ev.sem, head_ev.up(A))
            A.eng.wait_ge(ring.done, ring.products(A, U_UKV))
            for hh in range(MH):
                act.activation(kh[0:NOPE, hh, :], bank[hh][0:NOPE, :], ACT.Copy).then_inc(k_cp.sem, k_cp.up(A))
            A.eng.wait_ge(head_rope.sem, head_rope.at(A, 5))
            for hh in range(1, MH):
                act.activation(kh[R0:MD, hh, :], kh[R0:MD, 0, :], ACT.Copy).then_inc(k_cp.sem, k_cp.up(A))
            for n in range(16):
                A.eng.wait_ge(at_s.sem, at_s.at(A, n + 1))
                A.eng.wait_ge(at_mx.sem, at_mx.at(A, n + 1))
                if n >= 2:
                    A.eng.wait_ge(at_t.sem, at_t.at(A, n - 1))
                act.activation(pm[n % 2][:], bank[n % 2][:], ACT.Exp, bias=mmx[:, n:n + 1], scale=MLA_SCALE,
                                      accum_out=msum[:, n:n + 1]).then_inc(at_p.sem, at_p.up(A))
            tok_sd_a(A, 3, 4, 1.0 / W)
            tok_hi_a(A, 1, 4)
            norm_a(A, 0)
            load_gb(A, t["ln2_g"][bass.ds(l, 1), :], t["ln2_b"][bass.ds(l, 1), :])
            with act.Fori(0, FC // 2) as i:
                A.loop("a_up", i)
                for s in range(4):
                    A.eng.wait_ge(ring.done, ring.products(A, U_UP + s, turn=i))
                    act.activation(ubuf[:, s, 1:S + 1], bank[s][:], ACT.Copy).then_inc(up_ev.sem, up_ev.up(A))
                    if s == 1:
                        silu_hi(A, i, 0, False)
                silu_hi(A, i, 0, True)
                silu_hi(A, i, 1, False)
                silu_hi(A, i, 1, True)
                A.loop_end(FC // 2)
            norm_a(A, 1)

        def silu_hi(A, i, q, hi):
            if not hi:
                A.eng.wait_ge(up_cv.sem, up_cv.at(A, i * 4 + 2 * q + 1))
                A.eng.activation(cv[0][:], cv[0][:], ACT.Silu).then_inc(up_act.sem, up_act.up(A))
            else:
                A.eng.wait_ge(up_val.sem, up_val.at(A, i * 2 + q + 1))
                A.eng.activation(g_hi[:, bass.ds(i * 2 + q, 1), :], cv[0][:].unsqueeze(1), ACT.Copy).then_inc(up_hi.sem, up_hi.up(A))

        def gain_v(V, first, dst, src):
            for i in range(2):
                V.eng.wait_ge(y_hi.sem, y_hi.at(V, first + i + 1))
                V.eng.scalar_tensor_tensor(xT_lo[:, dst + i, :], src[:, i, :], col(G_BR + dst + i),
                                                  xT_hi[:, dst + i, :].bitcast(F32), MUL, SUB).then_inc(y_lo.sem, y_lo.up(V))

        def tok_v(V, n, k):
            v = V.eng
            v.tensor_tensor(flat(sq[:]), flat(og[:]), flat(og[:]), MUL).then_inc(v_step.sem, v_step.up(V))
            V.eng.wait_ge(v_step.sem, v_step.last(V))
            v.tensor_reduce(gst[:, 0:4], flat(sq[:]).rearrange("p (i w) -> p i w", i=NT), AX.X, ADD).then_inc(tok_ms.sem, tok_ms.up(V))
            V.eng.wait_ge(tok_ms.sem, tok_ms.last(V))
            V.eng.wait_ge(tok_sd.sem, tok_sd.at(V, k))
            v.reciprocal(gst[:, 32:36], gst[:, 16:20]).then_inc(v_step.sem, v_step.up(V))
            V.eng.wait_ge(v_step.sem, v_step.last(V))
            v.tensor_tensor(og[:], og[:], over(gst[:, 32:36].unsqueeze(2), [P, NT, W]), MUL).then_inc(tok_y.sem, tok_y.up(V))
            V.eng.wait_ge(tok_y.sem, tok_y.last(V))

        def tok_lo_v(V, n, dst):
            for x in range(2):
                V.eng.wait_ge(tok_hi.sem, tok_hi.at(V, 2 * n + x + 1))
                V.eng.scalar_tensor_tensor(xT_lo[:, dst + x, :], bank[6 + x][:], col(G_BR + dst + x),
                                                  xT_hi[:, dst + x, :].bitcast(F32), MUL, SUB).then_inc(tok_lo.sem, tok_lo.up(V))

        def vector1(V):
            v = V.eng
            V.eng.wait_ge(par_tr.sem, par_tr.at(V, 1))
            v.tensor_copy(pcol[:, 0:W_UP + 132], bank[7][:, 0:W_UP + 132]).then_inc(par_col.sem, par_col.up(V))
            V.eng.wait_ge(par_col.sem, par_col.last(V))
            v.memset(glu[:], 0.0).then_inc(v_step.sem, v_step.up(V))
            v.memset(scp[:], 0.0).then_inc(v_step.sem, v_step.up(V))
            V.eng.wait_ge(v_step.sem, v_step.last(V))
            for i in range(2):
                V.eng.wait_ge(proj_ev.sem, proj_ev.at(V, 2 * i + 2))
                v.tensor_tensor(glu[:, i, HALO:HALO + S], proj[:, 2 * i, :], proj[:, 2 * i + 1, :], MUL).then_inc(v_step.sem, v_step.up(V))
                V.eng.wait_ge(v_step.sem, v_step.last(V))
            for tap in range(TAPS):
                for i in range(2):
                    w = col(W_CF + 2 * tap + i)
                    if tap == 0:
                        v.tensor_scalar(u[:, i, :], glu[:, i, 0:S], w, None, MUL).then_inc(v_step.sem, v_step.up(V))
                    else:
                        v.scalar_tensor_tensor(u[:, i, :], glu[:, i, tap:tap + S], w, u[:, i, :], MUL, ADD).then_inc(v_step.sem, v_step.up(V))
                V.eng.wait_ge(v_step.sem, v_step.last(V))
            for i in range(2):
                V.eng.wait_ge(proj_ev.sem, proj_ev.at(V, 10))
                v.tensor_tensor(scp[:, i, 1:S + 1], proj[:, 6 + i, :], proj[:, 8 + i, :], MUL).then_inc(v_step.sem, v_step.up(V))
                V.eng.wait_ge(v_step.sem, v_step.last(V))
                v.tensor_scalar(ya[:, i, :], scp[:, i, 0:S], col(Q_G + i), None, MUL).then_inc(v_step.sem, v_step.up(V))
                V.eng.wait_ge(v_step.sem, v_step.last(V))
                for tap in (1, 2):
                    v.scalar_tensor_tensor(ya[:, i, :], scp[:, i, tap:tap + S], col(Q_G + 2 * tap + i), ya[:, i, :], MUL, ADD).then_inc(v_step.sem, v_step.up(V))
                    V.eng.wait_ge(v_step.sem, v_step.last(V))
                raised = rms_in if i else v_step
                v.tensor_tensor(ya[:, i, :], ya[:, i, :], proj[:, 4 + i, :], MUL).then_inc(raised.sem, raised.up(V))
                V.eng.wait_ge(raised.sem, raised.last(V))
            V.eng.wait_ge(la_part.sem, la_part.at(V, 4))
            for d in range(2):
                v.scalar_tensor_tensor(lax[:, d, :], lax[:, d, :], 0.0, qikd[:, d, 0, :], MIN, SUB).then_inc(v_step.sem, v_step.up(V))
                V.eng.wait_ge(v_step.sem, v_step.last(V))
                for c in range(NT):
                    cs = slice(c * P, c * P + P)
                    v.tensor_tensor_scan(eqk[:, d, 0, cs], ones[:], lax[:, d, cs], 0.0, MUL, ADD).then_inc(v_step.sem, v_step.up(V))
                V.eng.wait_ge(v_step.sem, v_step.last(V))
            x4 = lambda ap: ap.rearrange("p (c n) -> p c n", c=NT)
            b0, b1 = x4(eqk[:, 0, 0, :]), x4(eqk[:, 1, 0, :])
            xb = x4(eqk[:, 1, 1, :])
            v.tensor_tensor(xb, x4(lax[:, 1, :]), b1, SUB).then_inc(v_step.sem, v_step.up(V))
            V.eng.wait_ge(v_step.sem, v_step.last(V))
            tot0, tot1, mid0, mid1 = b0[:, :, P - 1:P], b1[:, :, P - 1:P], b0[:, :, 64:65], xb[:, :, 64:65]
            g3 = lambda d, k: gsm[:, d, k, :].unsqueeze(2)
            v.tensor_copy(g3(0, 0), mid0).then_inc(v_step.sem, v_step.up(V))
            v.tensor_tensor(g3(0, 1), tot0, mid0, SUB).then_inc(v_step.sem, v_step.up(V))
            v.tensor_copy(g3(0, 2), tot0).then_inc(v_step.sem, v_step.up(V))
            v.tensor_tensor(g3(1, 0), mid1, tot1, ADD).then_inc(v_step.sem, v_step.up(V))
            v.tensor_scalar(g3(1, 1), mid1, -1.0, None, MUL).then_inc(v_step.sem, v_step.up(V))
            v.tensor_copy(g3(1, 2), tot1).then_inc(v_step.sem, v_step.up(V))
            v.tensor_tensor(x4(lax[:, 0, :]), b0, over(mid0, [P, NT, P]), SUB).then_inc(v_step.sem, v_step.up(V))
            v.tensor_tensor(x4(lax[:, 1, :]), xb, over(mid1, [P, NT, P]), SUB).then_inc(la_x.sem, la_x.up(V))
            V.eng.wait_ge(la_x.sem, la_x.last(V))
            V.eng.wait_ge(rms_rs.sem, rms_rs.at(V, 1))
            for i in range(2):
                v.tensor_tensor(ya[:, i, :], ya[:, i, :], rstd[:], MUL).then_inc(y_val.sem, y_val.up(V))
                V.eng.wait_ge(y_val.sem, y_val.last(V))
            V.eng.wait_ge(cfm_mm.sem, cfm_mm.at(V, 1))
            for i in range(2):
                raised = rms_in if i else v_step
                v.tensor_tensor(u[:, i, :], u[:, i, :], bank[2][:], SUB).then_inc(raised.sem, raised.up(V))
                V.eng.wait_ge(raised.sem, raised.last(V))
            gain_v(V, 0, 0, ya)
            V.eng.wait_ge(rms_rs.sem, rms_rs.at(V, 2))
            for i in range(2):
                v.scalar_tensor_tensor(u[:, i, :], u[:, i, :], col(G_CF + i), rstd[:], MUL, MUL).then_inc(cfm_ln.sem, cfm_ln.up(V))
                V.eng.wait_ge(cfm_ln.sem, cfm_ln.last(V))
            V.eng.wait_ge(gexp.sem, gexp.at(V, 5))
            for d in range(2):
                qt, kt, qi, kd = eqk[:, d, 0, :], eqk[:, d, 1, :], qikd[:, d, 0, :], qikd[:, d, 1, :]
                v.scalar_tensor_tensor(qt, proj[:, 10, :], GK ** -0.5, qt, MUL, MUL).then_inc(v_step.sem, v_step.up(V))
                V.eng.wait_ge(v_step.sem, v_step.last(V))
                v.tensor_tensor(kt, proj[:, 11, :], kt, MUL).then_inc(v_step.sem, v_step.up(V))
                V.eng.wait_ge(v_step.sem, v_step.last(V))
                v.tensor_tensor(x4(qi), x4(qt), over(gse[:, d, 0, :].unsqueeze(2), [P, NT, P]), MUL).then_inc(v_step.sem, v_step.up(V))
                V.eng.wait_ge(v_step.sem, v_step.last(V))
                v.tensor_tensor(x4(kd), x4(kt), over(gse[:, d, 1, :].unsqueeze(2), [P, NT, P]), MUL).then_inc(kd_val.sem, kd_val.up(V))
                V.eng.wait_ge(kd_val.sem, kd_val.last(V))
            V.eng.wait_ge(rms_rs.sem, rms_rs.at(V, 3))
            for i in range(2):
                v.tensor_tensor(u[:, i, :], u[:, i, :], rstd[:], MUL).then_inc(y_val.sem, y_val.up(V))
                V.eng.wait_ge(y_val.sem, y_val.last(V))
            head = konst[:, K_HEAD:K_HEAD + GH].unsqueeze(2)
            for n in range(8):
                d, c = n // 4, n % 4 if n < 4 else 7 - n
                cs = slice(c * P, c * P + P)
                v.tensor_tensor(qbd[n % 2][:], over(eqk[:, d, 0, cs].unsqueeze(1), [P, GH, P]), over(head, [P, GH, P]), MUL).then_inc(g_q.sem, g_q.up(V))
                V.eng.wait_ge(g_q.sem, g_q.last(V))
                if n % 4 == 0:
                    v.memset(state[:], 0.0).then_inc(g_state.sem, g_state.up(V))
                    V.eng.wait_ge(g_state.sem, g_state.last(V))
                if n == 0:
                    gain_v(V, 2, 6, u)
                V.eng.wait_ge(g_s.sem, g_s.at(V, n + 1))
                tri = konst[:, K_TRF + P * d:K_TRF + P * d + P].unsqueeze(1)
                v.tensor_tensor(sT[n % 2][:], bank[n % 2][:].rearrange("p (h t) -> p h t", h=GH), over(tri, [P, GH, P]), MUL).then_inc(g_m.sem, g_m.up(V))
                if n % 4 != 3:
                    V.eng.wait_ge(g_st.sem, g_st.at(V, n + 1 if n < 4 else n))
                    v.tensor_tensor(stnew[:], bank[4 + n % 2][:, 0:W], konst[:, K_BLK:K_BLK + W], MUL).then_inc(v_step.sem, v_step.up(V))
                    V.eng.wait_ge(v_step.sem, v_step.last(V))
                V.eng.wait_ge(g_o.sem, g_o.at(V, n + 1))
                if n < 4:
                    v.tensor_copy(og[:, c, :], bank[2 + n % 2][:, 0:W]).then_inc(g_oev.sem, g_oev.up(V))
                    V.eng.wait_ge(g_oev.sem, g_oev.last(V))
                else:
                    v.tensor_tensor(og[:, c, :], og[:, c, :], bank[2 + n % 2][:, 0:W], ADD).then_inc(g_oev.sem, g_oev.up(V))
                    V.eng.wait_ge(g_oev.sem, g_oev.last(V))
                if n % 4 != 3:
                    v.scalar_tensor_tensor(state[:], state[:], gse[:, d, 2, c:c + 1], stnew[:], MUL, ADD).then_inc(g_state.sem, g_state.up(V))
                    V.eng.wait_ge(g_state.sem, g_state.last(V))
            og16 = flat(og[:]).rearrange("p (g n) -> p g n", n=GVD)
            v.tensor_tensor(flat(sq[:]), flat(og[:]), flat(og[:]), MUL).then_inc(v_step.sem, v_step.up(V))
            V.eng.wait_ge(v_step.sem, v_step.last(V))
            v.tensor_reduce(gst[:, 0:16], flat(sq[:]).rearrange("p (g n) -> p g n", n=GVD), AX.X, ADD).then_inc(tok_ms.sem, tok_ms.up(V))
            V.eng.wait_ge(tok_ms.sem, tok_ms.last(V))
            V.eng.wait_ge(tok_sd.sem, tok_sd.at(V, 1))
            v.reciprocal(gst[:, 32:48], gst[:, 16:32]).then_inc(v_step.sem, v_step.up(V))
            V.eng.wait_ge(v_step.sem, v_step.last(V))
            v.tensor_tensor(og16, og16, over(gst[:, 32:48].unsqueeze(2), [P, 16, GVD]), MUL).then_inc(v_step.sem, v_step.up(V))
            V.eng.wait_ge(v_step.sem, v_step.last(V))
            v.tensor_tensor(og[:], og[:], over(ghead[:].unsqueeze(1), [P, NT, W]), MUL).then_inc(v_step.sem, v_step.up(V))
            V.eng.wait_ge(v_step.sem, v_step.last(V))
            v.tensor_tensor(og[:], og[:], gvgg[:, :, W:S], MUL).then_inc(v_step.sem, v_step.up(V))
            V.eng.wait_ge(v_step.sem, v_step.last(V))
            tok_v(V, 0, 2)
            tok_lo_v(V, 0, 2)
            V.eng.wait_ge(rms_rs.sem, rms_rs.at(V, 4))
            for i in range(2):
                v.scalar_tensor_tensor(proj[:, CQ + i, :], proj[:, CQ + i, :], col(G_Q + i), rstd[:], MUL, MUL).then_inc(c_val.sem, c_val.up(V))
                V.eng.wait_ge(c_val.sem, c_val.last(V))
            V.eng.wait_ge(rms_rs.sem, rms_rs.at(V, 5))
            v.scalar_tensor_tensor(proj[:, CKV, :], proj[:, CKV, :], col(G_KV), rstd[:], MUL, MUL).then_inc(c_val.sem, c_val.up(V))
            V.eng.wait_ge(c_val.sem, c_val.last(V))
            for i in range(3):
                V.eng.wait_ge(c_h.sem, c_h.at(V, i + 1))
                v.tensor_tensor(c_lo[:, i, :], proj[:, CQ + i, :], c_hi[:, i, :].bitcast(F32), SUB).then_inc(c_l.sem, c_l.up(V))
            for hh in range(MH + 1):
                r = qh[R0:MD, hh, :] if hh < MH else proj[R0:MD, KR, :]
                o = r if hh < MH else kh[R0:MD, 0, :]
                b = bank[4 + hh] if hh < MH else bank[0]
                V.eng.wait_ge(head_sw.sem, head_sw.at(V, hh + 1))
                v.tensor_tensor(sq[R0:MD, 0, :], b[R0:MD, :], sinA[R0:MD, :], MUL).then_inc(v_step.sem, v_step.up(V))
                v.tensor_tensor(r, r, cosA[R0:MD, :], MUL).then_inc(v_step.sem, v_step.up(V))
                V.eng.wait_ge(v_step.sem, v_step.last(V))
                v.tensor_tensor(o, r, sq[R0:MD, 0, :], ADD).then_inc(head_rope.sem, head_rope.up(V))
                V.eng.wait_ge(head_rope.sem, head_rope.last(V))
            V.eng.wait_ge(ring.done, ring.products(V, U_UKV))
            v.tensor_copy(vml[:, 0:2, :], bank[4][:].rearrange("p (i n) -> p i n", i=2)).then_inc(v_step.sem, v_step.up(V))
            V.eng.wait_ge(v_step.sem, v_step.last(V))
            v.tensor_copy(vml[:, 2:4, :], bank[5][:].rearrange("p (i n) -> p i n", i=2)).then_inc(v_ev.sem, v_ev.up(V))
            V.eng.wait_ge(v_ev.sem, v_ev.last(V))
            for n in range(17):
                if n < 16:
                    V.eng.wait_ge(at_s.sem, at_s.at(V, n + 1))
                    v.tensor_reduce(mmx[:, n:n + 1], bank[n % 2][:], AX.X, MAX).then_inc(v_step.sem, v_step.up(V))
                    V.eng.wait_ge(v_step.sem, v_step.last(V))
                    v.tensor_scalar(mmx[:, n:n + 1], mmx[:, n:n + 1], -MLA_SCALE, None, MUL).then_inc(at_mx.sem, at_mx.up(V))
                    V.eng.wait_ge(at_mx.sem, at_mx.last(V))
                if n > 0:
                    V.eng.wait_ge(at_t.sem, at_t.at(V, n))
                    if n > 2:
                        V.eng.wait_ge(at_o.sem, at_o.at(V, n - 2))
                    v.tensor_copy(flat(pT[(n - 1) % 2][:]), bank[2 + (n - 1) % 2][:]).then_inc(at_te.sem, at_te.up(V))
                    V.eng.wait_ge(at_te.sem, at_te.last(V))
            v.reciprocal(mrs[:], msum[:]).then_inc(v_step.sem, v_step.up(V))
            V.eng.wait_ge(v_step.sem, v_step.last(V))
            V.eng.wait_ge(at_o.sem, at_o.at(V, 16))
            for i in range(NT):
                v.tensor_tensor(og[:, i, :].rearrange("p (g n) -> p g n", g=MH),
                                       bank[4 + i][:, 0:W].rearrange("p (g n) -> p g n", g=MH),
                                       over(mrs[:].rearrange("p (g i) -> p g i", i=NT)[:, :, i:i + 1], [P, MH, NOPE]), MUL).then_inc(v_step.sem, v_step.up(V))
            V.eng.wait_ge(v_step.sem, v_step.last(V))
            tok_v(V, 1, 3)
            tok_lo_v(V, 1, 4)
            norm_v(V, 0, U_OUT + KC - 1)
            v.memset(ubuf[:, :, 0:S + 2:S + 1], 0.0).then_inc(v_step.sem, v_step.up(V))
            V.eng.wait_ge(v_step.sem, V.alone(v_step.last(V)))
            with v.Fori(0, FC // 2) as i:
                V.loop("v_up", i)
                for q in range(2):
                    for x in range(2):
                        s = 2 * q + x
                        w = lambda tap: flat(pcol[:, W_UP + 22 * x + q + tap * 44:].rearrange("p (n a) -> p n a", a=1)[:, bass.ds(i * 2, 1), :])
                        V.eng.wait_ge(up_ev.sem, up_ev.at(V, i * 4 + s + 1))
                        v.tensor_scalar(cv[x][:], ubuf[:, s, 1:S + 1], w(1), None, MUL).then_inc(v_step.sem, v_step.up(V))
                        V.eng.wait_ge(v_step.sem, v_step.last(V))
                        v.scalar_tensor_tensor(cv[x][:], ubuf[:, s, 0:S], w(0), cv[x][:], MUL, ADD).then_inc(v_step.sem, v_step.up(V))
                        V.eng.wait_ge(v_step.sem, v_step.last(V))
                        v.scalar_tensor_tensor(cv[x][:], ubuf[:, s, 2:S + 2], w(2), cv[x][:], MUL, ADD).then_inc(up_cv.sem, up_cv.up(V))
                        V.eng.wait_ge(up_cv.sem, up_cv.last(V))
                    V.eng.wait_ge(up_act.sem, up_act.at(V, i * 2 + q + 1))
                    v.tensor_tensor(cv[0][:], cv[0][:], cv[1][:], MUL).then_inc(up_val.sem, up_val.up(V))
                    V.eng.wait_ge(up_val.sem, up_val.last(V))
                    V.eng.wait_ge(up_hi.sem, up_hi.at(V, i * 2 + q + 1))
                    v.tensor_tensor(g_lo[:, bass.ds(i * 2 + q, 1), :], cv[0][:].unsqueeze(1),
                                           g_hi[:, bass.ds(i * 2 + q, 1), :].bitcast(F32), SUB).then_inc(up_lo.sem, up_lo.up(V))
                    V.eng.wait_ge(up_lo.sem, up_lo.last(V))
                V.loop_end(FC // 2)
            norm_v(V, 1, U_DOWN + FC - 1)

        C_POOL, C_Q, C_K, C_V, C_IQ, C_IK, C_IW, C_MQ, C_GATES = 0, 512, 1024, 1536, 2048, 2560, 2624, 2632, 3144
        CHUNKS2 = ([C_POOL + P * i for i in range(12)] + [C_IQ + P * i for i in range(4)] + [C_IK]
                   + [C_MQ + P * i for i in range(4)])
        V_CH = {c: u for c, u in zip(range(21), list(range(12)) + list(range(16, 21)) + list(range(22, 26)))}
        U2_V, U2_IW, U2_PW, U2_MK, U2_MV, U2_G, U2_OUT, U2_R = 12, 21, 26, 27, 31, 35, 83, 91
        IK, MQ0, B_GT, P_SC, NROWS = 16, 17, 21, 45, 49
        AH, HD, MHD, NM = 8, 64, 128, 256
        NSEL = 128
        NE, NG, DE = 16, 4, 512
        NB = 2 * S // P + NE
        OUT_OF, TAKEN, HIDE = -1e38, -3e38, -1e30

        two = ExitStack()
        s5 = lambda name, shape, dt=F32: sb(name, shape, dt, two)
        qk = s5("qk", [P, 8, S])
        vv = s5("vv", [P, NT, S])
        iq = s5("iq", [P, 4, S])
        b_hi, b_lo = s5("b_hi", [P, 12, S], F32R), s5("b_lo", [P, 12, S], F32R)
        iwc = s5("iwc", [P, NT, AH])
        st8 = s5("st8", [P, 8])
        mmx2, msm2, mrc = s5("mem_max", [P, 16]), s5("mem_sum", [P, 16]), s5("mem_rec", [P, 4])
        asum, amx, ars = s5("asum", [P, AH]), s5("amx", [P, AH]), s5("ars", [P, AH])
        phase = ExitStack()
        s6 = lambda name, shape, dt=F32: sb(name, shape, dt, phase)
        up = s6("up", [P, 4, S])
        mq = s6("mq", [P, 4, S])
        mk = s6("mk", [P, 4, NM])
        mvv = s6("mvv", [P, 2, S])
        phase.close()
        phase = ExitStack()
        acc = s6("acc", [P, S])
        rel = [s6(f"rel{i}", [P, S]) for i in range(2)]
        sc = [s6(f"sc{i}", [P, S]) for i in range(2)]
        apT = [s6(f"apT{i}", [P, NT, P]) for i in range(2)]
        otok = s6("otok", [P, S])
        mask = acc
        phase.close()
        phase = ExitStack()
        sg, gt = [s6(f"sg{i}", [P, S]) for i in range(2)], s6("gt", [P, S])
        phase.close()
        two.close()
        moe = ExitStack()
        s7 = lambda name, shape, dt=F32: sb(name, shape, dt, moe)
        wt = [s7(f"wt{i}", [P, 4, S]) for i in range(6)]
        xb = [s7(f"xb{i}", [P, D]) for i in range(2)]
        xbT = s7("xbT", [P, KC, P])
        hs, hTm = s7("hs", [P, S]), s7("hTm", [P, 4, P])
        yb = [s7(f"yb{i}", [P, D]) for i in range(2)]
        yg = [s7(f"yg{i}", [P, D]) for i in range(4)]
        rsc, rbi = s7("rsc", [P, NT, NE]), s7("rbi", [P, NT, NE])
        rgs, rmx, rix = s7("rgs", [P, NT, 8]), s7("rmx", [P, 8]), s7("rix", [P, 8], U32)
        rtm = s7("rtm", [P, NT, 4, 8])
        oh = s7("oh", [P, 3, NT, NE])
        rbias = s7("rbias", [P, NE])
        gw = s7("gw", [P, NT, 4])
        cnt, nblk, pend, bst = (s7(n, [P, NE]) for n in ("cnt", "nblk", "pend", "bst"))
        rtmp = s7("rtmp", [P, NT, NE])
        dest, desti = s7("dest", [P, 2, NT]), s7("desti", [P, 2, NT], U32)
        tokid = s7("tokid", [P, NT], U32)
        zid = s7("zid", [P, NB + 1], U32)
        bcmp = s7("bcmp", [P, NB + 1, NE])
        bef, bei = s7("bef", [P, NB + 1]), s7("bei", [P, NB + 1], I32)
        slots = s7("slots", [P, NB + 1], U32)
        sid = [s7(f"sid{i}", [P, 1], U32) for i in range(2)]
        moe.close()
        memrow = gb
        om = gb[:, :, :].rearrange("p a (b n) -> p (a b) n", n=S)
        memT_hi, memT_lo = (b[:, 4:8, :].rearrange("p c (x m) -> p (c x) m", x=2) for b in (b_hi, b_lo))
        pd = om
        work = [flat(mk[:, x:x + 2, :]) for x in (0, 2)]
        prow_b = vv[:, 0, 0:P]
        brow = flat(mvv[0:1, :, :])
        ikd, turned = cosA, sinA
        h_dram = nc.dram_tensor("h_rows", (S, D), F32).ap()
        y_dram = nc.dram_tensor("y_rows", (NB * P, D), F32).ap()
        slot_dram = nc.dram_tensor("slot_token", ((NB + 1) * P, 1), U32).ap()

        mem_tr, mem_hi, mem_lo, v2_ev, iw_ev, mk_ev, mv_ev, pool_d, pool_dh, pool_dl, pool_hi, pool_lo = (signal(n) for n in (
            "mem_tr", "mem_hi", "mem_lo", "v2_ev", "iw_ev", "mk_ev", "mv_ev", "pool_d", "pool_dh", "pool_dl", "pool_hi", "pool_lo"))
        ix_s, ix_rel, ix_use, a_sc, a_te, a_or, a_ot, a_oh, a_ol = (signal(n) for n in (
            "ix_s", "ix_rel", "ix_use", "a_sc", "a_te", "a_or", "a_ot", "a_oh", "a_ol"))
        m_s, m_mx, m_p, m_t, m_te, m_o, m_or, m_ot, m_oh, m_ol = (signal(n) for n in (
            "m_s", "m_mx", "m_p", "m_t", "m_te", "m_o", "m_or", "m_ot", "m_oh", "m_ol"))
        gt_sig, gt_use, mg_hi, mg_lo, rt_sc, rt_oh, rt_rank, rt_dest, be_ok, bidx, sid_ok = (signal(n) for n in (
            "gt_sig", "gt_use", "mg_hi", "mg_lo", "rt_sc", "rt_oh", "rt_rank", "rt_dest", "be_ok", "bidx", "sid_ok"))
        x_tr, x_ev, act_h, h_val, h_tr, h_ev, y_ev, y_free, yg_use, wt_done = (signal(n) for n in (
            "x_tr", "x_ev", "act_h", "h_val", "h_tr", "h_ev", "y_ev", "y_free", "yg_use", "wt_done"))
        slot_zero, slot_st, slot_ld, h_st, rb_ld, y_st = (signal(n, 16) for n in (
            "slot_zero", "slot_st", "slot_ld", "h_st", "rb_ld", "y_st"))
        wt_ld = [signal(f"wt_ld{i}", 16) for i in range(6)]
        xbl = [signal(f"xb_ld{i}", 16) for i in range(2)]
        ygl = [signal(f"yg_ld{i}", 16) for i in range(4)]

        def loads2(E):
            l, sp = E.layer, E.eng
            w = t["w_in_2"][bass.ds(l, 1)].rearrange("o (k p) n -> (o p) k n", p=P)

            def wide(j, c):
                dst = cols3(j)
                ring.load(E, j, [(dst[:, x:x + 4, :], w[:, x:x + 4, c:c + P]) for x in (0, 4)])

            def pairs(j0, src, c0):
                for j in range(4):
                    dst = ring.raw[(j0 + j) % RAW][:, :].rearrange("p (k n) -> p k n", k=2)
                    ring.load(E, j0 + j, [(dst[:, k:k + 1, :], src[:, 2 * j + k:2 * j + k + 1, c0:c0 + S]) for k in range(2)])

            for j in range(12):
                wide(j, CHUNKS2[j])
            pairs(U2_V, w, C_V)
            for j in range(16, 20):
                wide(j, CHUNKS2[j - 4])
            dst = cols3(20)
            ring.load(E, 20, [(dst[:, :, x:x + HD], w[:, :, C_IK:C_IK + HD]) for x in (0, HD)])
            dst = ring.raw[U2_IW % RAW][:, 0:64].rearrange("p (k c) -> p k c", k=KC)
            ring.load(E, U2_IW, [(dst[:, x:x + 4, :], w[:, x:x + 4, C_IW:C_IW + AH]) for x in (0, 4)])
            for j in range(4):
                wide(22 + j, C_MQ + P * j)
            pw = t["pool_w_2"][bass.ds(l, 1)].rearrange("o g c e -> (o c) g e")
            dst = ring.raw[U2_PW % RAW][:, 0:S].rearrange("p (g e) -> p g e", g=4)
            ring.load(E, U2_PW, [(dst[:, x:x + 2, :], pw[:, x:x + 2, :]) for x in (0, 2)])
            wm = t["w_mem_kv_2"][bass.ds(l, 1)].rearrange("o (k p) n -> (o p) k n", p=P)
            for j in range(4):
                dst = cols3(U2_MK + j)
                ring.load(E, U2_MK + j, [(dst[:, x:x + 4, :], wm[:, x:x + 4, j * P:j * P + P]) for x in (0, 4)])
            pairs(U2_MV, wm, S)
            wb = [t["w_br_2"][bass.ds(l, 1), n, :, :].rearrange("o (k p) n -> (o p) k n", p=P) for n in range(3)]
            with sp.Fori(0, 4) as i:
                for dd in range(2):
                    for n in range(3):
                        j = U2_G + 6 * dd + 2 * n
                        dst = cols3(j)
                        ring.load(E, j, [(dst[:, x:x + 4, :], w[:, x:x + 4, bass.ds(i * (2 * P) + (C_GATES + n * D + dd * P), P)])
                                         for x in (0, 4)], turn=i, size=12)
                        dst = ring.raw[(j + 1) % RAW][:, 0:S].rearrange("p (k c) -> p k c", k=4)
                        ring.load(E, j + 1, [(dst[:, x:x + 2, :], wb[n][:, x:x + 2, bass.ds(i * (2 * P) + dd * P, P)])
                                             for x in (0, 2)], turn=i, size=12)
            rows_unit(E, U2_OUT, KC, t["w_out_2"], l)
            wr = t["w_router_2"].rearrange("(k p) n -> p k n", p=P)
            dst = ring.raw[U2_R % RAW][:, 0:P].rearrange("p (k c) -> p k c", k=KC)
            ring.load(E, U2_R, [(dst[:, x:x + 4, :], wr[:, x:x + 4, :]) for x in (0, 4)])
            for i in range(NT):
                E.eng.wait_ge(norm_z.sem, E.alone(norm_z.at(E, i + 1)))
                sp.dma_start(h_dram[i * P:i * P + P, :], h[:, i, :]).then_inc(h_st.sem, h_st.up(E))
            E.eng.wait_ge(be_ok.sem, E.alone(be_ok.at(E, 1)))
            w1, w3 = (t[n].rearrange("l e (k p) n -> (l e) p k n", p=P) for n in ("w1_2", "w3_2"))
            w2 = t["w2_2"].rearrange("l e (k p) n -> (l e) p k n", p=P)
            with sp.Fori(0, NB // 2) as bb:
                E.loop("sp_moe", bb)
                for q in range(2):
                    e = sp.value_load(bei[0:1, bass.ds(bb * 2 + q, 1)], min_val=0, max_val=NE - 1)
                    le = sp.snap(l * NE + e)
                    for i in range(6):
                        src = (w1, w3, w2)[i // 2]
                        if i < 4:
                            src = src[bass.ds(le, 1), :, 4 * (i % 2):4 * (i % 2) + 4, :].rearrange("o p k n -> (o p) k n")
                            dst = wt[i][:]
                        else:
                            src = src[bass.ds(le, 1), :, 2 * (i % 2):2 * (i % 2) + 2, :].rearrange("o p k n -> (o p) k n")
                            dst = wt[i][:].rearrange("p (k x) n -> p k (x n)", k=2)
                        E.eng.wait_ge(wt_done.sem, E.alone(wt_done.at(E, bb * 12 + (6 * q + i + 1 - 6))))
                        sp.dma_start(dst, src).then_inc(wt_ld[i].sem, wt_ld[i].up(E))
                E.loop_end(NB // 2)

        def splits2(G):
            g = G.eng
            widths = {U2_IW: 64, U2_PW: S}
            for j in range(U2_G):
                ring.part(G, j, width=widths.get(j, 1024))
            with g.Fori(0, 4) as i:
                for s in range(12):
                    ring.part(G, U2_G + s, turn=i, size=12, width=S if s % 2 else 1024)
            for j in range(U2_OUT, 92):
                ring.part(G, j, width=P if j == U2_R else 1024)
            g.iota(tokid[:], pattern=[[P, NT]], base=0, channel_multiplier=1).then_inc(bidx.sem, bidx.up(G))
            g.memset(zid[:], 0).then_inc(bidx.sem, bidx.up(G))
            G.eng.wait_ge(bidx.sem, G.alone(bidx.last(G)))
            g.dma_start(slot_dram.rearrange("(p b) o -> p (b o)", p=P), zid[:]).then_inc(slot_zero.sem, slot_zero.up(G))
            G.eng.wait_ge(slot_zero.sem, G.alone(slot_zero.last(G)))
            G.eng.wait_ge(rt_dest.sem, G.alone(rt_dest.at(G, 1)))
            for a in range(2):
                for i in range(NT):
                    g.indirect_dma_start(
                        out=slot_dram, out_offset=bass.IndirectOffsetOnAxis(ap=desti[:, a, i:i + 1], axis=0),
                        in_=tokid[:, i:i + 1], in_offset=None).then_inc(slot_st.sem, slot_st.up(G))
            G.eng.wait_ge(slot_st.sem, G.alone(slot_st.last(G)))
            g.dma_start(slots[:], slot_dram.rearrange("(b p) o -> p (b o)", p=P), allow_slow_non_contiguous=True).then_inc(slot_ld.sem, slot_ld.up(G))
            G.eng.wait_ge(slot_ld.sem, G.alone(slot_ld.last(G)))
            G.eng.wait_ge(h_st.sem, G.alone(h_st.at(G, 4)))

            def gather(b, x):
                g.tensor_copy(sid[x][:], slots[:, bass.ds(b, 1)]).then_inc(sid_ok.sem, sid_ok.up(G))
                G.eng.wait_ge(sid_ok.sem, G.alone(sid_ok.last(G)))
                g.indirect_dma_start(
                    out=xb[x][:], out_offset=None, in_=h_dram,
                    in_offset=bass.IndirectOffsetOnAxis(ap=sid[x][:, 0:1], axis=0)).then_inc(xbl[x].sem, xbl[x].up(G))

            gather(0, 0)
            with g.Fori(0, NB // 2) as bb:
                G.loop("g_moe", bb)
                for q in range(2):
                    G.eng.wait_ge(x_tr.sem, G.alone(x_tr.at(G, bb * 4 + 2 * q)))
                    gather(bb * 2 + (q + 1), 1 - q)
                    G.eng.wait_ge(y_ev.sem, G.alone(y_ev.at(G, bb * 4 + (2 * q + 2))))
                    g.dma_start(y_dram[bass.ds(bb * (2 * P) + q * P, P), :], yb[q][:]).then_inc(y_st.sem, y_st.up(G))
                    G.eng.wait_ge(y_st.sem, G.alone(y_st.last(G)))
                    g.nop().then_inc(y_free.sem, y_free.up(G))
                G.loop_end(NB // 2)
            for n in range(8):
                if n >= 4:
                    G.eng.wait_ge(yg_use.sem, G.alone(yg_use.at(G, n - 2 if n % 2 == 0 else n - 3)))
                g.indirect_dma_start(
                    out=yg[n % 4][:], out_offset=None, in_=y_dram,
                    in_offset=bass.IndirectOffsetOnAxis(ap=desti[:, n % 2, n // 2:n // 2 + 1], axis=0)).then_inc(ygl[n % 4].sem, ygl[n % 4].up(G))

        def tensor2(T):
            pe = T.eng
            T.eng.wait_ge(par_ld.sem, par_ld.at(T, 11))
            T.eng.wait_ge(norm_lo.sem, T.alone(norm_lo.at(T, 0)))
            pe.transpose(bank[7][:, 0:NROWS], prow_b[0:NROWS, :], ident[0:NROWS, 0:NROWS]).then_inc(par_tr.sem, par_tr.up(T))
            for b in range(4):
                for k in range(2):
                    for m in range(2):
                        last = pe.transpose(bank[b][:, k * NM + m * P:k * NM + m * P + P],
                                            memrow[:, m, (2 * b + k) * P:(2 * b + k + 1) * P], ident)
                last.then_inc(mem_tr.sem, mem_tr.up(T))
            T.eng.wait_ge(mem_lo.sem, mem_lo.at(T, 4))

            def swap(r):
                c = r + 4
                T.eng.wait_ge(proj_ev.sem, proj_ev.at(T, c + 1))
                if r >= 2:
                    T.eng.wait_ge(head_rope.sem, head_rope.at(T, r - 1))
                src = qk[:, r, :] if r < 8 else iq[:, r - 8, :] if r < 12 else ikd[:]
                pe.matmul(bank[4 + r % 2][:], konst[:, K_SWB:K_SWB + P], src, start=True, stop=True).then_inc(head_sw.sem, head_sw.up(T))

            for c in range(21):
                if c == 12:
                    T.eng.wait_ge(proj_ev.sem, proj_ev.at(T, 12))
                    for j in range(4):
                        wh, wl = ring.weights(T, U2_V + j)
                        for i in range(NT):
                            if j == 0:
                                pe.matmul(bank[i][:], ones[0:1, :], brow[:, 0:S], start=True, stop=False)
                            for kk in range(2):
                                k, cs, n = 2 * j + kk, slice(i * P, i * P + P), slice(kk * S, kk * S + S)
                                last = triple(pe, bank[i][:], xT_hi[:, k, cs], xT_lo[:, k, cs], wh[:, n], wl[:, n], False, k == 7)
                        last.then_inc(ring.done, 1)
                    T.eng.wait_ge(v2_ev.sem, v2_ev.at(T, 4))
                elif c >= 4:
                    T.eng.wait_ge(proj_ev.sem, proj_ev.at(T, c - 3))
                if c == 17:
                    wh, wl = (w[:, 0:64].rearrange("p (k c) -> p k c", k=KC) for w in ring.weights(T, U2_IW))
                    for i in range(NT):
                        o, cs = bank[6][:, 8 * i:8 * i + 8], slice(i * P, i * P + P)
                        pe.matmul(o, ones[0:1, :], brow[:, S:S + 8], start=True, stop=False)
                        for k in range(KC):
                            last = triple(pe, o, xT_hi[:, k, cs], xT_lo[:, k, cs], wh[:, k, :], wl[:, k, :], False, k == 7)
                    last.then_inc(ring.done, 1)
                chunk(T, ring, V_CH[c], bank[c % 4])
                if 5 <= c < 18:
                    swap(c - 5)
            wh, wl = (w[:, 0:S].rearrange("p (g e) -> p g e", g=4) for w in ring.weights(T, U2_PW))
            T.eng.wait_ge(proj_ev.sem, proj_ev.at(T, 21))
            T.eng.wait_ge(pool_dl.sem, pool_dl.at(T, 4))
            for g4 in range(4):
                last = triple(pe, bank[g4][:], wh[:, g4, :], wl[:, g4, :], b_hi[:, g4, :], b_lo[:, g4, :], True, True)
            last.then_inc(ring.done, 1)
            T.eng.wait_ge(head_rope.sem, head_rope.at(T, 13))
            for j in range(4):
                if j >= 2:
                    T.eng.wait_ge(mk_ev.sem, mk_ev.at(T, j - 1))
                chunk(T, ring, U2_MK + j, bank[4 + j % 2], n=NM, src=(memT_hi, memT_lo))
            T.eng.wait_ge(iw_ev.sem, iw_ev.at(T, 1))
            for j in range(4):
                wh, wl = ring.weights(T, U2_MV + j)
                for m in range(2):
                    for kk in range(2):
                        k, cs, n = 2 * j + kk, slice(m * P, m * P + P), slice(kk * S, kk * S + S)
                        last = triple(pe, bank[6 + m][:], memT_hi[:, k, cs], memT_lo[:, k, cs], wh[:, n], wl[:, n], k == 0, k == 7)
                last.then_inc(ring.done, 1)
            T.eng.wait_ge(mv_ev.sem, mv_ev.at(T, 2))
            T.eng.wait_ge(mk_ev.sem, mk_ev.at(T, 4))
            T.eng.wait_ge(pool_lo.sem, pool_lo.at(T, 4))
            for n in range(18):
                if n < 16:
                    i, hh = n // 4, n % 4
                    if n >= 2:
                        T.eng.wait_ge(m_p.sem, m_p.at(T, n - 1))
                    pe.matmul(bank[n % 2][:, 0:NM], mq[:, hh, i * P:i * P + P], mk[:, hh, :], start=True, stop=True).then_inc(m_s.sem, m_s.up(T))
                if 0 < n < 17:
                    m = n - 1
                    T.eng.wait_ge(m_p.sem, m_p.at(T, m + 1))
                    for k in range(2):
                        last = pe.transpose(bank[2 + m % 2][:, k * P:k * P + P], up[:, m % 2, k * P:k * P + P], ident)
                    last.then_inc(m_t.sem, m_t.up(T))
                if n > 1:
                    m = n - 2
                    i, hh = m // 4, m % 4
                    T.eng.wait_ge(m_te.sem, m_te.at(T, m + 1))
                    if hh == 0 and i >= 2:
                        T.eng.wait_ge(m_or.sem, m_or.at(T, i - 1))
                    for k in range(2):
                        last = pe.matmul(bank[4 + i % 2][:, hh * P:hh * P + P], up[:, 2 + m % 2, k * P:k * P + P],
                                         mvv[:, k, hh * P:hh * P + P], start=k == 0, stop=k == 1)
                    last.then_inc(m_o.sem, m_o.up(T))
            for i in range(NT):
                T.eng.wait_ge(m_or.sem, m_or.at(T, i + 1))
                if i >= 2:
                    T.eng.wait_ge(m_ol.sem, m_ol.at(T, i - 1))
                for c in range(4):
                    last = pe.transpose(bank[6 + i % 2][:, c * P:c * P + P], om[:, i, c * P:c * P + P], ident)
                last.then_inc(m_ot.sem, m_ot.up(T))
            ni = na = 0
            for i in range(NT):
                nk, qs = (i + 1) * P, slice(i * P, i * P + P)
                if i:
                    for hh in range(AH):
                        r = slice(64 * (hh % 2), 64 * (hh % 2) + 64)
                        if ni >= 2:
                            T.eng.wait_ge(ix_rel.sem, ix_rel.at(T, ni - 1))
                        ni += 1
                        pe.matmul(bank[hh % 2][:, 0:nk], iq[r, hh // 2, qs], ikd[r, 0:nk], start=True, stop=True).then_inc(ix_s.sem, ix_s.up(T))
                for n in range(AH + 2):
                    if n < AH:
                        r, k = slice(64 * (n % 2), 64 * (n % 2) + 64), na + n
                        if k >= 2:
                            T.eng.wait_ge(a_sc.sem, a_sc.at(T, k - 1))
                        pe.matmul(bank[2 + n % 2][:, 0:nk], qk[r, n // 2, qs], qk[r, 4 + n // 2, 0:nk], start=True, stop=True).then_inc(at_s.sem, at_s.up(T))
                    if 0 < n <= AH:
                        m, k = n - 1, na + n - 1
                        T.eng.wait_ge(at_p.sem, at_p.at(T, k + 1))
                        for x in range(i + 1):
                            last = pe.transpose(bank[4 + m % 2][:, x * P:x * P + P], sc[m % 2][:, x * P:x * P + P], ident)
                        last.then_inc(at_t.sem, at_t.up(T))
                    if n > 1:
                        m, k = n - 2, na + n - 2
                        T.eng.wait_ge(a_te.sem, a_te.at(T, k + 1))
                        for x in range(i + 1):
                            last = pe.matmul(bank[6][:, m * HD:m * HD + HD], apT[m % 2][:, x, :], vv[:, x, m * HD:m * HD + HD],
                                             start=x == 0, stop=x == i)
                        last.then_inc(at_o.sem, at_o.up(T))
                na += AH
                T.eng.wait_ge(a_or.sem, a_or.at(T, i + 1))
                for c in range(4):
                    last = pe.transpose(bank[7][:, c * P:c * P + P], otok[:, c * P:c * P + P], ident)
                last.then_inc(a_ot.sem, a_ot.up(T))
                T.eng.wait_ge(a_ol.sem, T.alone(a_ol.at(T, i + 1)))
            with pe.Fori(0, 4) as i:
                for s in range(0, 12, 2):
                    u6 = s // 2
                    T.eng.wait_ge(gt_use.sem, gt_use.at(T, i * 6 + (u6 - 1)))
                    chunk(T, ring, U2_G + s, bank[2 * (u6 % 2)], turn=i, size=12)
                    n = u6 % 3
                    wh, wl = (w[:, 0:S].rearrange("p (k c) -> p k c", k=4) for w in ring.weights(T, U2_G + s + 1, i, 12))
                    for k in range(4):
                        last = triple(pe, bank[2 * (u6 % 2) + 1][:], wh[:, k, :], wl[:, k, :], b_hi[:, 4 * n + k, :], b_lo[:, 4 * n + k, :],
                                      k == 0, k == 3)
                    last.then_inc(ring.done, 1)
            for k in range(KC):
                T.eng.wait_ge(mg_lo.sem, mg_lo.at(T, k + 1))
            rows_products(T, U2_OUT, KC, xT_hi, xT_lo)
            norm_pe(T, 0)
            T.eng.wait_ge(norm_lo.sem, norm_lo.at(T, 8))
            wh, wl = (w[:, 0:P].rearrange("p (k e) -> p k e", k=KC) for w in ring.weights(T, U2_R))
            for i in range(NT):
                for k in range(KC):
                    cs = slice(i * P, i * P + P)
                    last = triple(pe, bank[0][:, NE * i:NE * i + NE], xT_hi[:, k, cs], xT_lo[:, k, cs], wh[:, k, :], wl[:, k, :], k == 0, k == 7)
            last.then_inc(ring.done, 1)
            T.eng.wait_ge(rt_oh.sem, rt_oh.at(T, 1))
            for i in range(NT + 1):
                o = bank[1][:, NE * i:NE * i + NE]
                for j in range(min(i, NT - 1) + 1):
                    w = konst[:, K_TRF:K_TRF + P] if j == i else ones[:]
                    last = pe.matmul(o, w, oh[:, 2, j, :], start=j == 0, stop=j == min(i, NT - 1))
            last.then_inc(rt_rank.sem, rt_rank.up(T))
            T.eng.wait_ge(rt_dest.sem, rt_dest.at(T, 1))

            def transposed(b, x):
                for y in range(2):
                    for k in range(4):
                        last = pe.transpose(bank[y][:, k * P:k * P + P], xb[x][:, (4 * y + k) * P:(4 * y + k + 1) * P], ident)
                    last.then_inc(x_tr.sem, x_tr.up(T))

            T.eng.wait_ge(xbl[0].sem, xbl[0].at(T, 1))
            transposed(0, 0)
            T.eng.wait_ge(x_ev.sem, T.alone(x_ev.at(T, 2)))
            with pe.Fori(0, NB // 2) as bb:
                T.loop("t_moe", bb)
                for q in range(2):
                    T.eng.wait_ge(x_ev.sem, x_ev.at(T, bb * 4 + (2 * q + 2)))
                    for i in range(4):
                        T.eng.wait_ge(wt_ld[i].sem, wt_ld[i].at(T, bb * 2 + (q + 1)))
                        for k in range(4):
                            last = pe.matmul(bank[2 + i // 2][:], xbT[:, 4 * (i % 2) + k, :], wt[i][:, k, :],
                                             start=i % 2 == 0 and k == 0, stop=i % 2 == 1 and k == 3)
                        last.then_inc(wt_done.sem, wt_done.up(T))
                    T.eng.wait_ge(xbl[1 - q].sem, xbl[1 - q].at(T, bb + (1 + q)))
                    transposed(None, 1 - q)
                    T.eng.wait_ge(h_val.sem, h_val.at(T, bb * 2 + (q + 1)))
                    for k in range(4):
                        last = pe.transpose(bank[4][:, k * P:k * P + P], hs[:, k * P:k * P + P], ident)
                    last.then_inc(h_tr.sem, h_tr.up(T))
                    T.eng.wait_ge(y_ev.sem, y_ev.at(T, bb * 4 + 2 * q))
                    T.eng.wait_ge(h_ev.sem, h_ev.at(T, bb * 2 + (q + 1)))
                    for i in range(2):
                        T.eng.wait_ge(wt_ld[4 + i].sem, wt_ld[4 + i].at(T, bb * 2 + (q + 1)))
                        for k in range(2):
                            for x in range(2):
                                last = pe.matmul(bank[5 + x][:], hTm[:, 2 * i + k, :], wt[4 + i][:, 2 * k + x, :],
                                                 start=i == 0 and k == 0, stop=i == 1 and k == 1)
                        last.then_inc(wt_done.sem, wt_done.up(T))
                T.loop_end(NB // 2)
            T.eng.wait_ge(x_ev.sem, x_ev.at(T, 2 * NB + 2))
            T.eng.wait_ge(y_ev.sem, y_ev.at(T, 2 * NB))
            norm_pe(T, 1)

        def scalar2(A):
            act, l = A.eng, A.layer
            pl = par_ld
            b2 = lambda c, n: t["b_in_2"][bass.ds(l, 1), c:c + n * P].rearrange("o (c p) -> (o c) p", p=P)
            act.dma_start(prow_b[0:12, :], b2(0, 12)).then_inc(pl.sem, pl.up(A))
            act.dma_start(prow_b[12:16, :], b2(C_IQ, 4)).then_inc(pl.sem, pl.up(A))
            for x in (0, HD):
                act.dma_start(prow_b[IK:IK + 1, x:x + HD], t["b_in_2"][bass.ds(l, 1), C_IK:C_IK + HD]).then_inc(pl.sem, pl.up(A))
            act.dma_start(prow_b[MQ0:MQ0 + 4, :], b2(C_MQ, 4)).then_inc(pl.sem, pl.up(A))
            act.dma_start(prow_b[B_GT:B_GT + 24, :], b2(C_GATES, 24)).then_inc(pl.sem, pl.up(A))
            act.dma_start(prow_b[P_SC:P_SC + 4, :], t["pool_scale_2"][bass.ds(l, 1), :].rearrange("o (c p) -> (o c) p", p=P)).then_inc(pl.sem, pl.up(A))
            act.dma_start(brow[:, 0:S], t["b_in_2"][bass.ds(l, 1), C_V:C_V + S]).then_inc(pl.sem, pl.up(A))
            act.dma_start(brow[:, S:S + 8], t["b_in_2"][bass.ds(l, 1), C_IW:C_IW + 8]).then_inc(pl.sem, pl.up(A))
            mem = t["mem_2"].rearrange("o (m p) d -> (o p) m d", p=P)
            for m in range(2):
                act.dma_start(memrow[:, m, :], mem[:, m, :]).then_inc(pl.sem, pl.up(A))
            for b in range(4):
                A.eng.wait_ge(mem_tr.sem, mem_tr.at(A, b + 1))
                act.activation(memT_hi[:, 2 * b:2 * b + 2, :], bank[b][:].rearrange("p (k m) -> p k m", k=2), ACT.Copy).then_inc(mem_hi.sem, mem_hi.up(A))
            A.eng.wait_ge(par_col.sem, par_col.at(A, 1))
            pdest = [up[:, c, :] for c in range(4)] + [qk[:, c, :] for c in range(8)] + [iq[:, c, :] for c in range(4)] + [ikd[:]] \
                + [mq[:, c, :] for c in range(4)]
            for c in range(21):
                if c == 12:
                    A.eng.wait_ge(ring.done, ring.products(A, U2_V + 3))
                    for i in range(NT):
                        act.activation(vv[:, i, :], bank[i][:], ACT.Copy).then_inc(v2_ev.sem, v2_ev.up(A))
                A.eng.wait_ge(ring.done, ring.products(A, V_CH[c]))
                act.activation(pdest[c], bank[c % 4][:], ACT.Identity, bias=col(c)).then_inc(proj_ev.sem, proj_ev.up(A))
            for g4 in range(4):
                A.eng.wait_ge(pool_d.sem, pool_d.at(A, g4 + 1))
                act.activation(b_hi[:, g4, :], pd[:, g4, :], ACT.Copy).then_inc(pool_dh.sem, pool_dh.up(A))
            A.eng.wait_ge(ring.done, ring.products(A, U2_PW))
            for g4 in range(4):
                act.activation(b_hi[:, g4, :], bank[g4][:], ACT.Copy, scale=col(P_SC + g4)).then_inc(pool_hi.sem, pool_hi.up(A))
            for j in range(4):
                A.eng.wait_ge(ring.done, ring.products(A, U2_MK + j))
                act.activation(mk[:, j, :], bank[4 + j % 2][:, 0:NM], ACT.Copy).then_inc(mk_ev.sem, mk_ev.up(A))
            A.eng.wait_ge(ring.done, ring.products(A, U2_MV + 3))
            for m in range(2):
                act.activation(mvv[:, m, :], bank[6 + m][:], ACT.Copy).then_inc(mv_ev.sem, mv_ev.up(A))
            for n in range(16):
                A.eng.wait_ge(m_mx.sem, m_mx.at(A, n + 1))
                if n >= 2:
                    A.eng.wait_ge(m_t.sem, m_t.at(A, n - 1))
                act.activation(up[:, n % 2, 0:NM], bank[n % 2][:, 0:NM], ACT.Exp, bias=mmx2[:, n:n + 1], scale=MHD ** -0.5,
                                      accum_out=msm2[:, n:n + 1]).then_inc(m_p.sem, m_p.up(A))
            for i in range(NT):
                A.eng.wait_ge(m_ot.sem, m_ot.at(A, i + 1))
                act.activation(b_hi[:, 8:12, i * P:i * P + P], bank[6 + i % 2][:].rearrange("p (c n) -> p c n", c=4), ACT.Copy).then_inc(m_oh.sem, m_oh.up(A))
            load_gb(A, t["ln1_g_2"][bass.ds(l, 1), :], t["ln1_b_2"][bass.ds(l, 1), :])
            ni = na = 0
            for i in range(NT):
                nk = (i + 1) * P
                if i:
                    for hh in range(AH):
                        A.eng.wait_ge(ix_s.sem, ix_s.at(A, ni + 1))
                        if ni >= 2:
                            A.eng.wait_ge(ix_use.sem, ix_use.at(A, ni - 1))
                        ni += 1
                        act.activation(rel[hh % 2][:, 0:nk], bank[hh % 2][:, 0:nk], ACT.Relu, scale=HD ** -0.5).then_inc(ix_rel.sem, ix_rel.up(A))
                for n in range(AH + 1):
                    if n < AH:
                        A.eng.wait_ge(at_mx.sem, at_mx.at(A, na + n + 1))
                        act.activation(sc[n % 2][:, 0:nk], sc[n % 2][:, 0:nk], ACT.Exp, bias=amx[:, n:n + 1],
                                              accum_out=asum[:, n:n + 1]).then_inc(at_p.sem, at_p.up(A))
                    if n:
                        m = n - 1
                        A.eng.wait_ge(at_t.sem, at_t.at(A, na + m + 1))
                        if na + m >= 2:
                            A.eng.wait_ge(at_o.sem, at_o.at(A, na + m - 1))
                        act.activation(flat(apT[m % 2][:])[:, 0:nk], bank[4 + m % 2][:, 0:nk], ACT.Copy).then_inc(a_te.sem, a_te.up(A))
                na += AH
                A.eng.wait_ge(a_ot.sem, a_ot.at(A, i + 1))
                act.activation(b_hi[:, 4:8, i * P:i * P + P], bank[7][:].rearrange("p (c n) -> p c n", c=4), ACT.Copy).then_inc(a_oh.sem, a_oh.up(A))
            with act.Fori(0, 4) as i:
                A.loop("a_gates", i)
                for u6 in range(6):
                    n, dd = u6 % 3, u6 // 3
                    A.eng.wait_ge(ring.done, ring.products(A, U2_G + 2 * u6, turn=i, size=12))
                    A.eng.wait_ge(gt_use.sem, gt_use.at(A, i * 6 + (u6 - 1)))
                    bias = flat(pcol[:, B_GT + 8 * n + dd:].rearrange("p (n a) -> p n a", a=1)[:, bass.ds(i * 2, 1), :])
                    act.activation(sg[u6 % 2][:], bank[2 * (u6 % 2)][:], ACT.Sigmoid, bias=bias).then_inc(gt_sig.sem, gt_sig.up(A))
                A.loop_end(4)
            for k in range(KC):
                A.eng.wait_ge(gt_use.sem, gt_use.at(A, 24))
                act.activation(xT_hi[:, k, :], qk[:, k, :], ACT.Copy).then_inc(mg_hi.sem, mg_hi.up(A))
            norm_a(A, 0)
            load_gb(A, t["ln2_g_2"][bass.ds(l, 1), :], t["ln2_b_2"][bass.ds(l, 1), :])
            act.dma_start(rbias[:], over(t["router_bias_2"].rearrange("(o n) -> o n", o=1), [P, NE])).then_inc(rb_ld.sem, rb_ld.up(A))
            A.eng.wait_ge(ring.done, ring.products(A, U2_R))
            act.activation(flat(rsc[:]), bank[0][:, 0:NT * NE], ACT.Sigmoid).then_inc(rt_sc.sem, rt_sc.up(A))

            def evacuated(k):
                for y in range(2):
                    A.eng.wait_ge(x_tr.sem, x_tr.at(A, k + y))
                    act.activation(xbT[:, 4 * y:4 * y + 4, :], bank[y][:].rearrange("p (k t) -> p k t", k=4), ACT.Copy).then_inc(x_ev.sem, x_ev.up(A))

            evacuated(1)
            A.eng.wait_ge(x_ev.sem, x_ev.last(A))
            with act.Fori(0, NB // 2) as bb:
                A.loop("a_moe", bb)
                for q in range(2):
                    A.eng.wait_ge(wt_done.sem, wt_done.at(A, bb * 12 + (6 * q + 2)))
                    A.eng.wait_ge(h_tr.sem, h_tr.at(A, bb * 2 + q))
                    act.activation(hs[:], bank[2][:], ACT.Silu).then_inc(act_h.sem, act_h.up(A))
                    A.eng.wait_ge(wt_done.sem, wt_done.at(A, bb * 12 + (6 * q + 4)))
                    evacuated(bb * 4 + (2 * q + 3))
                    A.eng.wait_ge(h_tr.sem, h_tr.at(A, bb * 2 + (q + 1)))
                    act.activation(flat(hTm[:]), bank[4][:], ACT.Copy).then_inc(h_ev.sem, h_ev.up(A))
                A.loop_end(NB // 2)
            norm_a(A, 1)

        def vector2(V):
            v = V.eng
            V.eng.wait_ge(par_tr.sem, par_tr.at(V, 1))
            v.tensor_copy(pcol[:, 0:NROWS], bank[7][:, 0:NROWS]).then_inc(par_col.sem, par_col.up(V))
            V.eng.wait_ge(par_col.sem, par_col.last(V))
            for b in range(4):
                V.eng.wait_ge(mem_hi.sem, mem_hi.at(V, b + 1))
                v.tensor_tensor(memT_lo[:, 2 * b:2 * b + 2, :], bank[b][:].rearrange("p (k m) -> p k m", k=2),
                                       memT_hi[:, 2 * b:2 * b + 2, :].bitcast(F32), SUB).then_inc(mem_lo.sem, mem_lo.up(V))

            def rope(r):
                x = qk[:, r, :] if r < 8 else iq[:, r - 8, :] if r < 12 else ikd[:]
                V.eng.wait_ge(head_sw.sem, head_sw.at(V, r + 1))
                v.tensor_tensor(turned[:], bank[4 + r % 2][:], sinB[:], MUL).then_inc(v_step.sem, v_step.up(V))
                v.tensor_tensor(x, x, cosB[:], MUL).then_inc(v_step.sem, v_step.up(V))
                V.eng.wait_ge(v_step.sem, v_step.last(V))
                v.tensor_tensor(x, x, turned[:], ADD).then_inc(head_rope.sem, head_rope.up(V))
                V.eng.wait_ge(head_rope.sem, head_rope.last(V))

            def pool(g4):
                w, x = 2 << g4, up[:, g4, :]
                V.eng.wait_ge(proj_ev.sem, proj_ev.at(V, g4 + 1))
                cur, sh, k = x, 1, 0
                while sh < w:
                    nxt = work[k % 2]
                    v.tensor_copy(nxt[:, 0:sh], cur[:, 0:sh]).then_inc(v_step.sem, v_step.up(V))
                    v.tensor_tensor(nxt[:, sh:S], cur[:, sh:S], cur[:, 0:S - sh], ADD).then_inc(v_step.sem, v_step.up(V))
                    V.eng.wait_ge(v_step.sem, v_step.last(V))
                    cur, sh, k = nxt, 2 * sh, k + 1
                d = pd[:, g4, :]
                v.scalar_tensor_tensor(d[:, 16:S], cur[:, 16:S], 1.0 / w, x[:, 16:S], MUL, SUB).then_inc(v_step.sem, v_step.up(V))
                v.tensor_tensor(cur[:, 0:16], cur[:, 0:16], konst[:, K_CNT + 16 * g4:K_CNT + 16 * g4 + 16], MUL).then_inc(v_step.sem, v_step.up(V))
                V.eng.wait_ge(v_step.sem, v_step.last(V))
                v.tensor_tensor(d[:, 0:16], cur[:, 0:16], x[:, 0:16], SUB).then_inc(pool_d.sem, pool_d.up(V))
                V.eng.wait_ge(pool_d.sem, pool_d.last(V))

            for g4 in range(4):
                pool(g4)
            for r in range(8):
                rope(r)
            for r in range(8, 12):
                rope(r)
            V.eng.wait_ge(ring.done, ring.products(V, U2_IW))
            v.tensor_scalar(flat(iwc[:]), bank[6][:, 0:NT * AH], AH ** -0.5, None, MUL).then_inc(iw_ev.sem, iw_ev.up(V))
            V.eng.wait_ge(iw_ev.sem, iw_ev.last(V))
            rope(12)
            for g4 in range(4):
                V.eng.wait_ge(pool_dh.sem, pool_dh.at(V, g4 + 1))
                v.tensor_tensor(b_lo[:, g4, :], pd[:, g4, :], b_hi[:, g4, :].bitcast(F32), SUB).then_inc(pool_dl.sem, pool_dl.up(V))
            for g4 in range(4):
                V.eng.wait_ge(pool_hi.sem, pool_hi.at(V, g4 + 1))
                v.scalar_tensor_tensor(b_lo[:, g4, :], bank[g4][:], col(P_SC + g4), b_hi[:, g4, :].bitcast(F32), MUL, SUB).then_inc(pool_lo.sem, pool_lo.up(V))
            for n in range(19):
                if n < 16:
                    V.eng.wait_ge(m_s.sem, m_s.at(V, n + 1))
                    v.tensor_reduce(mmx2[:, n:n + 1], bank[n % 2][:, 0:NM], AX.X, MAX).then_inc(v_step.sem, v_step.up(V))
                    V.eng.wait_ge(v_step.sem, v_step.last(V))
                    v.tensor_scalar(mmx2[:, n:n + 1], mmx2[:, n:n + 1], -(MHD ** -0.5), None, MUL).then_inc(m_mx.sem, m_mx.up(V))
                    V.eng.wait_ge(m_mx.sem, m_mx.last(V))
                if 0 < n < 17:
                    m = n - 1
                    V.eng.wait_ge(m_t.sem, m_t.at(V, m + 1))
                    if m >= 2:
                        V.eng.wait_ge(m_o.sem, m_o.at(V, m - 1))
                    v.tensor_copy(up[:, 2 + m % 2, 0:NM], bank[2 + m % 2][:, 0:NM]).then_inc(m_te.sem, m_te.up(V))
                    V.eng.wait_ge(m_te.sem, m_te.last(V))
                if n >= 5 and (n - 5) % 4 == 0 and (n - 5) // 4 < 3 or n == 18:
                    i = (n - 5) // 4 if n < 18 else 3
                    V.eng.wait_ge(m_o.sem, m_o.at(V, 4 * i + 4))
                    v.reciprocal(mrc[:, 0:4], msm2[:, 4 * i:4 * i + 4]).then_inc(v_step.sem, v_step.up(V))
                    V.eng.wait_ge(v_step.sem, v_step.last(V))
                    v.tensor_tensor(om[:, i, :].rearrange("p (g n) -> p g n", g=4), bank[4 + i % 2][:].rearrange("p (g n) -> p g n", g=4),
                                           over(mrc[:, 0:4].unsqueeze(2), [P, 4, P]), MUL).then_inc(m_or.sem, m_or.up(V))
                    V.eng.wait_ge(m_or.sem, m_or.last(V))
            for i in range(NT):
                V.eng.wait_ge(m_oh.sem, m_oh.at(V, i + 1))
                v.tensor_tensor(b_lo[:, 8:12, i * P:i * P + P], bank[6 + i % 2][:].rearrange("p (c n) -> p c n", c=4),
                                       b_hi[:, 8:12, i * P:i * P + P].bitcast(F32), SUB).then_inc(m_ol.sem, m_ol.up(V))
            ni = na = 0
            for i in range(NT):
                nk, d0 = (i + 1) * P, i * P
                if i == 0:
                    v.memset(mask[:, 0:P], 0.0).then_inc(v_step.sem, v_step.up(V))
                    V.eng.wait_ge(v_step.sem, v_step.last(V))
                    v.memset(mask[0:64, 64:P], HIDE).then_inc(v_step.sem, v_step.up(V))
                    V.eng.wait_ge(v_step.sem, v_step.last(V))
                else:
                    for hh in range(AH):
                        V.eng.wait_ge(ix_rel.sem, ix_rel.at(V, ni + 1))
                        ni += 1
                        w = iwc[:, i, hh:hh + 1]
                        if hh == 0:
                            v.tensor_scalar(acc[:, 0:nk], rel[0][:, 0:nk], w, None, MUL).then_inc(ix_use.sem, ix_use.up(V))
                            V.eng.wait_ge(ix_use.sem, ix_use.last(V))
                        else:
                            v.scalar_tensor_tensor(acc[:, 0:nk], rel[hh % 2][:, 0:nk], w, acc[:, 0:nk], MUL, ADD).then_inc(ix_use.sem, ix_use.up(V))
                            V.eng.wait_ge(ix_use.sem, ix_use.last(V))
                    v.memset(acc[0:64, d0 + 64:d0 + P], OUT_OF).then_inc(v_step.sem, v_step.up(V))
                    for x in range(NSEL // 8):
                        V.eng.wait_ge(v_step.sem, V.alone(v_step.last(V)))
                        v.max(st8[:], acc[:, 0:nk]).then_inc(v_step.sem, v_step.up(V))
                        V.eng.wait_ge(v_step.sem, V.alone(v_step.last(V)))
                        v.match_replace(acc[:, 0:nk], st8[:], acc[:, 0:nk], TAKEN).then_inc(v_step.sem, v_step.up(V))
                    V.eng.wait_ge(v_step.sem, v_step.last(V))
                    v.tensor_scalar(mask[:, 0:nk], acc[:, 0:nk], -2e38, HIDE, ALU.is_gt, MUL).then_inc(v_step.sem, v_step.up(V))
                    V.eng.wait_ge(v_step.sem, v_step.last(V))
                for n in range(AH):
                    V.eng.wait_ge(at_s.sem, at_s.at(V, na + n + 1))
                    if na + n >= 2:
                        V.eng.wait_ge(at_t.sem, at_t.at(V, na + n - 1))
                    v.scalar_tensor_tensor(sc[n % 2][:, 0:nk], bank[2 + n % 2][:, 0:nk], HD ** -0.5, mask[:, 0:nk], MUL, ADD).then_inc(a_sc.sem, a_sc.up(V))
                    V.eng.wait_ge(a_sc.sem, a_sc.last(V))
                    v.tensor_reduce(amx[:, n:n + 1], sc[n % 2][:, 0:nk], AX.X, MAX).then_inc(v_step.sem, v_step.up(V))
                    V.eng.wait_ge(v_step.sem, v_step.last(V))
                    v.tensor_scalar(amx[:, n:n + 1], amx[:, n:n + 1], -1.0, None, MUL).then_inc(at_mx.sem, at_mx.up(V))
                    V.eng.wait_ge(at_mx.sem, at_mx.last(V))
                na += AH
                V.eng.wait_ge(at_o.sem, at_o.at(V, na))
                v.reciprocal(ars[:], asum[:]).then_inc(v_step.sem, v_step.up(V))
                V.eng.wait_ge(v_step.sem, v_step.last(V))
                v.tensor_tensor(otok[:].rearrange("p (g n) -> p g n", g=AH), bank[6][:].rearrange("p (g n) -> p g n", g=AH),
                                       over(ars[:].unsqueeze(2), [P, AH, HD]), MUL).then_inc(a_or.sem, a_or.up(V))
                V.eng.wait_ge(a_or.sem, a_or.last(V))
                V.eng.wait_ge(a_oh.sem, a_oh.at(V, i + 1))
                v.tensor_tensor(b_lo[:, 4:8, d0:d0 + P], bank[7][:].rearrange("p (c n) -> p c n", c=4),
                                       b_hi[:, 4:8, d0:d0 + P].bitcast(F32), SUB).then_inc(a_ol.sem, a_ol.up(V))
            V.eng.wait_ge(a_ol.sem, V.alone(a_ol.last(V)))
            with v.Fori(0, 4) as i:
                V.loop("v_gates", i)
                for u6 in range(6):
                    n, dd = u6 % 3, u6 // 3
                    m = qk[:, bass.ds(i * 2 + dd, 1), :]
                    V.eng.wait_ge(gt_sig.sem, gt_sig.at(V, i * 6 + (u6 + 1)))
                    V.eng.wait_ge(ring.done, ring.products(V, U2_G + 2 * u6 + 1, turn=i, size=12))
                    br = bank[2 * (u6 % 2) + 1][:].unsqueeze(1)
                    if n == 0:
                        v.tensor_tensor(m, sg[u6 % 2][:].unsqueeze(1), br, MUL).then_inc(gt_use.sem, gt_use.up(V))
                        V.eng.wait_ge(gt_use.sem, gt_use.last(V))
                    else:
                        v.tensor_tensor(gt[:].unsqueeze(1), sg[u6 % 2][:].unsqueeze(1), br, MUL).then_inc(v_step.sem, v_step.up(V))
                        V.eng.wait_ge(v_step.sem, v_step.last(V))
                        v.tensor_tensor(m, m, gt[:].unsqueeze(1), ADD).then_inc(gt_use.sem, gt_use.up(V))
                        V.eng.wait_ge(gt_use.sem, gt_use.last(V))
                V.loop_end(4)
            for k in range(KC):
                V.eng.wait_ge(mg_hi.sem, mg_hi.at(V, k + 1))
                v.tensor_tensor(xT_lo[:, k, :], qk[:, k, :], xT_hi[:, k, :].bitcast(F32), SUB).then_inc(mg_lo.sem, mg_lo.up(V))
            norm_v(V, 0, U2_OUT + KC - 1)
            V.eng.wait_ge(rt_sc.sem, rt_sc.at(V, 1))
            V.eng.wait_ge(rb_ld.sem, rb_ld.at(V, 1))
            v.memset(rgs[:], HIDE).then_inc(v_step.sem, v_step.up(V))
            v.tensor_tensor(rbi[:], rsc[:], over(rbias[:].unsqueeze(1), [P, NT, NE]), ADD).then_inc(v_step.sem, v_step.up(V))
            V.eng.wait_ge(v_step.sem, v_step.last(V))
            b4 = flat(rbi[:]).rearrange("p (g x) -> p g x", x=4)
            tm = rtm[:].rearrange("p i g x -> p (i g) x")
            e = lambda k: b4[:, :, k:k + 1]
            f = lambda k: tm[:, :, k:k + 1]
            for o, a, b, op in ((0, e(0), e(1), MAX), (1, e(0), e(1), MIN), (2, e(2), e(3), MAX), (3, e(2), e(3), MIN)):
                v.tensor_tensor(f(o), a, b, op).then_inc(v_step.sem, v_step.up(V))
            V.eng.wait_ge(v_step.sem, v_step.last(V))
            v.tensor_tensor(f(4), f(0), f(2), MAX).then_inc(v_step.sem, v_step.up(V))
            v.tensor_tensor(f(5), f(0), f(2), MIN).then_inc(v_step.sem, v_step.up(V))
            v.tensor_tensor(f(6), f(1), f(3), MAX).then_inc(v_step.sem, v_step.up(V))
            V.eng.wait_ge(v_step.sem, v_step.last(V))
            v.tensor_tensor(f(5), f(5), f(6), MAX).then_inc(v_step.sem, v_step.up(V))
            V.eng.wait_ge(v_step.sem, v_step.last(V))
            v.tensor_tensor(rgs[:, :, 0:4], rtm[:, :, :, 4], rtm[:, :, :, 5], ADD).then_inc(v_step.sem, v_step.up(V))

            def two_best(src):
                V.eng.wait_ge(v_step.sem, V.alone(v_step.last(V)))
                v.max(rmx[:], src).then_inc(v_step.sem, v_step.up(V))
                V.eng.wait_ge(v_step.sem, V.alone(v_step.last(V)))
                v.max_index(rix[:], rmx[:], src).then_inc(v_step.sem, v_step.up(V))
                V.eng.wait_ge(v_step.sem, v_step.last(V))

            for i in range(NT):
                two_best(rgs[:, i, :])
                v.tensor_copy(gw[:, i, 3:4], rix[:, 0:1]).then_inc(v_step.sem, v_step.up(V))
                V.eng.wait_ge(v_step.sem, v_step.last(V))
                v.tensor_scalar(rtmp[:, i, :], konst[:, K_G16:K_G16 + NE], gw[:, i, 3:4], None, ALU.is_equal).then_inc(v_step.sem, v_step.up(V))
                V.eng.wait_ge(v_step.sem, v_step.last(V))
                v.tensor_tensor(rbi[:, i, :], rbi[:, i, :], rtmp[:, i, :], MUL).then_inc(v_step.sem, v_step.up(V))
                V.eng.wait_ge(v_step.sem, v_step.last(V))
                v.tensor_scalar(rtmp[:, i, :], rtmp[:, i, :], 1.0, -HIDE, SUB, MUL).then_inc(v_step.sem, v_step.up(V))
                V.eng.wait_ge(v_step.sem, v_step.last(V))
                v.tensor_tensor(rbi[:, i, :], rbi[:, i, :], rtmp[:, i, :], ADD).then_inc(v_step.sem, v_step.up(V))
                two_best(rbi[:, i, :])
                v.tensor_copy(gw[:, i, 2:4], rix[:, 0:2]).then_inc(v_step.sem, v_step.up(V))
                V.eng.wait_ge(v_step.sem, v_step.last(V))
                for a in range(2):
                    v.tensor_scalar(oh[:, a, i, :], konst[:, K_E16:K_E16 + NE], gw[:, i, 2 + a:3 + a], None, ALU.is_equal).then_inc(v_step.sem, v_step.up(V))
            V.eng.wait_ge(v_step.sem, v_step.last(V))
            v.tensor_tensor(oh[:, 2, :, :], oh[:, 0, :, :], oh[:, 1, :, :], ADD).then_inc(rt_oh.sem, rt_oh.up(V))
            V.eng.wait_ge(rt_oh.sem, rt_oh.last(V))
            for a in range(2):
                v.tensor_tensor(rtmp[:], rsc[:], oh[:, a, :, :], MUL).then_inc(v_step.sem, v_step.up(V))
                V.eng.wait_ge(v_step.sem, v_step.last(V))
                v.tensor_reduce(gw[:, :, a:a + 1], rtmp[:], AX.X, ADD).then_inc(v_step.sem, v_step.up(V))
                V.eng.wait_ge(v_step.sem, v_step.last(V))
            v.tensor_tensor(gw[:, :, 2:3], gw[:, :, 0:1], gw[:, :, 1:2], ADD).then_inc(v_step.sem, v_step.up(V))
            V.eng.wait_ge(v_step.sem, v_step.last(V))
            v.reciprocal(gw[:, :, 2:3], gw[:, :, 2:3]).then_inc(v_step.sem, v_step.up(V))
            V.eng.wait_ge(v_step.sem, v_step.last(V))
            v.tensor_tensor(gw[:, :, 0:2], gw[:, :, 0:2], over(gw[:, :, 2:3], [P, NT, 2]), MUL).then_inc(v_step.sem, v_step.up(V))
            V.eng.wait_ge(v_step.sem, v_step.last(V))
            V.eng.wait_ge(rt_rank.sem, rt_rank.at(V, 1))
            v.tensor_copy(cnt[:], bank[1][:, NT * NE:NT * NE + NE]).then_inc(v_step.sem, v_step.up(V))
            V.eng.wait_ge(v_step.sem, v_step.last(V))
            v.tensor_scalar(nblk[:], cnt[:], 0.5, None, ALU.is_gt).then_inc(v_step.sem, v_step.up(V))
            V.eng.wait_ge(v_step.sem, v_step.last(V))
            for k in range(1, NT):
                v.scalar_tensor_tensor(nblk[:], cnt[:], P * k + 0.5, nblk[:], ALU.is_gt, ADD).then_inc(v_step.sem, v_step.up(V))
                V.eng.wait_ge(v_step.sem, v_step.last(V))
            v.tensor_tensor_scan(pend[:], ones[:, 0:NE], nblk[:], 0.0, MUL, ADD).then_inc(v_step.sem, v_step.up(V))
            V.eng.wait_ge(v_step.sem, v_step.last(V))
            v.tensor_tensor(bst[:], pend[:], nblk[:], SUB).then_inc(v_step.sem, v_step.up(V))
            V.eng.wait_ge(v_step.sem, v_step.last(V))
            v.tensor_tensor(bcmp[:], over(pend[:].unsqueeze(1), [P, NB + 1, NE]),
                                   over(konst[:, K_BNO:K_BNO + NB + 1].unsqueeze(2), [P, NB + 1, NE]), ALU.is_le).then_inc(v_step.sem, v_step.up(V))
            V.eng.wait_ge(v_step.sem, v_step.last(V))
            v.tensor_reduce(bef[:], bcmp[:], AX.X, ADD).then_inc(v_step.sem, v_step.up(V))
            V.eng.wait_ge(v_step.sem, v_step.last(V))
            v.tensor_scalar(bei[:], bef[:], NE - 1.0, None, MIN).then_inc(be_ok.sem, be_ok.up(V))
            V.eng.wait_ge(be_ok.sem, be_ok.last(V))
            v.tensor_scalar(bst[:], bst[:], float(P), -1.0, MUL, ADD).then_inc(v_step.sem, v_step.up(V))
            V.eng.wait_ge(v_step.sem, v_step.last(V))
            v.tensor_tensor(rtmp[:], bank[1][:, 0:NT * NE].rearrange("p (i e) -> p i e", i=NT), over(bst[:].unsqueeze(1), [P, NT, NE]), ADD).then_inc(v_step.sem, v_step.up(V))
            V.eng.wait_ge(v_step.sem, v_step.last(V))
            for a in range(2):
                v.tensor_tensor(rbi[:], rtmp[:], oh[:, a, :, :], MUL).then_inc(v_step.sem, v_step.up(V))
                V.eng.wait_ge(v_step.sem, v_step.last(V))
                v.tensor_reduce(dest[:, a, :], rbi[:], AX.X, ADD).then_inc(v_step.sem, v_step.up(V))
                V.eng.wait_ge(v_step.sem, v_step.last(V))
            v.tensor_copy(desti[:], dest[:]).then_inc(rt_dest.sem, rt_dest.up(V))
            V.eng.wait_ge(rt_dest.sem, V.alone(rt_dest.last(V)))
            with v.Fori(0, NB // 2) as bb:
                V.loop("v_moe", bb)
                for q in range(2):
                    V.eng.wait_ge(act_h.sem, act_h.at(V, bb * 2 + (q + 1)))
                    V.eng.wait_ge(wt_done.sem, wt_done.at(V, bb * 12 + (6 * q + 4)))
                    v.tensor_tensor(hs[:], hs[:], bank[3][:], MUL).then_inc(h_val.sem, h_val.up(V))
                    V.eng.wait_ge(h_val.sem, h_val.last(V))
                    V.eng.wait_ge(y_free.sem, y_free.at(V, bb * 2 + (q - 1)))
                    V.eng.wait_ge(wt_done.sem, wt_done.at(V, bb * 12 + (6 * q + 6)))
                    for x in range(2):
                        v.tensor_copy(yb[q][:, x * S:x * S + S], bank[5 + x][:]).then_inc(y_ev.sem, y_ev.up(V))
                V.loop_end(NB // 2)
            for i in range(NT):
                a, b = yg[(2 * i) % 4], yg[(2 * i + 1) % 4]
                V.eng.wait_ge(ygl[(2 * i) % 4].sem, ygl[(2 * i) % 4].at(V, i // 2 + 1))
                V.eng.wait_ge(ygl[(2 * i + 1) % 4].sem, ygl[(2 * i + 1) % 4].at(V, i // 2 + 1))
                v.tensor_scalar(a[:], a[:], gw[:, i, 0:1], None, MUL).then_inc(v_step.sem, v_step.up(V))
                V.eng.wait_ge(v_step.sem, v_step.last(V))
                v.scalar_tensor_tensor(a[:], b[:], gw[:, i, 1:2], a[:], MUL, ADD).then_inc(yg_use.sem, yg_use.up(V))
                V.eng.wait_ge(yg_use.sem, yg_use.last(V))
                v.scalar_tensor_tensor(h[:, i, :], h[:, i, :], ALPHA, a[:], MUL, ADD).then_inc(yg_use.sem, yg_use.up(V))
                V.eng.wait_ge(yg_use.sem, yg_use.last(V))
            norm_v(V, 1, None)

        def finish(E):
            for n in range(NT):
                E.eng.wait_ge(norm_z.sem, norm_z.at(E, NT + n + 1))
                E.eng.dma_start(out[0, n * P:n * P + P, :], h[:, n, :]).then_inc(stored, 16)
            E.eng.wait_ge(stored, 16 * NT)
            E.eng.wait_ge(h_st.sem, h_st.at(E, NT))

        TWO_PI = 6.283185307179586
        C1, C2, C3 = 6.28125, 0.0019350051879882812, 3.019916050501e-07
        MAGIC = 12582912.0
        HALF_PI, PI_BELOW = TWO_PI / 4, 3.1415925
        x_rows = t["x"].rearrange("o (i p) d -> (o p) i d", p=P)

        def loads0(E):
            sp = E.eng
            sp.dma_start(konst[:], t["konst"]).then_inc(ld.sem, ld.up(E))
            for k, name in enumerate(("positions", "positions_2")):
                sp.dma_start(proj[:, k, :].bitcast(I32), over(t[name], [P, S])).then_inc(ld.sem, ld.up(E))
            for i in range(NT):
                sp.dma_start(h[:, i, :], x_rows[:, i, :]).then_inc(ld.sem, ld.up(E))

        def gpsimd0(G):
            g = G.eng
            g.nop().then_inc(began, 1)
            g.memset(small[:, 0:1], EPS).then_inc(set_up.sem, set_up.up(G))
            g.memset(small[:, 1:2], 1.0).then_inc(set_up.sem, set_up.up(G))
            g.memset(mean_of[:], 1.0 / W).then_inc(set_up.sem, set_up.up(G))
            g.memset(ones[:], 1.0).then_inc(set_up.sem, set_up.up(G))
            g.memset(gaup[:], 0.0).then_inc(set_up.sem, set_up.up(G))
            ring.prime(g, None)
            for _ in range(2):
                g.nop().then_inc(y_free.sem, y_free.up(G))

        def tensor0(T):
            ring.prime(None, T.eng)
            for free in [wt_done] * 6 + [x_tr, h_tr]:
                T.eng.nop().then_inc(free.sem, free.up(T))
            T.eng.wait_ge(ld.sem, ld.at(T, 7))
            T.eng.wait_ge(set_up.sem, set_up.at(T, 5))
            norm_pe(T, 0)

        def scalar0(A):
            load_gb(A, t["ln_in_g"].rearrange("(o n) -> o n", o=1), t["ln_in_b"].rearrange("(o n) -> o n", o=1))
            A.eng.wait_ge(set_up.sem, set_up.at(A, 5))
            norm_a(A, 0)
            for n, tab in enumerate((sinA, cosA, sinB, cosB)):
                A.eng.wait_ge(tab_arg.sem, tab_arg.at(A, n + 1))
                A.eng.activation(tab[:], tab[:], ACT.Sin).then_inc(tab_sin.sem, tab_sin.up(A))
                A.eng.wait_ge(tab_sin.sem, tab_sin.last(A))

        def vector0(V):
            v = V.eng
            for free in (y_ev, gt_use, gt_use):
                v.nop().then_inc(free.sem, free.up(V))
            V.eng.wait_ge(ld.sem, ld.at(V, 7))
            V.eng.wait_ge(set_up.sem, set_up.at(V, 5))
            norm_v(V, 0, None)
            for k, (sin, cos) in enumerate(((sinA, cosA), (sinB, cosB))):
                ang, cyc, posi = proj[:, 4, :], proj[:, 5, :], proj[:, k, :].bitcast(I32)
                v.tensor_copy(ang, posi).then_inc(v_step.sem, v_step.up(V))
                V.eng.wait_ge(v_step.sem, v_step.last(V))
                v.tensor_scalar(ang, ang, konst[:, K_FREQ + 2 * k:K_FREQ + 2 * k + 1], None, MUL).then_inc(v_step.sem, v_step.up(V))
                V.eng.wait_ge(v_step.sem, v_step.last(V))
                for tab, quarter in ((sin, 0.0), (cos, 0.25)):
                    v.tensor_scalar(cyc, ang, 1.0 / TWO_PI, quarter, MUL, ADD).then_inc(v_step.sem, v_step.up(V))
                    V.eng.wait_ge(v_step.sem, v_step.last(V))
                    v.tensor_scalar(cyc, cyc, MAGIC, MAGIC, ADD, SUB).then_inc(v_step.sem, v_step.up(V))
                    V.eng.wait_ge(v_step.sem, v_step.last(V))
                    v.scalar_tensor_tensor(tab[:], cyc, -C1, ang, MUL, ADD).then_inc(v_step.sem, v_step.up(V))
                    V.eng.wait_ge(v_step.sem, v_step.last(V))
                    v.scalar_tensor_tensor(tab[:], cyc, -C2, tab[:], MUL, ADD).then_inc(v_step.sem, v_step.up(V))
                    V.eng.wait_ge(v_step.sem, v_step.last(V))
                    v.scalar_tensor_tensor(tab[:], cyc, -C3, tab[:], MUL, ADD).then_inc(v_step.sem, v_step.up(V))
                    V.eng.wait_ge(v_step.sem, v_step.last(V))
                    v.tensor_scalar(tab[:], tab[:], HALF_PI if quarter else 0.0, PI_BELOW, ADD, MIN).then_inc(v_step.sem, v_step.up(V))
                    V.eng.wait_ge(v_step.sem, v_step.last(V))
                    v.tensor_scalar(tab[:], tab[:], -PI_BELOW, None, MAX).then_inc(tab_arg.sem, tab_arg.up(V))
                    V.eng.wait_ge(tab_arg.sem, tab_arg.last(V))
            for k, sin in enumerate((sinA, sinB)):
                V.eng.wait_ge(tab_sin.sem, tab_sin.at(V, 2 * k + 1))
                v.tensor_scalar(sin[:], sin[:], konst[:, K_FREQ + 2 * k + 1:K_FREQ + 2 * k + 2], None, MUL).then_inc(v_step.sem, v_step.up(V))
                V.eng.wait_ge(v_step.sem, v_step.last(V))
            V.eng.wait_ge(tab_sin.sem, tab_sin.at(V, 4))

        stages = {
            "sync": (loads0, loads1, loads2), "gpsimd": (gpsimd0, splits1, splits2),
            "tensor": (tensor0, tensor1, tensor2), "scalar": (scalar0, scalar1, scalar2),
            "vector": (vector0, vector1, vector2),
        }

        def program(E, name):
            before, block1, block2 = stages[name]
            before(E)
            E.leave()
            for number, body in ((1, block1), (2, block2)):
                if body is None:
                    continue
                with E.eng.Fori(0, L) as l:
                    E.enter(number, l)
                    body(E)
                    E.leave()
            E.enter(2, L - 1)

        @block.sync
        def _(sp):
            E = Lane(sp, began)
            program(E, "sync")
            finish(E)

        @block.gpsimd
        def _(pool):
            program(Lane(pool, began), "gpsimd")

        @block.tensor
        def _(pe):
            program(Lane(pe, began), "tensor")

        @block.scalar
        def _(act):
            program(Lane(act, began), "scalar")

        @block.vector
        def _(dve):
            program(Lane(dve, began), "vector")


INPUTS = [
    "x", "positions", "ln_in_g", "ln_in_b", "w_in", "w_sc_conv", "w_gla_a_up", "b_gla_a", "g_gla_head", "g_mla_q",
    "w_mla_uq", "g_mla_kv", "w_mla_ukv", "w_cfm_dw", "g_cfm_ln", "b_cfm_ln", "g_branch", "w_out", "ln1_g", "ln1_b",
    "w_ffn_up", "w_ffn_dw", "w_ffn_down", "ln2_g", "ln2_b", "mem_2", "positions_2", "w_in_2", "b_in_2", "pool_w_2",
    "pool_scale_2", "w_mem_kv_2", "w_br_2", "w_out_2", "ln1_g_2", "ln1_b_2", "w_router_2", "router_bias_2",
    "w1_2", "w3_2", "w2_2", "ln2_g_2", "ln2_b_2",
]


def kernel(**inputs):
    import numpy as np
    import concourse.bacc as bacc
    from concourse.bass_utils import run_bass_kernel_spmd

    nc = bacc.Bacc("TRN2", target_bir_lowering=False, num_devices=1)
    arrays, t = {}, {}
    for name in INPUTS + ["konst"]:
        a = shape_constants() if name == "konst" else np.ascontiguousarray(inputs[name])
        arrays[f"in_{name}"] = a
        t[name] = nc.dram_tensor(f"in_{name}", a.shape, mybir.dt.from_np(a.dtype), kind="ExternalInput").ap()
    out = nc.dram_tensor("out_h", (1, S, D), F32, kind="ExternalOutput").ap()
    build(nc, t, out)
    r = run_bass_kernel_spmd(nc, [arrays], core_ids=[0])
    return r.results[0]["out_h"]
```

```python
from contextlib import ExitStack

import concourse.bass as bass
from concourse import mybir

P = 128
S = 512
NT = S // P
D = 1024
KC = D // P
L = 2
F32 = mybir.dt.float32
F32R = mybir.dt.float32r
I32 = mybir.dt.int32
U32 = mybir.dt.uint32
ALU = mybir.AluOpType
ACT = mybir.ActivationFunctionType
AX = mybir.AxisListType
ADD, SUB, MUL, MAX, MIN = ALU.add, ALU.subtract, ALU.mult, ALU.max, ALU.min
EPS = 1e-5
ALPHA = (2.0 * L) ** 0.25

C_SCB, C_SCC, C_SCH, C_GQ, C_GK, C_GV, C_GA, C_CQ, C_CKV, C_KR, C_A, C_GATE = (
    0, 256, 512, 768, 896, 1024, 1536, 1568, 1824, 1952, 1984, 2240)
W = 256
D_FF = 2816
FC = D_FF // P
TAPS = 31
HALO = TAPS // 2
GH, GK, GVD, TAU = 4, 32, 64, 16.0
MH, NOPE, ROPE, MD = 4, 64, 32, 96
R0 = NOPE
MLA_SCALE = MD ** -0.5

NE, NG = 16, 4
NB = 2 * S // P + NE
RAW, SPLIT = 4, 2

K_ID, K_SWA, K_SWB, K_TRF, K_TRB, K_HEAD, K_BLK, K_FREQ, K_CNT, K_REV, K_TOK, K_BNO, K_END = (
    0, 128, 256, 384, 512, 640, 644, 900, 904, 968, 984, 1000, 1026)
N_KONST = 1026 + P


def shape_constants():
    import numpy as np

    c = np.zeros((P, N_KONST), np.float32)
    i = np.arange(P)
    c[i, K_ID + i] = 1.0
    for r in range(ROPE):
        c[R0 + (r ^ 16), K_SWA + R0 + r] = 1.0
    c[i ^ 32, K_SWB + i] = 1.0
    s, t = i[:, None], i[None, :]
    c[:, K_TRF:K_TRF + P] = s <= t
    c[:, K_TRB:K_TRB + P] = s > t
    c[i, K_HEAD + i // GK] = 1.0
    c[:, K_BLK:K_BLK + W] = (s // GK) == (np.arange(W)[None, :] // GVD)
    c[:, K_FREQ] = np.float32(10000.0) ** (-(i % 16).astype(np.float32) / np.float32(16))
    c[:, K_FREQ + 1] = np.where(i % 32 < 16, -1.0, 1.0)
    c[:, K_FREQ + 2] = np.float32(10000.0) ** (-(i % 32).astype(np.float32) / np.float32(32))
    c[:, K_FREQ + 3] = np.where(i % 64 < 32, -1.0, 1.0)
    for g, w in enumerate((2, 4, 8, 16)):
        c[:, K_CNT + 16 * g:K_CNT + 16 * g + 16] = 1.0 / np.minimum(np.arange(16) + 1, w).astype(np.float32)
    c[:, K_REV:K_REV + 16] = 16 - np.arange(16)
    for a in range(4):
        c[:, K_TOK + a] = i + P * a
    c[:, K_BNO:K_END] = np.arange(K_END - K_BNO)
    c[:, K_END:] = np.arange(P)
    return c


COUNTS = {
    "ld_start": (7, 0, 0),
    "h_st": (0, 0, 4),
    "wt_ld0": (0, 0, 24),
    "wt_ld1": (0, 0, 24),
    "wt_ld2": (0, 0, 24),
    "wt_ld3": (0, 0, 24),
    "wt_ld4": (0, 0, 24),
    "wt_ld5": (0, 0, 24),
    "set_up": (7, 0, 0),
    "y_free": (2, 0, 24),
    "y_zero": (0, 12, 0),
    "sid_ok": (0, 0, 25),
    "xb_ld0": (0, 0, 13),
    "xb_ld1": (0, 0, 12),
    "y_st": (0, 0, 24),
    "yg_ld0": (0, 0, 2),
    "yg_ld1": (0, 0, 2),
    "yg_ld2": (0, 0, 2),
    "yg_ld3": (0, 0, 2),
    "wt_done": (6, 0, 144),
    "x_tr": (1, 0, 50),
    "h_tr": (1, 0, 24),
    "norm_tr": (8, 16, 16),
    "par_tr": (0, 1, 1),
    "ga_mm": (0, 2, 0),
    "kd_tr": (0, 2, 0),
    "gla_scores": (0, 8, 0),
    "gla_kv": (0, 6, 0),
    "gla_out": (0, 8, 0),
    "rms_mm": (0, 5, 0),
    "head_sw": (0, 5, 13),
    "at_scores": (0, 16, 32),
    "cfm_mm": (0, 1, 0),
    "at_tr": (0, 16, 32),
    "at_out": (0, 16, 32),
    "tok_tr": (0, 4, 0),
    "tile_sum": (0, 6, 3),
    "mem_tr": (0, 0, 4),
    "iw_tr": (0, 0, 1),
    "ix_s": (0, 0, 24),
    "m_s": (0, 0, 16),
    "m_t": (0, 0, 16),
    "m_o": (0, 0, 16),
    "a_ot": (0, 0, 4),
    "m_ot": (0, 0, 4),
    "rt_tr": (0, 0, 1),
    "rt_rank": (0, 0, 1),
    "slot_mm": (0, 0, 1),
    "gb_ld": (2, 4, 4),
    "norm_sd": (4, 8, 8),
    "norm_hi": (8, 16, 16),
    "tab_sin": (4, 0, 0),
    "par_ld": (0, 13, 11),
    "proj_ev": (0, 16, 21),
    "la_part": (0, 4, 0),
    "a_step": (0, 11, 0),
    "gv_ev": (0, 8, 0),
    "gexp": (0, 5, 0),
    "kd_ev": (0, 2, 0),
    "rms_sq": (0, 9, 0),
    "rms_rs": (0, 5, 0),
    "c_h": (0, 3, 0),
    "head_ev": (0, 4, 0),
    "k_cp": (0, 7, 0),
    "at_p": (0, 16, 32),
    "y_hi": (0, 4, 0),
    "tok_sd": (0, 3, 0),
    "tok_hi": (0, 4, 0),
    "up_ev": (0, 44, 0),
    "up_silu": (0, 22, 0),
    "up_hi": (0, 22, 0),
    "mem_hi": (0, 0, 4),
    "v2_ev": (0, 0, 4),
    "iw_fm": (0, 0, 1),
    "pool_dh": (0, 0, 4),
    "pool_hi": (0, 0, 4),
    "mk_ev": (0, 0, 4),
    "ix_rel": (0, 0, 24),
    "mv_ev": (0, 0, 2),
    "m_p": (0, 0, 16),
    "m_te": (0, 0, 16),
    "a_te": (0, 0, 32),
    "a_oh": (0, 0, 4),
    "m_oh": (0, 0, 4),
    "gt_sig": (0, 0, 24),
    "mg_hi": (0, 0, 8),
    "rb_ld": (0, 0, 2),
    "rt_sc": (0, 0, 1),
    "x_ev": (0, 0, 50),
    "act_h": (0, 0, 24),
    "h_ev": (0, 0, 24),
    "y_ev": (1, 0, 48),
    "gt_use": (2, 0, 24),
    "v_step": (46, 284, 343),
    "norm_var": (4, 8, 8),
    "norm_z": (4, 8, 8),
    "norm_lo": (8, 16, 16),
    "tab_arg": (4, 0, 0),
    "par_col": (0, 1, 1),
    "la_x": (0, 1, 0),
    "kd_val": (0, 2, 0),
    "gla_state": (0, 8, 0),
    "gla_q": (0, 8, 0),
    "gla_masked": (0, 8, 0),
    "gla_out_read": (0, 8, 0),
    "c_val": (0, 3, 0),
    "c_l": (0, 3, 0),
    "rms_in": (0, 2, 0),
    "head_rope": (0, 5, 13),
    "v_ev": (0, 1, 0),
    "at_max": (0, 16, 32),
    "at_pT": (0, 16, 0),
    "y_val": (0, 4, 0),
    "y_lo": (0, 4, 0),
    "cfm_ln": (0, 2, 0),
    "tok_ms": (0, 3, 0),
    "tok_y": (0, 2, 0),
    "tok_lo": (0, 4, 0),
    "up_conv": (0, 44, 0),
    "up_val": (0, 22, 0),
    "up_lo": (0, 22, 0),
    "mem_lo": (0, 0, 4),
    "pool_d": (0, 0, 4),
    "iw_ev": (0, 0, 1),
    "pool_dl": (0, 0, 4),
    "pool_lo": (0, 0, 4),
    "ix_use": (0, 0, 24),
    "m_mx": (0, 0, 16),
    "m_or": (0, 0, 4),
    "a_sc": (0, 0, 32),
    "a_or": (0, 0, 4),
    "a_ol": (0, 0, 4),
    "m_ol": (0, 0, 4),
    "mg_lo": (0, 0, 8),
    "rt_oh": (0, 0, 1),
    "be_ok": (0, 0, 1),
    "slot_oh": (0, 0, 1),
    "rt_dest": (0, 0, 1),
    "h_val": (0, 0, 24),
    "yg_use": (0, 0, 8),
}
TURNS = {
    "sp_moe": {"wt_ld0": 2, "wt_ld1": 2, "wt_ld2": 2, "wt_ld3": 2, "wt_ld4": 2, "wt_ld5": 2},
    "g_moe": {"sid_ok": 2, "xb_ld0": 1, "xb_ld1": 1, "y_st": 2, "y_free": 2},
    "t_moe": {"x_tr": 4, "wt_done": 12, "h_tr": 2},
    "a_up": {"up_ev": 4, "up_silu": 2, "up_hi": 2},
    "a_gates": {"gt_sig": 6},
    "a_moe": {"x_ev": 4, "act_h": 2, "h_ev": 2},
    "v_up": {"v_step": 8, "up_conv": 4, "up_val": 2, "up_lo": 2},
    "v_gates": {"v_step": 4, "gt_use": 6},
    "v_moe": {"h_val": 2, "y_ev": 4},
}
PACED = [name for name in TURNS if name.endswith("_moe")]
TURN_MAX = (2 * S // P + 16) // 2


class Signal:

    def __init__(self, name, sem, step=1):
        self.name, self.sem, self.step = name, sem, step
        self.counts = COUNTS.get(name, (0, 0, 0))
        self.paced = sum(TURNS[n].get(name, 0) for n in PACED)
        self.first = (0, self.counts[0], self.counts[0] + L * self.counts[1])

    def at(self, lane, k):
        layer_is = self.counts[lane.block]
        if lane.block == 2 and self.paced:
            layer_is -= self.paced * TURN_MAX
            k = lane.past * self.paced + k
        return lane.layer * (layer_is * self.step) + (self.first[lane.block] + k) * self.step

    def up(self, lane):
        lane.raised[self] = lane.raised.get(self, 0) + 1
        return self.step

    def last(self, lane, back=0):
        k = lane.raised[self] - back
        if lane.turn is not None:
            k = lane.turn[1] * TURNS.get(lane.turn[0], {}).get(self.name, 0) + k
        return self.at(lane, k)


class Lane:

    def __init__(self, eng, began):
        self.eng, self.began = eng, began
        self.enter(0, 0)

    def enter(self, block, layer):
        self.block, self.layer, self.raised, self.turn = block, layer, {}, None

    def leave(self):
        for s, n in self.raised.items():
            if n != s.counts[self.block]:
                raise ValueError(s.name, self.block, n)

    def loop(self, name, reg):
        self.turn, self.begun = (name, reg), dict(self.raised)

    def loop_end(self, count):
        name, _ = self.turn
        for s in list(self.raised):
            got = self.raised[s] - self.begun.get(s, 0)
            if got != TURNS.get(name, {}).get(s.name, 0):
                raise ValueError(s.name, name, got)
            self.raised[s] = self.begun.get(s, 0) + got * count
        self.turn = None

    def pace(self, tile):
        self.past = self.eng.value_load(tile[0:1, 0:1], min_val=0, max_val=TURN_MAX)
        self.turns = self.eng.value_load(tile[0:1, 1:2], min_val=0, max_val=TURN_MAX)

    def alone(self, value):
        value = self.eng.to_reg(value) if self.block else value
        self.eng.wait_ge(self.began, 1)
        return value


class Stream:

    PER = (0, 96, 92)

    def __init__(self, sb, sem):
        self.raw = [sb(f"unit_raw{i}", [P, 1024], F32) for i in range(RAW)]
        self.hi = [sb(f"unit_hi{i}", [P, 1024], F32R) for i in range(SPLIT)]
        self.lo = [sb(f"unit_lo{i}", [P, 1024], F32R) for i in range(SPLIT)]
        self.loaded = [sem(f"unit_loaded{i}") for i in range(RAW)]
        self.hi_made = sem("unit_hi_made")
        self.split = sem("unit_split")
        self.done = sem("unit_done")
        self.base = (0, 0, L * self.PER[1])

    def number(self, lane, j, turn=0, size=RAW):
        return lane.layer * self.PER[lane.block] + turn * size + (self.base[lane.block] + j)

    def prime(self, pool, pe):
        if pool is not None:
            for _ in range(RAW):
                pool.nop().then_inc(self.split, 1)
        if pe is not None:
            for _ in range(SPLIT):
                pe.nop().then_inc(self.done, 1)

    def load(self, sp, j, parts, turn=0, size=RAW):
        assert len(parts) == 2
        sp.eng.wait_ge(self.split, sp.alone(self.number(sp, j, turn, size) + 1))
        for dst, src in parts:
            sp.eng.dma_start(dst, src).then_inc(self.loaded[j % RAW], 16)

    def part(self, pool, j, turn=0, size=RAW, width=1024):
        n = self.number(pool, j, turn, size)
        laps = pool.layer * (self.PER[pool.block] // RAW) + turn * (size // RAW) + (self.base[pool.block] + j) // RAW
        raw, hi, lo = self.raw[j % RAW][:, 0:width], self.hi[j % SPLIT][:, 0:width], self.lo[j % SPLIT][:, 0:width]
        pool.eng.wait_ge(self.loaded[j % RAW], laps * 32 + 32)
        pool.eng.wait_ge(self.done, pool.alone(n + 1))
        pool.eng.tensor_scalar(hi, raw, 1.0, 0.0, MUL, ADD).then_inc(self.hi_made, 1)
        pool.eng.wait_ge(self.hi_made, n + 1)
        pool.eng.tensor_tensor(lo, raw, hi.bitcast(F32), SUB).then_inc(self.split, 1)

    def weights(self, pe, j, turn=0, size=RAW):
        pe.eng.wait_ge(self.split, self.split_is(pe, j, turn, size))
        return self.hi[j % SPLIT], self.lo[j % SPLIT]

    def hi_is(self, pe, j, turn=0, size=RAW):
        return self.number(pe, j, turn, size) + 1

    def split_is(self, pe, j, turn=0, size=RAW):
        return self.number(pe, j, turn, size) + 1 + RAW

    def products(self, lane, j, turn=0, size=RAW):
        return self.number(lane, j, turn, size) + 1 + SPLIT


def two_of_three(pe, out, wh, xh, xl, first):
    pe.matmul(out, wh, xh, start=first, stop=False)
    pe.matmul(out, wh, xl, start=False, stop=False)


def triple(pe, out, wh, wl, xh, xl, first, last):
    pe.matmul(out, wh, xh, start=first, stop=False)
    pe.matmul(out, wh, xl, start=False, stop=False)
    return pe.matmul(out, wl, xh, start=False, stop=last)


def flat(ap):
    return ap.rearrange("p a b -> p (a b)")


def over(ap, shape):
    return ap.broadcast_to(shape)


def build(nc, t, out):
    ctx = ExitStack()
    with ctx:
        def sb(name, shape, dt=F32, to=ctx):
            return to.enter_context(nc.sbuf_tensor(name, shape, dt))

        def sem(name):
            return ctx.enter_context(nc.semaphore(name))

        def signal(name, step=1):
            return Signal(name, sem(name), step)

        y_dram = nc.dram_tensor("y_rows", (NB * P, D), F32).ap()
        h = sb("h", [P, NT, D])
        xT_hi = sb("xT_hi", [P, KC, S], F32R)
        xT_lo = sb("xT_lo", [P, KC, S], F32R)
        ring = Stream(sb, sem)
        konst = sb("konst", [P, K_END])
        gb = sb("gb", [P, 2, D])
        cosA, sinA = sb("cosA", [P, S]), sb("sinA", [P, S])
        cosB, sinB = sb("cosB", [P, S]), sb("sinB", [P, S])
        small = sb("small", [P, 4])
        pace = sb("pace", [P, 2], I32)
        zeros = sb("zeros", [P, P])
        mean_of = sb("mean_of", [P, P])
        ones = sb("ones", [P, P])
        stats = sb("stats", [P, NT, 2, 6])
        mv = sb("mv", [P, NT, 2])
        sd = sb("sd", [P, NT])
        rs = sb("rs", [P, NT])
        pcol = sb("pcol", [P, 224])
        gaup = sb("gaup", [32, 2, P])
        eps, unit1 = small[:, 0:1], small[:, 1:2]
        ident = konst[:, K_ID:K_ID + P]
        bank = [ctx.enter_context(nc.psum_tensor(f"bank{i}", [P, S], F32)) for i in range(8)]

        one = ExitStack()
        s1 = lambda name, shape, dt=F32: sb(name, shape, dt, one)
        proj = s1("proj", [P, 16, S])
        glu = s1("glu", [P, 2, S + 2 * HALO])
        u = s1("u", [P, 2, S])
        scp = s1("scp", [P, 2, S + 2])
        ya = s1("ya", [P, 2, S])
        sq = s1("sq", [P, 2, S])
        rstd = s1("rstd", [P, S])
        gvgg = s1("gvgg", [P, NT, S])
        prow = s1("prow", [96, P])
        prow2 = s1("prow2", [66, 2, P])
        ghead = s1("ghead", [P, W])
        og = s1("og", [P, NT, W])
        gst = s1("gst", [P, 3 * 16])
        attn = ExitStack()
        s2 = lambda name, shape, dt=F32: sb(name, shape, dt, attn)
        lax = s2("lax", [P, 2, S])
        eqk = s2("eqk", [P, 2, 2, S])
        qikd = s2("qikd", [P, 2, 2, S])
        gsm = s2("gsm", [P, 2, 3, NT])
        gse = s2("gse", [P, 2, 3, NT])
        kdT = s2("kdT", [P, 8, P])
        qbd = [s2(f"qbd{i}", [P, GH, P]) for i in range(2)]
        sT = [s2(f"sT{i}", [P, GH, P]) for i in range(2)]
        state, stnew = s2("state", [P, W]), s2("stnew", [P, W])
        attn.close()
        attn = ExitStack()
        c_hi, c_lo = s2("c_hi", [P, 3, S], F32R), s2("c_lo", [P, 3, S], F32R)
        vml = s2("vml", [P, NT, W])
        pm = [s2(f"pm{i}", [P, S]) for i in range(2)]
        pT = [s2(f"pT{i}", [P, NT, P]) for i in range(2)]
        msum, mmx, mrs = s2("msum", [P, 16]), s2("mmx", [P, 16]), s2("mrs", [P, 16])
        attn.close()
        one.close()
        qh, kh = proj[:, 4:8, :], proj[:, 0:4, :]

        ffn = ExitStack()
        s4 = lambda name, shape, dt=F32: sb(name, shape, dt, ffn)
        g_hi, g_lo = s4("g_hi", [P, FC, S], F32R), s4("g_lo", [P, FC, S], F32R)
        ubuf = s4("ubuf", [P, 4, S + 2])
        cv = [s4(f"cv{i}", [P, S]) for i in range(2)]
        ffn.close()

        ld = signal("ld_start", 16)
        v_step, a_step = signal("v_step"), signal("a_step")
        set_up = signal("set_up")
        tab_arg, tab_sin = signal("tab_arg"), signal("tab_sin")
        gb_ld = signal("gb_ld", 16)
        norm_var, norm_sd, norm_z = signal("norm_var"), signal("norm_sd"), signal("norm_z")
        tile_sum = signal("tile_sum")
        norm_tr, norm_hi, norm_lo = signal("norm_tr"), signal("norm_hi"), signal("norm_lo")
        par_ld = signal("par_ld", 16)
        par_tr, par_col = signal("par_tr"), signal("par_col")
        proj_ev = signal("proj_ev")
        ga_mm, la_part, la_x, gexp = signal("ga_mm"), signal("la_part"), signal("la_x"), signal("gexp")
        gv_ev = signal("gv_ev")
        rms_in, rms_sq, rms_mm, rms_rs = signal("rms_in"), signal("rms_sq"), signal("rms_mm"), signal("rms_rs")
        y_val, y_hi, y_lo = signal("y_val"), signal("y_hi"), signal("y_lo")
        cfm_mm, cfm_dev, cfm_ln = signal("cfm_mm"), signal("cfm_dev"), signal("cfm_ln")
        kd_val, kd_tr, kd_ev = signal("kd_val"), signal("kd_tr"), signal("kd_ev")
        g_q, g_s, g_m, g_o, g_st, g_state, g_oev = (signal(n) for n in (
            "gla_q", "gla_scores", "gla_masked", "gla_out", "gla_kv", "gla_state", "gla_out_read"))
        tok_ms, tok_sd, tok_y, tok_tr, tok_hi, tok_lo = (signal(n) for n in (
            "tok_ms", "tok_sd", "tok_y", "tok_tr", "tok_hi", "tok_lo"))
        c_val, c_h, c_l = signal("c_val"), signal("c_h"), signal("c_l")
        head_ev, head_sw, head_rope, k_cp, v_ev = (signal(n) for n in (
            "head_ev", "head_sw", "head_rope", "k_cp", "v_ev"))
        at_s, at_mx, at_p, at_t, at_te, at_o = (signal(n) for n in (
            "at_scores", "at_max", "at_p", "at_tr", "at_pT", "at_out"))
        up_ev, up_cv, up_act, up_val, up_hi, up_lo = (signal(n) for n in (
            "up_ev", "up_conv", "up_silu", "up_val", "up_hi", "up_lo"))
        y_zero = signal("y_zero", 16)
        stored, began = sem("stored"), sem("began")

        block = ctx.enter_context(nc.Block())

        def norm_v(V, n, last_unit, summed=None):
            def sums(i):
                if summed:
                    summed(i)
                if last_unit is None:
                    return
                if i < NT - 1:
                    V.eng.wait_ge(tile_sum.sem, tile_sum.at(V, (NT - 1) * n + i + 1))
                else:
                    V.eng.wait_ge(ring.done, ring.products(V, last_unit))
                for x in range(2):
                    c = slice(x * S, x * S + S)
                    V.eng.scalar_tensor_tensor(h[:, i, c], h[:, i, c], ALPHA, bank[2 * i + x][:], MUL, ADD).then_inc(v_step.sem, v_step.up(V))

            def moments(i):
                for x in range(2):
                    V.eng.bn_stats(stats[:, i, x, :], h[:, i, x * S:x * S + S]).then_inc(v_step.sem, v_step.up(V))

            def variance(i):
                V.eng.wait_ge(v_step.sem, V.alone(v_step.last(V)))
                V.eng.bn_aggr(mv[:, i, :], flat(stats[:, i, :, :])).then_inc(norm_var.sem, norm_var.up(V))

            def low(i):
                for x in range(2):
                    V.eng.wait_ge(norm_hi.sem, norm_hi.at(V, 2 * (NT * n + i) + x + 1))
                    V.eng.tensor_tensor(
                        xT_lo[:, 4 * x:4 * x + 4, i * P:i * P + P], bank[2 * i + x][:].rearrange("p (k t) -> p k t", k=4),
                        xT_hi[:, 4 * x:4 * x + 4, i * P:i * P + P].bitcast(F32), SUB).then_inc(norm_lo.sem, norm_lo.up(V))

            sums(0)
            if last_unit is not None or summed:
                V.eng.wait_ge(v_step.sem, v_step.last(V))
            moments(0)
            variance(0)
            V.eng.wait_ge(gb_ld.sem, gb_ld.at(V, 2 * n + 2))
            for i in range(NT):
                V.eng.wait_ge(norm_sd.sem, norm_sd.at(V, NT * n + i + 1))
                V.eng.reciprocal(rs[:, i:i + 1], sd[:, i:i + 1]).then_inc(v_step.sem, v_step.up(V))
                if i + 1 < NT:
                    sums(i + 1)
                V.eng.scalar_tensor_tensor(h[:, i, :], h[:, i, :], mv[:, i, 0:1], gb[:, 0, :], SUB, MUL).then_inc(v_step.sem, v_step.up(V))
                if i + 1 < NT:
                    V.eng.wait_ge(v_step.sem, v_step.last(V, 1))
                    moments(i + 1)
                    V.eng.wait_ge(v_step.sem, v_step.last(V, 2))
                else:
                    V.eng.wait_ge(v_step.sem, v_step.last(V))
                V.eng.scalar_tensor_tensor(h[:, i, :], h[:, i, :], rs[:, i:i + 1], gb[:, 1, :], MUL, ADD).then_inc(norm_z.sem, norm_z.up(V))
                if i + 1 < NT:
                    variance(i + 1)
                if i:
                    low(i - 1)
            low(NT - 1)

        def norm_a(A, n):
            def deviation(i):
                A.eng.wait_ge(norm_var.sem, norm_var.at(A, NT * n + i + 1))
                A.eng.activation(sd[:, i:i + 1], mv[:, i, 1:2], ACT.Sqrt, bias=eps).then_inc(norm_sd.sem, norm_sd.up(A))

            def high(i):
                for x in range(2):
                    A.eng.wait_ge(norm_tr.sem, norm_tr.at(A, 2 * (NT * n + i) + x + 1))
                    A.eng.activation(xT_hi[:, 4 * x:4 * x + 4, i * P:i * P + P],
                                            bank[2 * i + x][:].rearrange("p (k t) -> p k t", k=4), ACT.Copy).then_inc(norm_hi.sem, norm_hi.up(A))

            deviation(0)
            deviation(1)
            for i in range(NT):
                if i + 2 < NT:
                    deviation(i + 2)
                high(i)

        def norm_pe(T, n):
            for i in range(NT):
                T.eng.wait_ge(norm_z.sem, norm_z.at(T, NT * n + i + 1))
                for x in range(2):
                    for k in range(4):
                        last = T.eng.transpose(bank[2 * i + x][:, k * P:k * P + P],
                                               h[:, i, (4 * x + k) * P:(4 * x + k + 1) * P], ident)
                    last.then_inc(norm_tr.sem, norm_tr.up(T))

        def load_gb(A, g_row, b_row):
            A.eng.dma_start(gb[:, 0, :], over(g_row, [P, D])).then_inc(gb_ld.sem, gb_ld.up(A))
            A.eng.dma_start(gb[:, 1, :], over(b_row, [P, D])).then_inc(gb_ld.sem, gb_ld.up(A))

        def row(name, layer):
            return t[name][bass.ds(layer, 1), :]

        def chunk(T, units, j, out_bank, cols=slice(0, P), turn=0, size=RAW, kc=KC, n=S, src=None):
            wh, wl = (w[j % SPLIT][:, 0:kc * P].rearrange("p (k c) -> p k c", c=P) for w in (units.hi, units.lo))
            xh, xl = src or ([xT_hi[:, k, :] for k in range(kc)], [xT_lo[:, k, :] for k in range(kc)])
            T.eng.wait_ge(units.hi_made, units.hi_is(T, j, turn, size))
            for k in range(kc):
                two_of_three(T.eng, out_bank[:, 0:n], wh[:, k, :], xh[k], xl[k], k == 0)
            T.eng.wait_ge(units.split, units.split_is(T, j, turn, size))
            for k in range(kc):
                last = T.eng.matmul(out_bank[:, 0:n], wl[:, k, :], xh[k], start=False, stop=k == kc - 1)
            last.then_inc(units.done, 1)

        CHUNKS = [C_A, C_GATE, C_A + P, C_GATE + P, C_SCB, C_SCB + P, C_SCC, C_SCC + P, C_SCH, C_SCH + P,
                  C_GQ, C_GK, None, C_CQ, C_CQ + P, C_CKV]
        ORDER = [10, 11, 12, 0, 1, 2, 3, 4, 5, 6, 7, 8, 9, 13, 14, 15]
        POS = {c: k for k, c in enumerate(ORDER)}
        U_GV, U_UQ, U_UKV, U_OUT, U_UP, U_DOWN = 5, 20, 21, 22, 30, 74
        U_OF = [k if k < U_GV else k + 4 for k in range(16)]
        GLA0 = 8
        TAPS0, TAPS_STEP = 22, 5
        GA, KR, CQ, CKV = 12, 12, 13, 15
        Q_G, B_GA, G_Q, G_KV, W_CF, G_CF, B_CF, G_BR, W_UP = 0, 6, 8, 10, 11, 73, 75, 77, 85

        def col(k):
            return pcol[:, k:k + 1]

        def cols3(j):
            return ring.raw[j % RAW][:, :].rearrange("p (k c) -> p k c", c=P)

        def loads1(E):
            l = E.layer
            w = t["w_in"][bass.ds(l, 1)].rearrange("o (k p) n -> (o p) k n", p=P)
            for k, chunk_no in enumerate(ORDER):
                if k == U_GV:
                    for j in range(4):
                        dst = ring.raw[(U_GV + j) % RAW][:, :].rearrange("p (k n) -> p k n", k=2)
                        ring.load(E, U_GV + j, [(dst[:, x:x + 1, :], w[:, 2 * j + x:2 * j + x + 1, C_GV:C_GV + S]) for x in range(2)])
                j, c = U_OF[k], CHUNKS[chunk_no]
                dst = cols3(j)
                if c is None:
                    parts = [(dst[:, :, 0:64], w[:, :, C_GA:C_GA + 64]), (dst[:, :, 64:P], w[:, :, C_KR:C_KR + 64])]
                else:
                    parts = [(dst[:, 0:4, :], w[:, 0:4, c:c + P]), (dst[:, 4:8, :], w[:, 4:8, c:c + P])]
                ring.load(E, j, parts)
            uq = t["w_mla_uq"][bass.ds(l, 1)].rearrange("o (k p) n -> (o p) k n", p=P)
            dst = ring.raw[U_UQ % RAW][:, 0:768].rearrange("p (k n) -> p k n", k=2)
            ring.load(E, U_UQ, [(dst[:, k:k + 1, :], uq[:, k:k + 1, :]) for k in range(2)])
            ukv = t["w_mla_ukv"][bass.ds(l, 1)].rearrange("o p n -> (o p) n")
            dst = ring.raw[U_UKV % RAW]
            ring.load(E, U_UKV, [(dst[:, x:x + W], ukv[:, x:x + W]) for x in (0, W)])
            rows_unit(E, U_OUT, KC, t["w_out"], l)
            up = t["w_ffn_up"][bass.ds(l, 1)].rearrange("o (k p) n -> (o p) k n", p=P)
            with E.eng.Fori(0, FC // 2) as i:
                for s in range(4):
                    dst, j = cols3(U_UP + s), i * 2 + s // 2 + FC * (s % 2)
                    ring.load(E, U_UP + s, [(dst[:, x:x + 4, :], up[:, x:x + 4, bass.ds(j * P, P)]) for x in (0, 4)], turn=i)
            rows_unit(E, U_DOWN, FC, t["w_ffn_down"], l)

        def rows_unit(E, first, count, w, l):
            w = w[bass.ds(l, 1)].rearrange("o (k p) n -> (o p) k n", p=P)
            for k in range(count):
                dst = ring.raw[(first + k) % RAW]
                ring.load(E, first + k, [(dst[:, x:x + S], w[:, k, x:x + S]) for x in (0, S)])

        def splits1(G):
            for j in range(U_UP):
                ring.part(G, j, width=768 if j == U_UQ else 512 if j == U_UKV else 1024)
            with G.eng.Fori(0, FC // 2) as i:
                for s in range(4):
                    ring.part(G, U_UP + s, turn=i)
            for j in range(U_DOWN, U_DOWN + FC):
                ring.part(G, j)
                if j - U_DOWN < NB // L:
                    rows = bass.ds(G.layer * (NB // L * P) + (j - U_DOWN) * P, P)
                    G.eng.dma_start(y_dram[rows, :].rearrange("p (x c) -> p x c", c=P), over(zeros[:].unsqueeze(1), [P, KC, P])).then_inc(y_zero.sem, y_zero.up(G))

        def rows_products(T, first, count, x_hi, x_lo, made=None):
            def passes(k, i, hi, lo):
                wh, wl = ring.hi[(first + k) % SPLIT], ring.lo[(first + k) % SPLIT]
                c = slice(i * P, i * P + P)
                for x in range(2):
                    n, o = slice(x * S, x * S + S), bank[2 * i + x][:]
                    if hi:
                        T.eng.matmul(o, x_hi[:, k, c], wh[:, n], start=k == 0, stop=False)
                        T.eng.matmul(o, x_lo[:, k, c], wh[:, n], start=False, stop=False)
                    if lo:
                        last = T.eng.matmul(o, x_hi[:, k, c], wl[:, n], start=False, stop=k == count - 1)
                return last if lo else None

            for k in range(count - 2):
                if made is not None:
                    T.eng.wait_ge(made.sem, made.at(T, k + 1))
                T.eng.wait_ge(ring.hi_made, ring.hi_is(T, first + k))
                for i in range(NT):
                    passes(k, i, True, False)
                T.eng.wait_ge(ring.split, ring.split_is(T, first + k))
                for i in range(NT):
                    last = passes(k, i, False, True)
                last.then_inc(ring.done, 1)
            if made is not None:
                T.eng.wait_ge(made.sem, made.at(T, count))
            T.eng.wait_ge(ring.split, ring.split_is(T, first + count - 2))
            passes(count - 2, 0, True, True)
            passes(count - 2, 1, True, True)
            T.eng.wait_ge(ring.split, ring.split_is(T, first + count - 1))
            for i in range(NT):
                last = passes(count - 1, i, True, True)
                if i < NT - 1:
                    last.then_inc(tile_sum.sem, tile_sum.up(T))
                else:
                    last.then_inc(ring.done, 1)
                if i + 2 < NT:
                    last = passes(count - 2, i + 2, True, True)
                    if i + 3 == NT:
                        last.then_inc(ring.done, 1)

        def rms_t(T, r, first, n, b):
            for i in range(n):
                T.eng.wait_ge(rms_sq.sem, rms_sq.at(T, first + i + 1))
                last = T.eng.matmul(bank[b][:], mean_of[:], sq[:, i, :], start=i == 0, stop=i == n - 1)
            last.then_inc(rms_mm.sem, rms_mm.up(T))

        def tok_t(T, n, src):
            T.eng.wait_ge(tok_y.sem, tok_y.at(T, n + 1))
            for x in range(2):
                for i in range(NT):
                    last = T.eng.transpose(bank[6 + x][:, i * P:i * P + P], src[:, i, x * P:x * P + P], ident)
                last.then_inc(tok_tr.sem, tok_tr.up(T))

        def tensor1(T):
            pe = T.eng
            T.eng.wait_ge(norm_lo.sem, norm_lo.at(T, 0))
            def gv_units():
                T.eng.wait_ge(la_part.sem, la_part.at(T, 4))
                T.eng.wait_ge(par_col.sem, par_col.at(T, 1))
                for j in range(4):
                    wh, wl = ring.weights(T, U_GV + j)
                    for kk in range(2):
                        for i in range(NT):
                            k, c, n = 2 * j + kk, slice(i * P, i * P + P), slice(kk * S, kk * S + S)
                            last = triple(pe, bank[4 + i][:], xT_hi[:, k, c], xT_lo[:, k, c], wh[:, n], wl[:, n], k == 0, k == 7)
                    last.then_inc(ring.done, 1)

            def gla_keys():
                T.eng.wait_ge(gv_ev.sem, gv_ev.at(T, 8))
                for d in range(2):
                    T.eng.wait_ge(kd_val.sem, kd_val.at(T, d + 1))
                    for c in range(NT):
                        last = pe.transpose(bank[6 + d][:, c * P:c * P + P], qikd[:, d, 1, c * P:c * P + P], ident)
                    last.then_inc(kd_tr.sem, kd_tr.up(T))

            def gla_scores(n):
                d, c = n // 4, n % 4 if n < 4 else 7 - n
                T.eng.wait_ge(g_q.sem, g_q.at(T, n + 1))
                pe.matmul(bank[2 + n % 2][:], eqk[:, d, 1, c * P:c * P + P], flat(qbd[n % 2][:]), start=True, stop=True).then_inc(g_s.sem, g_s.up(T))
                if n == 0:
                    T.eng.wait_ge(kd_ev.sem, kd_ev.at(T, 2))
                if n % 4 != 3:
                    pe.matmul(bank[6 + n % 2][:, 0:W], kdT[:, 4 * d + c, :], gvgg[:, c, 0:W], start=True, stop=True).then_inc(g_st.sem, g_st.up(T))

            def gla_output(n):
                d, c = n // 4, n % 4 if n < 4 else 7 - n
                T.eng.wait_ge(g_m.sem, g_m.at(T, n + 1))
                T.eng.wait_ge(g_state.sem, g_state.at(T, n + 1))
                if n >= 2:
                    T.eng.wait_ge(g_oev.sem, g_oev.at(T, n - 1))
                pe.matmul(bank[4 + n % 2][:, 0:W], qikd[:, d, 0, c * P:c * P + P], state[:], start=True, stop=False)
                for hh in range(GH):
                    v = slice(hh * GVD, hh * GVD + GVD)
                    last = pe.matmul(bank[4 + n % 2][:, v], sT[n % 2][:, hh, :], gvgg[:, c, v], start=False, stop=hh == GH - 1)
                last.then_inc(g_o.sem, g_o.up(T))

            for k, c in enumerate(ORDER):
                if k == 2:
                    T.eng.wait_ge(par_ld.sem, par_ld.at(T, 13))
                    pe.transpose(bank[7][:, 0:W_UP], prow[0:W_UP, :], ident[0:W_UP, 0:W_UP])
                    pe.transpose(bank[7][:, W_UP:W_UP + 66], prow2[:, 0, :], ident[0:66, 0:66])
                    pe.transpose(bank[7][:, W_UP + 66:W_UP + 132], prow2[:, 1, :], ident[0:66, 0:66]).then_inc(par_tr.sem, par_tr.up(T))
                if k == U_GV:
                    gv_units()
                if k == GLA0:
                    gla_keys()
                if k > GLA0:
                    if k > GLA0 + 1:
                        gla_output(k - GLA0 - 2)
                    gla_scores(k - GLA0 - 1)
                if k >= 2:
                    T.eng.wait_ge(proj_ev.sem, proj_ev.at(T, k - 1))
                chunk(T, ring, U_OF[k], bank[k % 2])
                if k == POS[GA] + 1:
                    T.eng.wait_ge(proj_ev.sem, proj_ev.at(T, POS[GA] + 1))
                    for d in range(2):
                        pe.matmul(bank[4 + d][:], gaup[:, d, :], proj[0:32, GA, :], start=True, stop=True).then_inc(ga_mm.sem, ga_mm.up(T))
            for n in range(16 - GLA0 - 2, 8):
                gla_output(n)
                if n + 1 < 8:
                    gla_scores(n + 1)
            T.eng.wait_ge(proj_ev.sem, proj_ev.at(T, 16))
            rms_t(T, 0, 0, 2, 1)
            rms_t(T, 1, 2, 1, 0)
            T.eng.wait_ge(c_l.sem, c_l.at(T, 2))
            wh, wl = ring.weights(T, U_UQ)
            wh, wl = (w[:, 0:768].rearrange("p (k n) -> p k n", k=2) for w in (wh, wl))
            T.eng.wait_ge(rms_rs.sem, rms_rs.at(T, 2))
            for hh in range(MH):
                for k in range(2):
                    n = slice(hh * MD, hh * MD + MD)
                    last = triple(pe, bank[hh][0:MD, :], wh[:, k, n], wl[:, k, n], c_hi[:, k, :], c_lo[:, k, :], k == 0, k == 1)
            last.then_inc(ring.done, 1)
            for hh in range(MH):
                T.eng.wait_ge(head_ev.sem, head_ev.at(T, hh + 1))
                pe.matmul(bank[4 + hh][0:MD, :], konst[0:MD, K_SWA:K_SWA + MD], qh[0:MD, hh, :], start=True, stop=True).then_inc(head_sw.sem, head_sw.up(T))
            pe.matmul(bank[0][0:MD, :], konst[0:MD, K_SWA:K_SWA + MD], proj[0:MD, KR, :], start=True, stop=True).then_inc(head_sw.sem, head_sw.up(T))
            T.eng.wait_ge(c_l.sem, c_l.at(T, 3))
            wh, wl = ring.weights(T, U_UKV)
            T.eng.wait_ge(head_rope.sem, head_rope.at(T, 5))
            for hh in range(MH):
                n = slice(hh * P, hh * P + P)
                triple(pe, bank[hh][:], wh[:, n], wl[:, n], c_hi[:, 2, :], c_lo[:, 2, :], True, True)
            wh, wl = (w[:, 0:S].rearrange("p (h n) -> p h n", h=MH)[:, :, NOPE:P] for w in (wh, wl))
            for i in range(NT):
                c = slice(i * P, i * P + P)
                last = triple(pe, bank[4 + i // 2][:, (i % 2) * W:(i % 2) * W + W], c_hi[:, 2, c], c_lo[:, 2, c], wh, wl, True, True)
            last.then_inc(ring.done, 1)
            T.eng.wait_ge(v_ev.sem, v_ev.at(T, 1))
            T.eng.wait_ge(k_cp.sem, k_cp.at(T, 7))

            def beside(n):
                if n == 1:
                    rms_t(T, 2, 3, 2, 6)
                    for i in range(2):
                        last = pe.matmul(bank[7][:], mean_of[:], u[:, i, :], start=i == 0, stop=i == 1)
                    last.then_inc(cfm_mm.sem, cfm_mm.up(T))
                if n == 4:
                    T.eng.wait_ge(rms_rs.sem, rms_rs.at(T, 3))
                    rms_t(T, 3, 5, 2, 6)
                if n == 8:
                    rms_t(T, 4, 7, 2, 7)
                if n == 17:
                    tok_t(T, 0, og)

            for n in range(18):
                beside(n)
                if n < 16:
                    hh, i = n // 4, n % 4
                    if n >= 2:
                        T.eng.wait_ge(at_p.sem, at_p.at(T, n - 1))
                    pe.matmul(bank[n % 2][:], qh[0:MD, hh, i * P:i * P + P], kh[0:MD, hh, :], start=True, stop=True).then_inc(at_s.sem, at_s.up(T))
                if 0 < n < 17:
                    m = n - 1
                    T.eng.wait_ge(at_p.sem, at_p.at(T, m + 1))
                    if m >= 2:
                        T.eng.wait_ge(at_te.sem, at_te.at(T, m - 1))
                    for k in range(NT):
                        last = pe.transpose(bank[2 + m % 2][:, k * P:k * P + P], pm[m % 2][:, k * P:k * P + P], ident)
                    last.then_inc(at_t.sem, at_t.up(T))
                if n > 1:
                    m = n - 2
                    hh, i = m // 4, m % 4
                    T.eng.wait_ge(at_te.sem, at_te.at(T, m + 1))
                    for k in range(NT):
                        last = pe.matmul(bank[4 + i // 2][:, i % 2 * W + hh * NOPE:i % 2 * W + hh * NOPE + NOPE], pT[m % 2][:, k, :],
                                         vml[:, k, hh * NOPE:hh * NOPE + NOPE], start=k == 0, stop=k == NT - 1)
                    last.then_inc(at_o.sem, at_o.up(T))
            T.eng.wait_ge(tok_lo.sem, tok_lo.at(T, 2))
            tok_t(T, 1, og)
            T.eng.wait_ge(y_lo.sem, y_lo.at(T, 4))
            T.eng.wait_ge(tok_lo.sem, tok_lo.at(T, 4))
            rows_products(T, U_OUT, KC, xT_hi, xT_lo)
            norm_pe(T, 0)
            T.eng.wait_ge(norm_lo.sem, T.alone(norm_lo.at(T, 8)))
            with pe.Fori(0, FC // 2) as i:
                for s in range(4):
                    if s == 3:
                        T.eng.wait_ge(up_ev.sem, up_ev.at(T, i * 4 + 1))
                    chunk(T, ring, U_UP + s, bank[s], turn=i)
                T.eng.wait_ge(up_ev.sem, up_ev.at(T, i * 4 + 3))
            T.eng.wait_ge(up_lo.sem, up_lo.at(T, FC))
            T.eng.wait_ge(up_ev.sem, up_ev.at(T, 2 * FC))
            rows_products(T, U_DOWN, FC, g_hi, g_lo)
            norm_pe(T, 1)

        def squares_a(A, srcs):
            for i, src in enumerate(srcs):
                A.eng.activation(sq[:, i, :], src, ACT.Square).then_inc(rms_sq.sem, rms_sq.up(A))

        def rstd_a(A, r, b, scale=1.0):
            A.eng.wait_ge(rms_mm.sem, rms_mm.at(A, r + 1))
            A.eng.activation(rstd[:], bank[b][:], ACT.Ln, bias=eps, scale=scale).then_inc(a_step.sem, a_step.up(A))
            A.eng.wait_ge(a_step.sem, a_step.last(A))
            A.eng.activation(rstd[:], rstd[:], ACT.Exp, scale=-0.5).then_inc(rms_rs.sem, rms_rs.up(A))
            A.eng.wait_ge(rms_rs.sem, rms_rs.last(A))

        def gain_a(A, first, dst, src):
            for i in range(2):
                A.eng.wait_ge(y_val.sem, y_val.at(A, first + i + 1))
                A.eng.activation(xT_hi[:, dst + i, :], src[:, i, :], ACT.Copy, scale=col(G_BR + dst + i)).then_inc(y_hi.sem, y_hi.up(A))

        def tok_sd_a(A, k, cnt, scale):
            A.eng.wait_ge(tok_ms.sem, tok_ms.at(A, k))
            A.eng.activation(gst[:, 16:16 + cnt], gst[:, 0:cnt], ACT.Sqrt, bias=eps, scale=scale).then_inc(tok_sd.sem, tok_sd.up(A))

        def tok_hi_a(A, n, dst):
            for x in range(2):
                A.eng.wait_ge(tok_tr.sem, tok_tr.at(A, 2 * n + x + 1))
                A.eng.activation(xT_hi[:, dst + x, :], bank[6 + x][:], ACT.Copy, scale=col(G_BR + dst + x)).then_inc(tok_hi.sem, tok_hi.up(A))

        def scalar1(A):
            act, l = A.eng, A.layer
            act.dma_start(prow[0:6, :], t["w_sc_conv"][bass.ds(l, 1)].rearrange("o t (c p) -> (o t c) p", p=P)).then_inc(par_ld.sem, par_ld.up(A))
            act.dma_start(prow[6:8, :], t["b_gla_a"][bass.ds(l, 1)].rearrange("o d p -> (o d) p")).then_inc(par_ld.sem, par_ld.up(A))
            act.dma_start(prow[8:10, :], t["g_mla_q"][bass.ds(l, 1)].rearrange("o (c p) -> (o c) p", p=P)).then_inc(par_ld.sem, par_ld.up(A))
            act.dma_start(prow[10:11, :], t["g_mla_kv"][bass.ds(l, 1)]).then_inc(par_ld.sem, par_ld.up(A))
            act.dma_start(prow[11:73, :], t["w_cfm_dw"][bass.ds(l, 1)].rearrange("o t (c p) -> (o t c) p", p=P)).then_inc(par_ld.sem, par_ld.up(A))
            act.dma_start(prow[73:75, :], t["g_cfm_ln"][bass.ds(l, 1)].rearrange("o (c p) -> (o c) p", p=P)).then_inc(par_ld.sem, par_ld.up(A))
            act.dma_start(prow[75:77, :], t["b_cfm_ln"][bass.ds(l, 1)].rearrange("o (c p) -> (o c) p", p=P)).then_inc(par_ld.sem, par_ld.up(A))
            act.dma_start(prow[77:85, :], t["g_branch"][bass.ds(l, 1)].rearrange("o (c p) -> (o c) p", p=P)).then_inc(par_ld.sem, par_ld.up(A))
            dw = t["w_ffn_dw"][bass.ds(l, 1)].rearrange("o t (c p) -> (o t c) p", p=P)
            for x in range(2):
                act.dma_start(prow2[:, x, :], dw[x * 66:x * 66 + 66, :]).then_inc(par_ld.sem, par_ld.up(A))
                act.dma_start(gaup[16 * x:16 * x + 16, x, :], t["w_gla_a_up"][bass.ds(l, 1), x, :, :].rearrange("o r n -> (o r) n")).then_inc(par_ld.sem, par_ld.up(A))
            act.dma_start(ghead[:], over(t["g_gla_head"][bass.ds(l, 1), :], [P, W])).then_inc(par_ld.sem, par_ld.up(A))
            load_gb(A, t["ln1_g"][bass.ds(l, 1), :], t["ln1_b"][bass.ds(l, 1), :])
            for k, c in enumerate(ORDER):
                if k == U_GV:
                    A.eng.wait_ge(ring.done, ring.products(A, U_GV + 3))
                    for i in range(NT):
                        act.activation(gvgg[:, i, 0:W], bank[4 + i][:, 0:W], ACT.Copy).then_inc(gv_ev.sem, gv_ev.up(A))
                        act.activation(gvgg[:, i, W:S], bank[4 + i][:, W:S], ACT.Silu).then_inc(gv_ev.sem, gv_ev.up(A))
                    A.eng.wait_ge(la_x.sem, la_x.at(A, 1))
                    for d in range(2):
                        act.activation(eqk[:, d, 0, :], lax[:, d, :], ACT.Exp, scale=1.0 / TAU).then_inc(gexp.sem, gexp.up(A))
                        act.activation(eqk[:, d, 1, :], lax[:, d, :], ACT.Exp, scale=-1.0 / TAU).then_inc(gexp.sem, gexp.up(A))
                    act.activation(gse[:], gsm[:], ACT.Exp, scale=1.0 / TAU).then_inc(gexp.sem, gexp.up(A))
                if k == GLA0:
                    for d in range(2):
                        A.eng.wait_ge(kd_tr.sem, kd_tr.at(A, d + 1))
                        act.activation(kdT[:, 4 * d:4 * d + 4, :], bank[6 + d][:].rearrange("p (c n) -> p c n", c=4), ACT.Copy).then_inc(kd_ev.sem, kd_ev.up(A))
                A.eng.wait_ge(ring.done, ring.products(A, U_OF[k]))
                act.activation(proj[:, c, :], bank[k % 2][:], ACT.Sigmoid if c in (1, 3) else ACT.Copy).then_inc(proj_ev.sem, proj_ev.up(A))
                if c == GA:
                    A.eng.wait_ge(proj_ev.sem, proj_ev.last(A))
                    A.eng.wait_ge(par_col.sem, par_col.at(A, 1))
                    for d in range(2):
                        A.eng.wait_ge(ga_mm.sem, ga_mm.at(A, d + 1))
                        act.activation(lax[:, d, :], bank[4 + d][:], ACT.Identity, bias=col(B_GA + d)).then_inc(la_part.sem, la_part.up(A))
                        act.activation(qikd[:, d, 0, :], bank[4 + d][:], ACT.Abs, bias=col(B_GA + d)).then_inc(a_step.sem, a_step.up(A))
                        A.eng.wait_ge(a_step.sem, a_step.last(A))
                        act.activation(qikd[:, d, 0, :], qikd[:, d, 0, :], ACT.Exp, scale=-1.0).then_inc(a_step.sem, a_step.up(A))
                        A.eng.wait_ge(a_step.sem, a_step.last(A))
                        act.activation(qikd[:, d, 0, :], qikd[:, d, 0, :], ACT.Ln, bias=unit1).then_inc(la_part.sem, la_part.up(A))
            A.eng.wait_ge(proj_ev.sem, proj_ev.last(A))
            squares_a(A, [proj[:, CQ + i, :] for i in range(2)])
            rstd_a(A, 0, 1)
            A.eng.wait_ge(c_val.sem, c_val.at(A, 2))
            squares_a(A, [proj[:, CKV, :]])
            rstd_a(A, 1, 0, scale=2.0)
            for i in range(3):
                A.eng.wait_ge(c_val.sem, c_val.at(A, i + 1))
                act.activation(c_hi[:, i, :], proj[:, CQ + i, :], ACT.Copy).then_inc(c_h.sem, c_h.up(A))
            A.eng.wait_ge(ring.done, ring.products(A, U_UQ))
            A.eng.wait_ge(rms_in.sem, rms_in.at(A, 1))
            for hh in range(MH):
                act.activation(qh[0:MD, hh, :], bank[hh][0:MD, :], ACT.Copy).then_inc(head_ev.sem, head_ev.up(A))
            A.eng.wait_ge(ring.done, ring.products(A, U_UKV))
            for hh in range(MH):
                act.activation(kh[0:NOPE, hh, :], bank[hh][0:NOPE, :], ACT.Copy).then_inc(k_cp.sem, k_cp.up(A))
            A.eng.wait_ge(head_rope.sem, head_rope.at(A, 5))
            for hh in range(1, MH):
                act.activation(kh[R0:MD, hh, :], kh[R0:MD, 0, :], ACT.Copy).then_inc(k_cp.sem, k_cp.up(A))

            def beside(n):
                if n == 0:
                    A.eng.wait_ge(rms_in.sem, rms_in.at(A, 1))
                    squares_a(A, [ya[:, i, :] for i in range(2)])
                if n == 2:
                    rstd_a(A, 2, 6)
                if n == 3:
                    A.eng.wait_ge(rms_in.sem, rms_in.at(A, 2))
                    squares_a(A, [u[:, i, :] for i in range(2)])
                if n == 4:
                    gain_a(A, 0, 0, ya)
                if n == 5:
                    rstd_a(A, 3, 6)
                if n == 7:
                    for i in range(2):
                        A.eng.wait_ge(cfm_ln.sem, cfm_ln.at(A, i + 1))
                        act.activation(u[:, i, :], u[:, i, :], ACT.Silu, bias=col(B_CF + i)).then_inc(a_step.sem, a_step.up(A))
                    A.eng.wait_ge(a_step.sem, a_step.last(A))
                    squares_a(A, [u[:, i, :] for i in range(2)])
                if n == 9:
                    rstd_a(A, 4, 7)
                if n == 11:
                    gain_a(A, 2, 6, u)
                if n == 12:
                    tok_sd_a(A, 1, 16, 1.0 / GVD)
                if n == 15:
                    tok_sd_a(A, 2, 4, 1.0 / W)

            for n in range(16):
                beside(n)
                A.eng.wait_ge(at_s.sem, at_s.at(A, n + 1))
                A.eng.wait_ge(at_mx.sem, at_mx.at(A, n + 1))
                if n >= 2:
                    A.eng.wait_ge(at_t.sem, at_t.at(A, n - 1))
                act.activation(pm[n % 2][:], bank[n % 2][:], ACT.Exp, bias=mmx[:, n:n + 1], scale=MLA_SCALE,
                                      accum_out=msum[:, n:n + 1]).then_inc(at_p.sem, at_p.up(A))
            tok_hi_a(A, 0, 2)
            tok_sd_a(A, 3, 4, 1.0 / W)
            tok_hi_a(A, 1, 4)
            norm_a(A, 0)
            load_gb(A, t["ln2_g"][bass.ds(l, 1), :], t["ln2_b"][bass.ds(l, 1), :])
            with act.Fori(0, FC // 2) as i:
                A.loop("a_up", i)
                for s in range(4):
                    A.eng.wait_ge(ring.done, ring.products(A, U_UP + s, turn=i))
                    act.activation(ubuf[:, s, 1:S + 1], bank[s][:], ACT.Copy).then_inc(up_ev.sem, up_ev.up(A))
                    if s == 1:
                        silu_hi(A, i, 0, False)
                silu_hi(A, i, 0, True)
                silu_hi(A, i, 1, False)
                silu_hi(A, i, 1, True)
                A.loop_end(FC // 2)
            norm_a(A, 1)

        def silu_hi(A, i, q, hi):
            if not hi:
                A.eng.wait_ge(up_cv.sem, up_cv.at(A, i * 4 + 2 * q + 1))
                A.eng.activation(cv[0][:], cv[0][:], ACT.Silu).then_inc(up_act.sem, up_act.up(A))
            else:
                A.eng.wait_ge(up_val.sem, up_val.at(A, i * 2 + q + 1))
                A.eng.activation(g_hi[:, bass.ds(i * 2 + q, 1), :], cv[0][:].unsqueeze(1), ACT.Copy).then_inc(up_hi.sem, up_hi.up(A))

        def gain_v(V, first, dst, src):
            for i in range(2):
                V.eng.wait_ge(y_hi.sem, y_hi.at(V, first + i + 1))
                V.eng.scalar_tensor_tensor(xT_lo[:, dst + i, :], src[:, i, :], col(G_BR + dst + i),
                                                  xT_hi[:, dst + i, :].bitcast(F32), MUL, SUB).then_inc(y_lo.sem, y_lo.up(V))

        def tok_ms_v(V, w):
            V.eng.tensor_tensor(flat(sq[:]), flat(og[:]), flat(og[:]), MUL).then_inc(v_step.sem, v_step.up(V))
            V.eng.wait_ge(v_step.sem, v_step.last(V))
            V.eng.tensor_reduce(gst[:, 0:NT * W // w], flat(sq[:]).rearrange("p (g n) -> p g n", n=w), AX.X, ADD).then_inc(tok_ms.sem, tok_ms.up(V))
            V.eng.wait_ge(tok_ms.sem, tok_ms.last(V))

        def tok_y_v(V, k):
            V.eng.wait_ge(tok_sd.sem, tok_sd.at(V, k))
            V.eng.reciprocal(gst[:, 32:36], gst[:, 16:20]).then_inc(v_step.sem, v_step.up(V))
            V.eng.wait_ge(v_step.sem, v_step.last(V))
            V.eng.tensor_tensor(og[:], og[:], over(gst[:, 32:36].unsqueeze(2), [P, NT, W]), MUL).then_inc(tok_y.sem, tok_y.up(V))
            V.eng.wait_ge(tok_y.sem, tok_y.last(V))

        def tok_lo_v(V, n, dst):
            for x in range(2):
                V.eng.wait_ge(tok_hi.sem, tok_hi.at(V, 2 * n + x + 1))
                V.eng.scalar_tensor_tensor(xT_lo[:, dst + x, :], bank[6 + x][:], col(G_BR + dst + x),
                                                  xT_hi[:, dst + x, :].bitcast(F32), MUL, SUB).then_inc(tok_lo.sem, tok_lo.up(V))

        def vector1(V):
            v = V.eng
            V.eng.wait_ge(par_tr.sem, par_tr.at(V, 1))
            v.tensor_copy(pcol[:, 0:W_UP + 132], bank[7][:, 0:W_UP + 132]).then_inc(par_col.sem, par_col.up(V))
            V.eng.wait_ge(par_col.sem, par_col.last(V))
            v.memset(glu[:], 0.0).then_inc(v_step.sem, v_step.up(V))
            v.memset(scp[:], 0.0).then_inc(v_step.sem, v_step.up(V))
            V.eng.wait_ge(v_step.sem, v_step.last(V))
            def short_conv():
                for i in range(2):
                    V.eng.wait_ge(proj_ev.sem, proj_ev.at(V, POS[9] + 1))
                    v.tensor_tensor(scp[:, i, 1:S + 1], proj[:, 6 + i, :], proj[:, 8 + i, :], MUL).then_inc(v_step.sem, v_step.up(V))
                    V.eng.wait_ge(v_step.sem, v_step.last(V))
                    v.tensor_scalar(ya[:, i, :], scp[:, i, 0:S], col(Q_G + i), None, MUL).then_inc(v_step.sem, v_step.up(V))
                    V.eng.wait_ge(v_step.sem, v_step.last(V))
                    for tap in (1, 2):
                        v.scalar_tensor_tensor(ya[:, i, :], scp[:, i, tap:tap + S], col(Q_G + 2 * tap + i), ya[:, i, :], MUL, ADD).then_inc(v_step.sem, v_step.up(V))
                        V.eng.wait_ge(v_step.sem, v_step.last(V))
                    raised = rms_in if i else v_step
                    v.tensor_tensor(ya[:, i, :], ya[:, i, :], proj[:, 4 + i, :], MUL).then_inc(raised.sem, raised.up(V))
                    V.eng.wait_ge(raised.sem, raised.last(V))

            V.eng.wait_ge(la_part.sem, la_part.at(V, 4))
            for d in range(2):
                v.scalar_tensor_tensor(lax[:, d, :], lax[:, d, :], 0.0, qikd[:, d, 0, :], MIN, SUB).then_inc(v_step.sem, v_step.up(V))
                V.eng.wait_ge(v_step.sem, v_step.last(V))
                for c in range(NT):
                    cs = slice(c * P, c * P + P)
                    v.tensor_tensor_scan(eqk[:, d, 0, cs], ones[:], lax[:, d, cs], 0.0, MUL, ADD).then_inc(v_step.sem, v_step.up(V))
                V.eng.wait_ge(v_step.sem, v_step.last(V))
            x4 = lambda ap: ap.rearrange("p (c n) -> p c n", c=NT)
            b0, b1 = x4(eqk[:, 0, 0, :]), x4(eqk[:, 1, 0, :])
            xb = x4(eqk[:, 1, 1, :])
            v.tensor_tensor(xb, x4(lax[:, 1, :]), b1, SUB).then_inc(v_step.sem, v_step.up(V))
            V.eng.wait_ge(v_step.sem, v_step.last(V))
            tot0, tot1, mid0, mid1 = b0[:, :, P - 1:P], b1[:, :, P - 1:P], b0[:, :, 64:65], xb[:, :, 64:65]
            g3 = lambda d, k: gsm[:, d, k, :].unsqueeze(2)
            v.tensor_copy(g3(0, 0), mid0).then_inc(v_step.sem, v_step.up(V))
            v.tensor_tensor(g3(0, 1), tot0, mid0, SUB).then_inc(v_step.sem, v_step.up(V))
            v.tensor_copy(g3(0, 2), tot0).then_inc(v_step.sem, v_step.up(V))
            v.tensor_tensor(g3(1, 0), mid1, tot1, ADD).then_inc(v_step.sem, v_step.up(V))
            v.tensor_scalar(g3(1, 1), mid1, -1.0, None, MUL).then_inc(v_step.sem, v_step.up(V))
            v.tensor_copy(g3(1, 2), tot1).then_inc(v_step.sem, v_step.up(V))
            v.tensor_tensor(x4(lax[:, 0, :]), b0, over(mid0, [P, NT, P]), SUB).then_inc(v_step.sem, v_step.up(V))
            v.tensor_tensor(x4(lax[:, 1, :]), xb, over(mid1, [P, NT, P]), SUB).then_inc(la_x.sem, la_x.up(V))
            V.eng.wait_ge(la_x.sem, la_x.last(V))
            taps = [(tap, i) for i in range(2) for tap in range(TAPS)]

            def conformer(count):
                for _ in range(min(count, len(taps))):
                    tap, i = taps.pop(0)
                    w = col(W_CF + 2 * tap + i)
                    if tap == 0:
                        V.eng.wait_ge(proj_ev.sem, proj_ev.at(V, POS[2 * i + 1] + 1))
                        v.tensor_tensor(glu[:, i, HALO:HALO + S], proj[:, 2 * i, :], proj[:, 2 * i + 1, :], MUL).then_inc(v_step.sem, v_step.up(V))
                        V.eng.wait_ge(v_step.sem, v_step.last(V))
                        v.tensor_scalar(u[:, i, :], glu[:, i, 0:S], w, None, MUL).then_inc(v_step.sem, v_step.up(V))
                        V.eng.wait_ge(v_step.sem, v_step.last(V))
                    else:
                        v.scalar_tensor_tensor(u[:, i, :], glu[:, i, tap:tap + S], w, u[:, i, :], MUL, ADD).then_inc(v_step.sem, v_step.up(V))
                        V.eng.wait_ge(v_step.sem, v_step.last(V))

            conformer(TAPS0)
            V.eng.wait_ge(gexp.sem, gexp.at(V, 5))
            for d in range(2):
                qt, kt, qi, kd = eqk[:, d, 0, :], eqk[:, d, 1, :], qikd[:, d, 0, :], qikd[:, d, 1, :]
                v.scalar_tensor_tensor(qt, proj[:, 10, :], GK ** -0.5, qt, MUL, MUL).then_inc(v_step.sem, v_step.up(V))
                V.eng.wait_ge(v_step.sem, v_step.last(V))
                v.tensor_tensor(kt, proj[:, 11, :], kt, MUL).then_inc(v_step.sem, v_step.up(V))
                V.eng.wait_ge(v_step.sem, v_step.last(V))
                v.tensor_tensor(x4(qi), x4(qt), over(gse[:, d, 0, :].unsqueeze(2), [P, NT, P]), MUL).then_inc(v_step.sem, v_step.up(V))
                V.eng.wait_ge(v_step.sem, v_step.last(V))
                v.tensor_tensor(x4(kd), x4(kt), over(gse[:, d, 1, :].unsqueeze(2), [P, NT, P]), MUL).then_inc(kd_val.sem, kd_val.up(V))
                V.eng.wait_ge(kd_val.sem, kd_val.last(V))
            head = konst[:, K_HEAD:K_HEAD + GH].unsqueeze(2)

            def spread(n):
                d, c = n // 4, n % 4 if n < 4 else 7 - n
                v.tensor_tensor(qbd[n % 2][:], over(eqk[:, d, 0, c * P:c * P + P].unsqueeze(1), [P, GH, P]), over(head, [P, GH, P]), MUL).then_inc(g_q.sem, g_q.up(V))

            v.memset(state[:], 0.0).then_inc(g_state.sem, g_state.up(V))
            spread(0)
            for n in range(8):
                d, c = n // 4, n % 4 if n < 4 else 7 - n
                V.eng.wait_ge(g_s.sem, g_s.at(V, n + 1))
                tri = konst[:, K_TRF + P * d:K_TRF + P * d + P].unsqueeze(1)
                v.tensor_tensor(sT[n % 2][:], bank[2 + n % 2][:].rearrange("p (h t) -> p h t", h=GH), over(tri, [P, GH, P]), MUL).then_inc(g_m.sem, g_m.up(V))
                if n + 1 < 8:
                    spread(n + 1)
                if n % 4 != 3:
                    V.eng.wait_ge(g_st.sem, g_st.at(V, n + 1 if n < 4 else n))
                    v.tensor_tensor(stnew[:], bank[6 + n % 2][:, 0:W], konst[:, K_BLK:K_BLK + W], MUL).then_inc(v_step.sem, v_step.up(V))
                    V.eng.wait_ge(v_step.sem, v_step.last(V))
                conformer(TAPS_STEP)
                V.eng.wait_ge(g_o.sem, g_o.at(V, n + 1))
                if n < 4:
                    v.tensor_copy(og[:, c, :], bank[4 + n % 2][:, 0:W]).then_inc(g_oev.sem, g_oev.up(V))
                    V.eng.wait_ge(g_oev.sem, g_oev.last(V))
                else:
                    v.tensor_tensor(og[:, c, :], og[:, c, :], bank[4 + n % 2][:, 0:W], ADD).then_inc(g_oev.sem, g_oev.up(V))
                    V.eng.wait_ge(g_oev.sem, g_oev.last(V))
                if n % 4 != 3:
                    v.scalar_tensor_tensor(state[:], state[:], gse[:, d, 2, c:c + 1], stnew[:], MUL, ADD).then_inc(g_state.sem, g_state.up(V))
                    V.eng.wait_ge(g_state.sem, g_state.last(V))
                elif n == 3:
                    v.memset(state[:], 0.0).then_inc(g_state.sem, g_state.up(V))
                    V.eng.wait_ge(g_state.sem, g_state.last(V))
            V.eng.wait_ge(rms_rs.sem, rms_rs.at(V, 1))
            for i in range(2):
                v.scalar_tensor_tensor(proj[:, CQ + i, :], proj[:, CQ + i, :], col(G_Q + i), rstd[:], MUL, MUL).then_inc(c_val.sem, c_val.up(V))
                V.eng.wait_ge(c_val.sem, c_val.last(V))
            V.eng.wait_ge(rms_rs.sem, rms_rs.at(V, 2))
            v.scalar_tensor_tensor(proj[:, CKV, :], proj[:, CKV, :], col(G_KV), rstd[:], MUL, MUL).then_inc(c_val.sem, c_val.up(V))
            V.eng.wait_ge(c_val.sem, c_val.last(V))
            for i in range(3):
                V.eng.wait_ge(c_h.sem, c_h.at(V, i + 1))
                v.tensor_tensor(c_lo[:, i, :], proj[:, CQ + i, :], c_hi[:, i, :].bitcast(F32), SUB).then_inc(c_l.sem, c_l.up(V))
            conformer(2 * TAPS)
            short_conv()
            for hh in range(MH + 1):
                r = qh[R0:MD, hh, :] if hh < MH else proj[R0:MD, KR, :]
                o = r if hh < MH else kh[R0:MD, 0, :]
                b = bank[4 + hh] if hh < MH else bank[0]
                V.eng.wait_ge(head_sw.sem, head_sw.at(V, hh + 1))
                v.tensor_tensor(sq[R0:MD, 0, :], b[R0:MD, :], sinA[R0:MD, :], MUL).then_inc(v_step.sem, v_step.up(V))
                v.tensor_tensor(r, r, cosA[R0:MD, :], MUL).then_inc(v_step.sem, v_step.up(V))
                V.eng.wait_ge(v_step.sem, v_step.last(V))
                v.tensor_tensor(o, r, sq[R0:MD, 0, :], ADD).then_inc(head_rope.sem, head_rope.up(V))
                V.eng.wait_ge(head_rope.sem, head_rope.last(V))
            V.eng.wait_ge(ring.done, ring.products(V, U_UKV))
            v.tensor_copy(vml[:, 0:2, :], bank[4][:].rearrange("p (i n) -> p i n", i=2)).then_inc(v_step.sem, v_step.up(V))
            V.eng.wait_ge(v_step.sem, v_step.last(V))
            v.tensor_copy(vml[:, 2:4, :], bank[5][:].rearrange("p (i n) -> p i n", i=2)).then_inc(v_ev.sem, v_ev.up(V))
            V.eng.wait_ge(v_ev.sem, v_ev.last(V))

            def beside(n):
                if n == 2:
                    V.eng.wait_ge(cfm_mm.sem, cfm_mm.at(V, 1))
                    for i in range(2):
                        raised = rms_in if i else v_step
                        v.tensor_tensor(u[:, i, :], u[:, i, :], bank[7][:], SUB).then_inc(raised.sem, raised.up(V))
                        V.eng.wait_ge(raised.sem, raised.last(V))
                if n == 3:
                    V.eng.wait_ge(rms_rs.sem, rms_rs.at(V, 3))
                    for i in range(2):
                        v.tensor_tensor(ya[:, i, :], ya[:, i, :], rstd[:], MUL).then_inc(y_val.sem, y_val.up(V))
                        V.eng.wait_ge(y_val.sem, y_val.last(V))
                if n == 5:
                    gain_v(V, 0, 0, ya)
                if n == 6:
                    V.eng.wait_ge(rms_rs.sem, rms_rs.at(V, 4))
                    for i in range(2):
                        v.scalar_tensor_tensor(u[:, i, :], u[:, i, :], col(G_CF + i), rstd[:], MUL, MUL).then_inc(cfm_ln.sem, cfm_ln.up(V))
                        V.eng.wait_ge(cfm_ln.sem, cfm_ln.last(V))
                if n == 10:
                    V.eng.wait_ge(rms_rs.sem, rms_rs.at(V, 5))
                    for i in range(2):
                        v.tensor_tensor(u[:, i, :], u[:, i, :], rstd[:], MUL).then_inc(y_val.sem, y_val.up(V))
                        V.eng.wait_ge(y_val.sem, y_val.last(V))
                if n == 11:
                    tok_ms_v(V, GVD)
                if n == 12:
                    gain_v(V, 2, 6, u)
                if n == 13:
                    og16 = flat(og[:]).rearrange("p (g n) -> p g n", n=GVD)
                    V.eng.wait_ge(tok_sd.sem, tok_sd.at(V, 1))
                    v.reciprocal(gst[:, 32:48], gst[:, 16:32]).then_inc(v_step.sem, v_step.up(V))
                    V.eng.wait_ge(v_step.sem, v_step.last(V))
                    v.tensor_tensor(og16, og16, over(gst[:, 32:48].unsqueeze(2), [P, 16, GVD]), MUL).then_inc(v_step.sem, v_step.up(V))
                    V.eng.wait_ge(v_step.sem, v_step.last(V))
                    v.tensor_tensor(og[:], og[:], over(ghead[:].unsqueeze(1), [P, NT, W]), MUL).then_inc(v_step.sem, v_step.up(V))
                    V.eng.wait_ge(v_step.sem, v_step.last(V))
                if n == 14:
                    v.tensor_tensor(og[:], og[:], gvgg[:, :, W:S], MUL).then_inc(v_step.sem, v_step.up(V))
                    V.eng.wait_ge(v_step.sem, v_step.last(V))
                    tok_ms_v(V, W)
                if n == 16:
                    tok_y_v(V, 2)

            for n in range(17):
                beside(n)
                if n < 16:
                    V.eng.wait_ge(at_s.sem, at_s.at(V, n + 1))
                    v.tensor_reduce(mmx[:, n:n + 1], bank[n % 2][:], AX.X, MAX).then_inc(v_step.sem, v_step.up(V))
                    V.eng.wait_ge(v_step.sem, v_step.last(V))
                    v.tensor_scalar(mmx[:, n:n + 1], mmx[:, n:n + 1], -MLA_SCALE, None, MUL).then_inc(at_mx.sem, at_mx.up(V))
                    V.eng.wait_ge(at_mx.sem, at_mx.last(V))
                if n > 0:
                    V.eng.wait_ge(at_t.sem, at_t.at(V, n))
                    if n > 2:
                        V.eng.wait_ge(at_o.sem, at_o.at(V, n - 2))
                    v.tensor_copy(flat(pT[(n - 1) % 2][:]), bank[2 + (n - 1) % 2][:]).then_inc(at_te.sem, at_te.up(V))
                    V.eng.wait_ge(at_te.sem, at_te.last(V))
            v.reciprocal(mrs[:], msum[:]).then_inc(v_step.sem, v_step.up(V))
            V.eng.wait_ge(v_step.sem, v_step.last(V))
            tok_lo_v(V, 0, 2)
            V.eng.wait_ge(at_o.sem, at_o.at(V, 16))
            for i in range(NT):
                v.tensor_tensor(og[:, i, :].rearrange("p (g n) -> p g n", g=MH),
                                       bank[4 + i // 2][:, i % 2 * W:i % 2 * W + W].rearrange("p (g n) -> p g n", g=MH),
                                       over(mrs[:].rearrange("p (g i) -> p g i", i=NT)[:, :, i:i + 1], [P, MH, NOPE]), MUL).then_inc(v_step.sem, v_step.up(V))
            V.eng.wait_ge(v_step.sem, v_step.last(V))
            tok_ms_v(V, W)
            tok_y_v(V, 3)
            tok_lo_v(V, 1, 4)
            norm_v(V, 0, U_OUT + KC - 1)
            v.memset(ubuf[:, :, 0:S + 2:S + 1], 0.0).then_inc(v_step.sem, v_step.up(V))
            V.eng.wait_ge(v_step.sem, V.alone(v_step.last(V)))
            with v.Fori(0, FC // 2) as i:
                V.loop("v_up", i)
                for q in range(2):
                    for x in range(2):
                        s = 2 * q + x
                        w = lambda tap: flat(pcol[:, W_UP + 22 * x + q + tap * 44:].rearrange("p (n a) -> p n a", a=1)[:, bass.ds(i * 2, 1), :])
                        V.eng.wait_ge(up_ev.sem, up_ev.at(V, i * 4 + s + 1))
                        v.tensor_scalar(cv[x][:], ubuf[:, s, 1:S + 1], w(1), None, MUL).then_inc(v_step.sem, v_step.up(V))
                        V.eng.wait_ge(v_step.sem, v_step.last(V))
                        v.scalar_tensor_tensor(cv[x][:], ubuf[:, s, 0:S], w(0), cv[x][:], MUL, ADD).then_inc(v_step.sem, v_step.up(V))
                        V.eng.wait_ge(v_step.sem, v_step.last(V))
                        v.scalar_tensor_tensor(cv[x][:], ubuf[:, s, 2:S + 2], w(2), cv[x][:], MUL, ADD).then_inc(up_cv.sem, up_cv.up(V))
                        V.eng.wait_ge(up_cv.sem, up_cv.last(V))
                    V.eng.wait_ge(up_act.sem, up_act.at(V, i * 2 + q + 1))
                    v.tensor_tensor(cv[0][:], cv[0][:], cv[1][:], MUL).then_inc(up_val.sem, up_val.up(V))
                    V.eng.wait_ge(up_val.sem, up_val.last(V))
                    V.eng.wait_ge(up_hi.sem, up_hi.at(V, i * 2 + q + 1))
                    v.tensor_tensor(g_lo[:, bass.ds(i * 2 + q, 1), :], cv[0][:].unsqueeze(1),
                                           g_hi[:, bass.ds(i * 2 + q, 1), :].bitcast(F32), SUB).then_inc(up_lo.sem, up_lo.up(V))
                    V.eng.wait_ge(up_lo.sem, up_lo.last(V))
                V.loop_end(FC // 2)
            norm_v(V, 1, U_DOWN + FC - 1)

        IX_PER_UNIT = 3
        C_POOL, C_Q, C_K, C_V, C_IQ, C_IK, C_IW, C_MQ, C_GATES = 0, 512, 1024, 1536, 2048, 2560, 2624, 2632, 3144
        CHUNKS2 = ([C_POOL + P * i for i in range(12)] + [C_IQ + P * i for i in range(4)] + [C_IK]
                   + [C_MQ + P * i for i in range(4)])
        V_CH = {c: u for c, u in zip(range(21), list(range(12)) + list(range(16, 21)) + list(range(22, 26)))}
        U2_V, U2_IW, U2_PW, U2_MK, U2_MV, U2_G, U2_OUT, U2_R = 12, 21, 26, 27, 31, 35, 83, 91
        IK, MQ0, B_GT, P_SC, IW, NROWS = 16, 17, 21, 45, 49, 50
        AH, HD, MHD, NM = 8, 64, 128, 256
        NSEL = 128
        OUT_OF, TAKEN, HIDE = -1e38, -3e38, -1e30

        two = ExitStack()
        s5 = lambda name, shape, dt=F32: sb(name, shape, dt, two)
        qk = s5("qk", [P, 8, S])
        vv = s5("vv", [P, NT, S])
        iq = s5("iq", [P, 4, S])
        b_hi, b_lo = s5("b_hi", [P, 12, S], F32R), s5("b_lo", [P, 8, S], F32R)
        last_lo = ExitStack()
        bm_lo = sb("bm_lo", [P, 4, S], F32R, last_lo)
        last_lo.close()
        ranked = s5("ranked", [P, 4 * S])
        mask_of = [ranked[:, P * i * (i + 1) // 2:P * (i + 1) * (i + 2) // 2] for i in range(NT)]
        iwc = pcol[:, 52:52 + NT * AH].rearrange("p (i h) -> p i h", i=NT)
        mmx2, msm2, mrc = pcol[:, 84:100], pcol[:, 100:116], pcol[:, 116:120]
        st8 = [pcol[:, 120 + 8 * x:128 + 8 * x] for x in range(3)]
        asum, amx, ars = pcol[:, 144:176], pcol[:, 184:216], pcol[:, 176:184]
        phase = ExitStack()
        s6 = lambda name, shape, dt=F32: sb(name, shape, dt, phase)
        up = s6("up", [P, 4, S])
        mq = s6("mq", [P, 4, S])
        mk = s6("mk", [P, 4, NM])
        mvv = s6("mvv", [P, 2, S])
        phase.close()
        phase = ExitStack()
        sc = [s6(f"sc{i}", [P, S]) for i in range(4)]
        apT = [s6(f"apT{i}", [P, NT, P]) for i in range(2)]
        otok = s6("otok", [P, S])
        phase.close()
        phase = ExitStack()
        sg, gt = [s6(f"sg{i}", [P, S]) for i in range(2)], s6("gt", [P, S])
        phase.close()
        two.close()
        moe = ExitStack()
        s7 = lambda name, shape, dt=F32: sb(name, shape, dt, moe)
        wt = [s7(f"wt{i}", [P, 4, S]) for i in range(6)]
        xb = [s7(f"xb{i}", [P, D]) for i in range(2)]
        xbT = s7("xbT", [P, KC, P])
        hs, hTm = s7("hs", [P, S]), s7("hTm", [P, 4, P])
        yb = [s7(f"yb{i}", [P, D]) for i in range(2)]
        yg = [s7(f"yg{i}", [P, D]) for i in range(4)]
        rsc, rbi = s7("rsc", [P, NT, NE]), s7("rbi", [P, NT, NE])
        scT, row128 = s7("scT", [NE, S]), s7("row128", [P, P])
        rgs, ghot, rbest = s7("rgs", [P, NT, NG]), s7("ghot", [P, NT, NG]), s7("rbest", [P, NT, 1])
        slot_ge, slot_b, slot_p = (s7(n, [P, 2 * NT, w]) for n, w in (("slot_ge", NB + 2), ("slot_b", NB + 1), ("slot_p", P)))
        hot2, d128 = s7("hot2", [P, NT, NE]), s7("d128", [P, 2 * NT])
        rtm = s7("rtm", [P, NT, 4, 8])
        oh = s7("oh", [P, 3, NT, NE])
        rbias = s7("rbias", [P, NE])
        gw = s7("gw", [P, NT, 4])
        nblk, pend, bst = (s7(n, [P, NE]) for n in ("nblk", "pend", "bst"))
        used, turns = s7("used", [P, NB // 2]), s7("turns", [P, 1])
        rtmp = s7("rtmp", [P, NT, NE])
        dest, desti = s7("dest", [P, 2, NT]), s7("desti", [P, 2, NT], U32)
        bcmp = s7("bcmp", [P, NB + 1, NE])
        bef, bei = s7("bef", [P, NB + 1]), s7("bei", [P, NB + 1], I32)
        slots = s7("slots", [P, NB + 1], U32)
        sid = [s7(f"sid{i}", [P, 1], U32) for i in range(2)]
        moe.close()
        memrow = gb
        om = gb[:, :, :].rearrange("p a (b n) -> p (a b) n", n=S)
        memT_hi, memT_lo = (b[:, 4:8, :].rearrange("p c (x m) -> p (c x) m", x=2) for b in (b_hi, b_lo))
        pd = om
        work = [flat(mk[:, x:x + 2, :]) for x in (0, 2)]
        prow_b = vv[:, 0, 0:P]
        brow = flat(mvv[0:1, :, :])
        iwT = mvv[0:AH, 1, :]
        rel = [up[:, x, :] for x in range(2)]
        mem_p = [up[:, 2, x * NM:x * NM + NM] for x in range(2)]
        mem_pT = [up[:, 3, x * NM:x * NM + NM] for x in range(2)]
        ikd, turned = cosA, sinA
        h_dram = nc.dram_tensor("h_rows", (S, D), F32).ap()

        mem_tr, mem_hi, mem_lo, v2_ev, iw_fm, iw_tr, iw_ev, mk_ev, mv_ev, pool_d, pool_dh, pool_dl, pool_hi, pool_lo = (signal(n) for n in (
            "mem_tr", "mem_hi", "mem_lo", "v2_ev", "iw_fm", "iw_tr", "iw_ev", "mk_ev", "mv_ev", "pool_d", "pool_dh", "pool_dl", "pool_hi", "pool_lo"))
        ix_s, ix_rel, ix_use, a_sc, a_te, a_or, a_ot, a_oh, a_ol = (signal(n) for n in (
            "ix_s", "ix_rel", "ix_use", "a_sc", "a_te", "a_or", "a_ot", "a_oh", "a_ol"))
        m_s, m_mx, m_p, m_t, m_te, m_o, m_or, m_ot, m_oh, m_ol = (signal(n) for n in (
            "m_s", "m_mx", "m_p", "m_t", "m_te", "m_o", "m_or", "m_ot", "m_oh", "m_ol"))
        gt_sig, gt_use, mg_hi, mg_lo, rt_sc, rt_oh, rt_rank, rt_dest, be_ok, sid_ok, rt_tr, slot_oh, slot_mm = (signal(n) for n in (
            "gt_sig", "gt_use", "mg_hi", "mg_lo", "rt_sc", "rt_oh", "rt_rank", "rt_dest", "be_ok", "sid_ok", "rt_tr", "slot_oh", "slot_mm"))
        x_tr, x_ev, act_h, h_val, h_tr, h_ev, y_ev, y_free, yg_use, wt_done = (signal(n) for n in (
            "x_tr", "x_ev", "act_h", "h_val", "h_tr", "h_ev", "y_ev", "y_free", "yg_use", "wt_done"))
        h_st, rb_ld, y_st = (signal(n, 16) for n in ("h_st", "rb_ld", "y_st"))
        PAR2 = 11
        wt_ld = [signal(f"wt_ld{i}", 16) for i in range(6)]
        xbl = [signal(f"xb_ld{i}", 16) for i in range(2)]
        ygl = [signal(f"yg_ld{i}", 16) for i in range(4)]

        def loads2(E):
            l, sp = E.layer, E.eng
            w = t["w_in_2"][bass.ds(l, 1)].rearrange("o (k p) n -> (o p) k n", p=P)

            def wide(j, c):
                dst = cols3(j)
                ring.load(E, j, [(dst[:, x:x + 4, :], w[:, x:x + 4, c:c + P]) for x in (0, 4)])

            def pairs(j0, src, c0):
                for j in range(4):
                    dst = ring.raw[(j0 + j) % RAW][:, :].rearrange("p (k n) -> p k n", k=2)
                    ring.load(E, j0 + j, [(dst[:, k:k + 1, :], src[:, 2 * j + k:2 * j + k + 1, c0:c0 + S]) for k in range(2)])

            for j in range(12):
                wide(j, CHUNKS2[j])
            pairs(U2_V, w, C_V)
            for j in range(16, 20):
                wide(j, CHUNKS2[j - 4])
            dst = cols3(20)
            ring.load(E, 20, [(dst[:, :, x:x + HD], w[:, :, C_IK:C_IK + HD]) for x in (0, HD)])
            dst = ring.raw[U2_IW % RAW][:, 0:64].rearrange("p (k c) -> p k c", k=KC)
            ring.load(E, U2_IW, [(dst[:, x:x + 4, :], w[:, x:x + 4, C_IW:C_IW + AH]) for x in (0, 4)])
            for j in range(4):
                wide(22 + j, C_MQ + P * j)
            pw = t["pool_w_2"][bass.ds(l, 1)].rearrange("o g c e -> (o c) g e")
            dst = ring.raw[U2_PW % RAW][:, 0:S].rearrange("p (g e) -> p g e", g=4)
            ring.load(E, U2_PW, [(dst[:, x:x + 2, :], pw[:, x:x + 2, :]) for x in (0, 2)])
            wm = t["w_mem_kv_2"][bass.ds(l, 1)].rearrange("o (k p) n -> (o p) k n", p=P)
            for j in range(4):
                dst = cols3(U2_MK + j)
                ring.load(E, U2_MK + j, [(dst[:, x:x + 4, :], wm[:, x:x + 4, j * P:j * P + P]) for x in (0, 4)])
            pairs(U2_MV, wm, S)
            wb = [t["w_br_2"][bass.ds(l, 1), n, :, :].rearrange("o (k p) n -> (o p) k n", p=P) for n in range(3)]
            with sp.Fori(0, 4) as i:
                for dd in range(2):
                    for n in range(3):
                        j = U2_G + 6 * dd + 2 * n
                        dst = cols3(j)
                        ring.load(E, j, [(dst[:, x:x + 4, :], w[:, x:x + 4, bass.ds(i * (2 * P) + (C_GATES + n * D + dd * P), P)])
                                         for x in (0, 4)], turn=i, size=12)
                        dst = ring.raw[(j + 1) % RAW][:, 0:S].rearrange("p (k c) -> p k c", k=4)
                        ring.load(E, j + 1, [(dst[:, x:x + 2, :], wb[n][:, x:x + 2, bass.ds(i * (2 * P) + dd * P, P)])
                                             for x in (0, 2)], turn=i, size=12)
            rows_unit(E, U2_OUT, KC, t["w_out_2"], l)
            wr = t["w_router_2"].rearrange("(k p) n -> p k n", p=P)
            dst = ring.raw[U2_R % RAW][:, 0:P].rearrange("p (k c) -> p k c", k=KC)
            ring.load(E, U2_R, [(dst[:, x:x + 4, :], wr[:, x:x + 4, :]) for x in (0, 4)])
            for i in range(NT):
                E.eng.wait_ge(norm_z.sem, E.alone(norm_z.at(E, i + 1)))
                sp.dma_start(h_dram[i * P:i * P + P, :], h[:, i, :]).then_inc(h_st.sem, h_st.up(E))
            E.eng.wait_ge(be_ok.sem, E.alone(be_ok.at(E, 1)))
            E.pace(pace)
            w1, w3 = (t[n].rearrange("l e (k p) n -> (l e) p k n", p=P) for n in ("w1_2", "w3_2"))
            w2 = t["w2_2"].rearrange("l e (k p) n -> (l e) p k n", p=P)
            with sp.Fori(0, NB // 2) as bb:
                E.loop("sp_moe", bb)
                with E.eng.If(bb < E.turns):
                    for q in range(2):
                        e = sp.value_load(bei[0:1, bass.ds(bb * 2 + q, 1)], min_val=0, max_val=NE - 1)
                        le = sp.snap(l * NE + e)
                        for i in range(6):
                            src = (w1, w3, w2)[i // 2]
                            if i < 4:
                                src = src[bass.ds(le, 1), :, 4 * (i % 2):4 * (i % 2) + 4, :].rearrange("o p k n -> (o p) k n")
                                dst = wt[i][:]
                            else:
                                src = src[bass.ds(le, 1), :, 2 * (i % 2):2 * (i % 2) + 2, :].rearrange("o p k n -> (o p) k n")
                                dst = wt[i][:].rearrange("p (k x) n -> p k (x n)", k=2)
                            if i == 2:
                                E.eng.wait_ge(xbl[q].sem, E.alone(xbl[q].at(E, bb + 1)))
                            E.eng.wait_ge(wt_done.sem, E.alone(wt_done.at(E, bb * 12 + (6 * q + i + 1 - 6))))
                            sp.dma_start(dst, src).then_inc(wt_ld[i].sem, wt_ld[i].up(E))
                E.loop_end(NB // 2)

        def splits2(G):
            g = G.eng
            widths = {U2_IW: 64, U2_PW: S}
            for j in range(U2_G):
                ring.part(G, j, width=widths.get(j, 1024))
            with g.Fori(0, 4) as i:
                for s in range(12):
                    ring.part(G, U2_G + s, turn=i, size=12, width=S if s % 2 else 1024)
            for j in range(U2_OUT, U2_R):
                ring.part(G, j)
            ring.part(G, U2_R, width=P)
            G.eng.wait_ge(rt_dest.sem, G.alone(rt_dest.at(G, 1)))
            G.pace(pace)
            G.eng.wait_ge(h_st.sem, G.alone(h_st.at(G, 4)))

            def gather(b, x):
                g.tensor_copy(sid[x][:], slots[:, bass.ds(b, 1)]).then_inc(sid_ok.sem, sid_ok.up(G))
                G.eng.wait_ge(sid_ok.sem, G.alone(sid_ok.last(G)))
                g.indirect_dma_start(
                    out=xb[x][:], out_offset=None, in_=h_dram,
                    in_offset=bass.IndirectOffsetOnAxis(ap=sid[x][:, 0:1], axis=0)).then_inc(xbl[x].sem, xbl[x].up(G))

            G.eng.wait_ge(y_zero.sem, G.alone(y_zero.at(G, 0)))
            gather(0, 0)
            with g.Fori(0, NB // 2) as bb:
                G.loop("g_moe", bb)
                with G.eng.If(bb < G.turns):
                    for q in range(2):
                        G.eng.wait_ge(x_tr.sem, G.alone(x_tr.at(G, bb * 4 + 2 * q)))
                        gather(bb * 2 + (q + 1), 1 - q)
                        G.eng.wait_ge(y_ev.sem, G.alone(y_ev.at(G, bb * 4 + (2 * q + 2))))
                        g.dma_start(y_dram[bass.ds(bb * (2 * P) + q * P, P), :], yb[q][:]).then_inc(y_st.sem, y_st.up(G))
                        G.eng.wait_ge(y_st.sem, G.alone(y_st.last(G)))
                        g.nop().then_inc(y_free.sem, y_free.up(G))
                G.loop_end(NB // 2)
            for n in range(8):
                if n >= 4:
                    G.eng.wait_ge(yg_use.sem, G.alone(yg_use.at(G, n - 2 if n % 2 == 0 else n - 3)))
                g.indirect_dma_start(
                    out=yg[n % 4][:], out_offset=None, in_=y_dram,
                    in_offset=bass.IndirectOffsetOnAxis(ap=desti[:, n % 2, n // 2:n // 2 + 1], axis=0)).then_inc(ygl[n % 4].sem, ygl[n % 4].up(G))

        def tensor2(T):
            pe = T.eng
            T.eng.wait_ge(norm_lo.sem, norm_lo.at(T, 0))

            def vectors_and_memory():
                T.eng.wait_ge(par_ld.sem, T.alone(par_ld.at(T, PAR2)))
                pe.transpose(bank[7][:, 0:NROWS], prow_b[0:NROWS, :], ident[0:NROWS, 0:NROWS]).then_inc(par_tr.sem, par_tr.up(T))
                for b in range(4):
                    if b == 3:
                        T.eng.wait_ge(par_col.sem, par_col.at(T, 1))
                    for k in range(2):
                        for m in range(2):
                            last = pe.transpose(bank[4 + b][:, k * NM + m * P:k * NM + m * P + P],
                                                memrow[:, m, (2 * b + k) * P:(2 * b + k + 1) * P], ident)
                    last.then_inc(mem_tr.sem, mem_tr.up(T))

            def swap(r):
                c = r + 4
                T.eng.wait_ge(proj_ev.sem, proj_ev.at(T, c + 1))
                if r >= 2:
                    T.eng.wait_ge(head_rope.sem, head_rope.at(T, r - 1))
                src = qk[:, r, :] if r < 8 else iq[:, r - 8, :] if r < 12 else ikd[:]
                pe.matmul(bank[4 + r % 2][:], konst[:, K_SWB:K_SWB + P], src, start=True, stop=True).then_inc(head_sw.sem, head_sw.up(T))

            for c in range(21):
                if c == 2:
                    vectors_and_memory()
                if c == 5:
                    T.eng.wait_ge(mem_lo.sem, mem_lo.at(T, 4))
                if c == 12:
                    T.eng.wait_ge(proj_ev.sem, proj_ev.at(T, 12))
                    for j in range(4):
                        wh, wl = ring.weights(T, U2_V + j)
                        for i in range(NT):
                            if j == 0:
                                pe.matmul(bank[i][:], ones[0:1, :], brow[:, 0:S], start=True, stop=False)
                            for kk in range(2):
                                k, cs, n = 2 * j + kk, slice(i * P, i * P + P), slice(kk * S, kk * S + S)
                                last = triple(pe, bank[i][:], xT_hi[:, k, cs], xT_lo[:, k, cs], wh[:, n], wl[:, n], False, k == 7)
                        last.then_inc(ring.done, 1)
                    T.eng.wait_ge(v2_ev.sem, v2_ev.at(T, 4))
                elif c >= 4:
                    T.eng.wait_ge(proj_ev.sem, proj_ev.at(T, c - 3))
                if c == 17:
                    wh, wl = (w[:, 0:64].rearrange("p (k c) -> p k c", k=KC) for w in ring.weights(T, U2_IW))
                    for k in range(KC):
                        last = triple(pe, bank[6][0:AH, :], wh[:, k, :], wl[:, k, :], xT_hi[:, k, :], xT_lo[:, k, :], k == 0, k == 7)
                    last.then_inc(ring.done, 1)
                if c == 19:
                    T.eng.wait_ge(iw_fm.sem, T.alone(iw_fm.at(T, 1)))
                    for i in range(NT):
                        last = pe.transpose(bank[7][:, AH * i:AH * i + AH], iwT[:, i * P:i * P + P], ident[0:AH, 0:AH])
                    last.then_inc(iw_tr.sem, iw_tr.up(T))
                chunk(T, ring, V_CH[c], bank[c % 4])
                if 5 <= c < 18:
                    swap(c - 5)
            wh, wl = (w[:, 0:S].rearrange("p (g e) -> p g e", g=4) for w in ring.weights(T, U2_PW))
            T.eng.wait_ge(proj_ev.sem, proj_ev.at(T, 21))
            T.eng.wait_ge(pool_dl.sem, pool_dl.at(T, 4))
            for g4 in range(4):
                last = triple(pe, bank[g4][:], wh[:, g4, :], wl[:, g4, :], b_hi[:, g4, :], b_lo[:, g4, :], True, True)
            last.then_inc(ring.done, 1)
            T.eng.wait_ge(head_rope.sem, head_rope.at(T, 13))
            T.eng.wait_ge(pool_lo.sem, pool_lo.at(T, 4))

            def index_scores(j):
                for n in range(IX_PER_UNIT * j, IX_PER_UNIT * (j + 1)):
                    i, hh = 1 + n // AH, n % AH
                    r = slice(64 * (hh % 2), 64 * (hh % 2) + 64)
                    if n >= 2:
                        T.eng.wait_ge(ix_rel.sem, ix_rel.at(T, n - 1))
                    pe.matmul(bank[n % 2][:, 0:(i + 1) * P], iq[r, hh // 2, i * P:i * P + P], ikd[r, 0:(i + 1) * P],
                                     start=True, stop=True).then_inc(ix_s.sem, ix_s.up(T))

            for j in range(4):
                if j >= 2:
                    T.eng.wait_ge(mk_ev.sem, mk_ev.at(T, j - 1))
                chunk(T, ring, U2_MK + j, bank[4 + j % 2], n=NM, src=tuple([m[:, k, :] for k in range(KC)] for m in (memT_hi, memT_lo)))
                index_scores(j)
            T.eng.wait_ge(iw_ev.sem, iw_ev.at(T, 1))
            for j in range(4):
                wh, wl = ring.weights(T, U2_MV + j)
                for m in range(2):
                    for kk in range(2):
                        k, cs, n = 2 * j + kk, slice(m * P, m * P + P), slice(kk * S, kk * S + S)
                        last = triple(pe, bank[6 + m][:], memT_hi[:, k, cs], memT_lo[:, k, cs], wh[:, n], wl[:, n], k == 0, k == 7)
                last.then_inc(ring.done, 1)
                index_scores(4 + j)
            T.eng.wait_ge(mv_ev.sem, mv_ev.at(T, 2))
            T.eng.wait_ge(mk_ev.sem, mk_ev.at(T, 4))
            T.eng.wait_ge(ix_rel.sem, ix_rel.at(T, 3 * AH))
            for n in range(18):
                if n < 16:
                    i, hh = n // 4, n % 4
                    if n >= 2:
                        T.eng.wait_ge(m_p.sem, m_p.at(T, n - 1))
                    pe.matmul(bank[n % 2][:, 0:NM], mq[:, hh, i * P:i * P + P], mk[:, hh, :], start=True, stop=True).then_inc(m_s.sem, m_s.up(T))
                if 0 < n < 17:
                    m = n - 1
                    T.eng.wait_ge(m_p.sem, m_p.at(T, m + 1))
                    for k in range(2):
                        last = pe.transpose(bank[2 + m % 2][:, k * P:k * P + P], mem_p[m % 2][:, k * P:k * P + P], ident)
                    last.then_inc(m_t.sem, m_t.up(T))
                if n > 1:
                    m = n - 2
                    i, hh = m // 4, m % 4
                    T.eng.wait_ge(m_te.sem, m_te.at(T, m + 1))
                    if hh == 0 and i >= 2:
                        T.eng.wait_ge(m_or.sem, m_or.at(T, i - 1))
                    for k in range(2):
                        last = pe.matmul(bank[4 + i % 2][:, hh * P:hh * P + P], mem_pT[m % 2][:, k * P:k * P + P],
                                         mvv[:, k, hh * P:hh * P + P], start=k == 0, stop=k == 1)
                    last.then_inc(m_o.sem, m_o.up(T))
            T.eng.wait_ge(m_or.sem, m_or.at(T, 4))
            for s in range(NT * AH + 5):
                if s < NT * AH:
                    i, n = s // AH, s % AH
                    r, nk = slice(64 * (n % 2), 64 * (n % 2) + 64), (i + 1) * P
                    if s >= 4:
                        T.eng.wait_ge(a_sc.sem, a_sc.at(T, s - 3))
                    pe.matmul(bank[s % 4][:, 0:nk], qk[r, n // 2, i * P:i * P + P], qk[r, 4 + n // 2, 0:nk], start=True, stop=True).then_inc(at_s.sem, at_s.up(T))
                if 0 <= s - 2 < NT * AH:
                    k = s - 2
                    T.eng.wait_ge(at_p.sem, at_p.at(T, k + 1))
                    for x in range(k // AH + 1):
                        last = pe.transpose(bank[4 + k % 2][:, x * P:x * P + P], sc[k % 4][:, x * P:x * P + P], ident)
                    last.then_inc(at_t.sem, at_t.up(T))
                if 0 <= s - 3 < NT * AH:
                    k = s - 3
                    i, m = k // AH, k % AH
                    T.eng.wait_ge(a_te.sem, a_te.at(T, k + 1))
                    if m == 0 and i >= 2:
                        T.eng.wait_ge(a_ol.sem, a_ol.at(T, i - 1))
                    for x in range(i + 1):
                        last = pe.matmul(bank[6 + i % 2][:, m * HD:m * HD + HD], apT[k % 2][:, x, :], vv[:, x, m * HD:m * HD + HD],
                                         start=x == 0, stop=x == i)
                    last.then_inc(at_o.sem, at_o.up(T))
                if s >= 5 and (s - 5) % AH == AH - 1:
                    i = (s - 5) // AH
                    T.eng.wait_ge(a_or.sem, a_or.at(T, i + 1))
                    for c in range(4):
                        last = pe.transpose(bank[6 + i % 2][:, c * P:c * P + P], otok[:, c * P:c * P + P], ident)
                    last.then_inc(a_ot.sem, a_ot.up(T))
            T.eng.wait_ge(a_ol.sem, a_ol.at(T, NT))
            for i in range(NT):
                if i >= 2:
                    T.eng.wait_ge(m_ol.sem, m_ol.at(T, i - 1))
                for c in range(4):
                    last = pe.transpose(bank[6 + i % 2][:, c * P:c * P + P], om[:, i, c * P:c * P + P], ident)
                last.then_inc(m_ot.sem, m_ot.up(T))
            T.eng.wait_ge(m_ol.sem, T.alone(m_ol.at(T, 4)))
            with pe.Fori(0, 4) as i:
                for s in range(0, 12, 2):
                    u6 = s // 2
                    T.eng.wait_ge(gt_use.sem, gt_use.at(T, i * 6 + (u6 - 1)))
                    chunk(T, ring, U2_G + s, bank[2 * (u6 % 2)], turn=i, size=12)
                    n = u6 % 3
                    xh = [b_hi[:, 4 * n + k, :] for k in range(4)]
                    xl = [bm_lo[:, k, :] if n == 2 else b_lo[:, 4 * n + k, :] for k in range(4)]
                    chunk(T, ring, U2_G + s + 1, bank[2 * (u6 % 2) + 1], turn=i, size=12, kc=4, src=(xh, xl))
            rows_products(T, U2_OUT, KC, xT_hi, xT_lo, mg_lo)
            norm_pe(T, 0)
            T.eng.wait_ge(norm_lo.sem, norm_lo.at(T, 8))
            wh, wl = (w[:, 0:P].rearrange("p (k e) -> p k e", k=KC) for w in ring.weights(T, U2_R))
            for k in range(KC):
                last = triple(pe, bank[0][0:NE, :], wh[:, k, :], wl[:, k, :], xT_hi[:, k, :], xT_lo[:, k, :], k == 0, k == 7)
            last.then_inc(ring.done, 1)
            T.eng.wait_ge(rt_sc.sem, T.alone(rt_sc.at(T, 1)))
            for i in range(NT):
                last = pe.transpose(bank[2][:, NE * i:NE * i + NE], scT[:, i * P:i * P + P], ident[0:NE, 0:NE])
            last.then_inc(rt_tr.sem, rt_tr.up(T))
            T.eng.wait_ge(rt_oh.sem, rt_oh.at(T, 1))
            pe.matmul(bank[1][:, 0:NT * NE], konst[:, K_TRF:K_TRF + P], flat(oh[:, 2, :, :]), start=True, stop=True)
            pe.matmul(bank[1][:, NT * NE:2 * NT * NE], ones[:], flat(oh[:, 2, :, :]), start=True, stop=True).then_inc(rt_rank.sem, rt_rank.up(T))
            T.eng.wait_ge(slot_oh.sem, slot_oh.at(T, 1))
            for n in range(2 * NT):
                last = pe.matmul(bank[3][:, 0:NB + 1], slot_p[:, n, :], slot_b[:, n, :], start=n == 0, stop=n == 2 * NT - 1)
            last.then_inc(slot_mm.sem, slot_mm.up(T))
            T.eng.wait_ge(rt_dest.sem, T.alone(rt_dest.at(T, 1)))
            T.pace(pace)

            def transposed(b, x):
                for y in range(2):
                    for k in range(4):
                        last = pe.transpose(bank[y][:, k * P:k * P + P], xb[x][:, (4 * y + k) * P:(4 * y + k + 1) * P], ident)
                    last.then_inc(x_tr.sem, x_tr.up(T))

            T.eng.wait_ge(xbl[0].sem, xbl[0].at(T, 1))
            transposed(0, 0)
            T.eng.wait_ge(x_ev.sem, T.alone(x_ev.at(T, 2)))
            with pe.Fori(0, NB // 2) as bb:
                T.loop("t_moe", bb)
                with T.eng.If(bb < T.turns):
                    for q in range(2):
                        T.eng.wait_ge(x_ev.sem, x_ev.at(T, bb * 4 + (2 * q + 2)))
                        for i in range(4):
                            T.eng.wait_ge(wt_ld[i].sem, wt_ld[i].at(T, bb * 2 + (q + 1)))
                            for k in range(4):
                                last = pe.matmul(bank[2 + i // 2][:], xbT[:, 4 * (i % 2) + k, :], wt[i][:, k, :],
                                                 start=i % 2 == 0 and k == 0, stop=i % 2 == 1 and k == 3)
                            last.then_inc(wt_done.sem, wt_done.up(T))
                        T.eng.wait_ge(xbl[1 - q].sem, xbl[1 - q].at(T, bb + (1 + q)))
                        transposed(None, 1 - q)
                        T.eng.wait_ge(h_val.sem, h_val.at(T, bb * 2 + (q + 1)))
                        for k in range(4):
                            last = pe.transpose(bank[4][:, k * P:k * P + P], hs[:, k * P:k * P + P], ident)
                        last.then_inc(h_tr.sem, h_tr.up(T))
                        T.eng.wait_ge(y_ev.sem, y_ev.at(T, bb * 4 + 2 * q))
                        T.eng.wait_ge(h_ev.sem, h_ev.at(T, bb * 2 + (q + 1)))
                        for i in range(2):
                            T.eng.wait_ge(wt_ld[4 + i].sem, wt_ld[4 + i].at(T, bb * 2 + (q + 1)))
                            for k in range(2):
                                for x in range(2):
                                    last = pe.matmul(bank[5 + x][:], hTm[:, 2 * i + k, :], wt[4 + i][:, 2 * k + x, :],
                                                     start=i == 0 and k == 0, stop=i == 1 and k == 1)
                            last.then_inc(wt_done.sem, wt_done.up(T))
                T.loop_end(NB // 2)
            T.eng.wait_ge(x_ev.sem, x_ev.at(T, T.turns * 4 + 2))
            T.eng.wait_ge(y_ev.sem, y_ev.at(T, T.turns * 4))
            norm_pe(T, 1)

        def scalar2(A):
            act, l = A.eng, A.layer
            pl = par_ld
            b2 = lambda c, n: t["b_in_2"][bass.ds(l, 1), c:c + n * P].rearrange("o (c p) -> (o c) p", p=P)
            act.dma_start(prow_b[0:12, :], b2(0, 12)).then_inc(pl.sem, pl.up(A))
            act.dma_start(prow_b[12:16, :], b2(C_IQ, 4)).then_inc(pl.sem, pl.up(A))
            for x in (0, HD):
                act.dma_start(prow_b[IK:IK + 1, x:x + HD], t["b_in_2"][bass.ds(l, 1), C_IK:C_IK + HD]).then_inc(pl.sem, pl.up(A))
            act.dma_start(prow_b[IW:IW + 1, 0:AH], t["b_in_2"][bass.ds(l, 1), C_IW:C_IW + AH]).then_inc(pl.sem, pl.up(A))
            act.dma_start(prow_b[MQ0:MQ0 + 4, :], b2(C_MQ, 4)).then_inc(pl.sem, pl.up(A))
            act.dma_start(prow_b[B_GT:B_GT + 24, :], b2(C_GATES, 24)).then_inc(pl.sem, pl.up(A))
            act.dma_start(prow_b[P_SC:P_SC + 4, :], t["pool_scale_2"][bass.ds(l, 1), :].rearrange("o (c p) -> (o c) p", p=P)).then_inc(pl.sem, pl.up(A))
            act.dma_start(brow[:, 0:S], t["b_in_2"][bass.ds(l, 1), C_V:C_V + S]).then_inc(pl.sem, pl.up(A))
            mem = t["mem_2"].rearrange("o (m p) d -> (o p) m d", p=P)
            for m in range(2):
                act.dma_start(memrow[:, m, :], mem[:, m, :]).then_inc(pl.sem, pl.up(A))
            for b in range(4):
                A.eng.wait_ge(mem_tr.sem, mem_tr.at(A, b + 1))
                act.activation(memT_hi[:, 2 * b:2 * b + 2, :], bank[4 + b][:].rearrange("p (k m) -> p k m", k=2), ACT.Copy).then_inc(mem_hi.sem, mem_hi.up(A))
            A.eng.wait_ge(par_col.sem, par_col.at(A, 1))
            pdest = [up[:, c, :] for c in range(4)] + [qk[:, c, :] for c in range(8)] + [iq[:, c, :] for c in range(4)] + [ikd[:]] \
                + [mq[:, c, :] for c in range(4)]
            for c in range(21):
                if c == 12:
                    A.eng.wait_ge(ring.done, ring.products(A, U2_V + 3))
                    for i in range(NT):
                        act.activation(vv[:, i, :], bank[i][:], ACT.Copy).then_inc(v2_ev.sem, v2_ev.up(A))
                A.eng.wait_ge(ring.done, ring.products(A, V_CH[c]))
                act.activation(pdest[c], bank[c % 4][:], ACT.Identity, bias=col(c)).then_inc(proj_ev.sem, proj_ev.up(A))
                if c == 16:
                    A.eng.wait_ge(ring.done, ring.products(A, U2_IW))
                    act.activation(iwT, bank[6][0:AH, :], ACT.Identity, bias=pcol[0:AH, IW:IW + 1]).then_inc(iw_fm.sem, iw_fm.up(A))
            for g4 in range(4):
                A.eng.wait_ge(pool_d.sem, pool_d.at(A, g4 + 1))
                act.activation(b_hi[:, g4, :], pd[:, g4, :], ACT.Copy).then_inc(pool_dh.sem, pool_dh.up(A))
            A.eng.wait_ge(ring.done, ring.products(A, U2_PW))
            for g4 in range(4):
                act.activation(b_hi[:, g4, :], bank[g4][:], ACT.Copy, scale=col(P_SC + g4)).then_inc(pool_hi.sem, pool_hi.up(A))
            for n in range(3 * AH):
                if n % IX_PER_UNIT == 0 and n // IX_PER_UNIT < 4:
                    j = n // IX_PER_UNIT
                    A.eng.wait_ge(ring.done, ring.products(A, U2_MK + j))
                    act.activation(mk[:, j, :], bank[4 + j % 2][:, 0:NM], ACT.Copy).then_inc(mk_ev.sem, mk_ev.up(A))
                nk = (2 + n // AH) * P
                A.eng.wait_ge(ix_s.sem, ix_s.at(A, n + 1))
                if n >= 2:
                    A.eng.wait_ge(ix_use.sem, ix_use.at(A, n - 1))
                act.activation(rel[n % 2][:, 0:nk], bank[n % 2][:, 0:nk], ACT.Relu, scale=HD ** -0.5).then_inc(ix_rel.sem, ix_rel.up(A))
            A.eng.wait_ge(ring.done, ring.products(A, U2_MV + 3))
            for m in range(2):
                act.activation(mvv[:, m, :], bank[6 + m][:], ACT.Copy).then_inc(mv_ev.sem, mv_ev.up(A))
            for n in range(17):
                if n:
                    A.eng.wait_ge(m_t.sem, m_t.at(A, n))
                    if n >= 3:
                        A.eng.wait_ge(m_o.sem, m_o.at(A, n - 2))
                    act.activation(mem_pT[(n - 1) % 2], bank[2 + (n - 1) % 2][:, 0:NM], ACT.Copy).then_inc(m_te.sem, m_te.up(A))
                if n == 16:
                    break
                A.eng.wait_ge(m_mx.sem, m_mx.at(A, n + 1))
                if n >= 2:
                    A.eng.wait_ge(m_t.sem, m_t.at(A, n - 1))
                act.activation(mem_p[n % 2], bank[n % 2][:, 0:NM], ACT.Exp, bias=mmx2[:, n:n + 1], scale=MHD ** -0.5,
                                      accum_out=msm2[:, n:n + 1]).then_inc(m_p.sem, m_p.up(A))
            for s in range(NT * AH + 3):
                if s < NT * AH:
                    nk = (s // AH + 1) * P
                    A.eng.wait_ge(at_mx.sem, at_mx.at(A, s + 1))
                    act.activation(sc[s % 4][:, 0:nk], sc[s % 4][:, 0:nk], ACT.Exp, bias=amx[:, s:s + 1],
                                          accum_out=asum[:, s:s + 1]).then_inc(at_p.sem, at_p.up(A))
                if 0 < s <= NT * AH:
                    k = s - 1
                    nk = (k // AH + 1) * P
                    A.eng.wait_ge(at_t.sem, at_t.at(A, k + 1))
                    if k >= 2:
                        A.eng.wait_ge(at_o.sem, at_o.at(A, k - 1))
                    act.activation(flat(apT[k % 2][:])[:, 0:nk], bank[4 + k % 2][:, 0:nk], ACT.Copy).then_inc(a_te.sem, a_te.up(A))
                if s >= 3 and (s - 3) % AH == AH - 1:
                    i = (s - 3) // AH
                    A.eng.wait_ge(a_ot.sem, a_ot.at(A, i + 1))
                    act.activation(b_hi[:, 4:8, i * P:i * P + P], bank[6 + i % 2][:].rearrange("p (c n) -> p c n", c=4), ACT.Copy).then_inc(a_oh.sem, a_oh.up(A))
            for i in range(NT):
                A.eng.wait_ge(m_ot.sem, m_ot.at(A, i + 1))
                act.activation(b_hi[:, 8:12, i * P:i * P + P], bank[6 + i % 2][:].rearrange("p (c n) -> p c n", c=4), ACT.Copy).then_inc(m_oh.sem, m_oh.up(A))
            load_gb(A, t["ln1_g_2"][bass.ds(l, 1), :], t["ln1_b_2"][bass.ds(l, 1), :])
            with act.Fori(0, 4) as i:
                A.loop("a_gates", i)
                for u6 in range(6):
                    n, dd = u6 % 3, u6 // 3
                    A.eng.wait_ge(ring.done, ring.products(A, U2_G + 2 * u6, turn=i, size=12))
                    A.eng.wait_ge(gt_use.sem, gt_use.at(A, i * 6 + (u6 - 1)))
                    bias = flat(pcol[:, B_GT + 8 * n + dd:].rearrange("p (n a) -> p n a", a=1)[:, bass.ds(i * 2, 1), :])
                    act.activation(sg[u6 % 2][:], bank[2 * (u6 % 2)][:], ACT.Sigmoid, bias=bias).then_inc(gt_sig.sem, gt_sig.up(A))
                A.loop_end(4)
            for k in range(KC):
                A.eng.wait_ge(gt_use.sem, gt_use.at(A, 24))
                act.activation(xT_hi[:, k, :], qk[:, k, :], ACT.Copy).then_inc(mg_hi.sem, mg_hi.up(A))
            norm_a(A, 0)
            load_gb(A, t["ln2_g_2"][bass.ds(l, 1), :], t["ln2_b_2"][bass.ds(l, 1), :])
            act.dma_start(rbias[:], over(t["router_bias_2"].rearrange("(o n) -> o n", o=1), [P, NE])).then_inc(rb_ld.sem, rb_ld.up(A))
            act.dma_start(row128[:], t["konst"][:, K_END:K_END + P]).then_inc(rb_ld.sem, rb_ld.up(A))
            A.eng.wait_ge(ring.done, ring.products(A, U2_R))
            act.activation(scT[:], bank[0][0:NE, :], ACT.Sigmoid).then_inc(rt_sc.sem, rt_sc.up(A))

            def evacuated(k):
                for y in range(2):
                    A.eng.wait_ge(x_tr.sem, x_tr.at(A, k + y))
                    act.activation(xbT[:, 4 * y:4 * y + 4, :], bank[y][:].rearrange("p (k t) -> p k t", k=4), ACT.Copy).then_inc(x_ev.sem, x_ev.up(A))

            A.eng.wait_ge(rt_dest.sem, A.alone(rt_dest.at(A, 1)))
            A.pace(pace)
            evacuated(1)
            A.eng.wait_ge(x_ev.sem, x_ev.last(A))
            with act.Fori(0, NB // 2) as bb:
                A.loop("a_moe", bb)
                with A.eng.If(bb < A.turns):
                    for q in range(2):
                        A.eng.wait_ge(wt_done.sem, wt_done.at(A, bb * 12 + (6 * q + 2)))
                        A.eng.wait_ge(h_tr.sem, h_tr.at(A, bb * 2 + q))
                        act.activation(hs[:], bank[2][:], ACT.Silu).then_inc(act_h.sem, act_h.up(A))
                        A.eng.wait_ge(wt_done.sem, wt_done.at(A, bb * 12 + (6 * q + 4)))
                        evacuated(bb * 4 + (2 * q + 3))
                        A.eng.wait_ge(h_tr.sem, h_tr.at(A, bb * 2 + (q + 1)))
                        act.activation(flat(hTm[:]), bank[4][:], ACT.Copy).then_inc(h_ev.sem, h_ev.up(A))
                A.loop_end(NB // 2)
            norm_a(A, 1)

        def vector2(V):
            v = V.eng
            V.eng.wait_ge(par_tr.sem, par_tr.at(V, 1))
            v.tensor_copy(pcol[:, 0:NROWS], bank[7][:, 0:NROWS]).then_inc(par_col.sem, par_col.up(V))
            V.eng.wait_ge(par_col.sem, par_col.last(V))
            for b in range(4):
                V.eng.wait_ge(mem_hi.sem, mem_hi.at(V, b + 1))
                v.tensor_tensor(memT_lo[:, 2 * b:2 * b + 2, :], bank[4 + b][:].rearrange("p (k m) -> p k m", k=2),
                                       memT_hi[:, 2 * b:2 * b + 2, :].bitcast(F32), SUB).then_inc(mem_lo.sem, mem_lo.up(V))

            def rope(r):
                x = qk[:, r, :] if r < 8 else iq[:, r - 8, :] if r < 12 else ikd[:]
                V.eng.wait_ge(head_sw.sem, head_sw.at(V, r + 1))
                v.tensor_tensor(turned[:], bank[4 + r % 2][:], sinB[:], MUL).then_inc(v_step.sem, v_step.up(V))
                v.tensor_tensor(x, x, cosB[:], MUL).then_inc(v_step.sem, v_step.up(V))
                V.eng.wait_ge(v_step.sem, v_step.last(V))
                v.tensor_tensor(x, x, turned[:], ADD).then_inc(head_rope.sem, head_rope.up(V))
                V.eng.wait_ge(head_rope.sem, head_rope.last(V))

            def pool(g4):
                w, x = 2 << g4, up[:, g4, :]
                V.eng.wait_ge(proj_ev.sem, proj_ev.at(V, g4 + 1))
                cur, sh, k = x, 1, 0
                while sh < w:
                    nxt = work[k % 2]
                    v.tensor_copy(nxt[:, 0:sh], cur[:, 0:sh]).then_inc(v_step.sem, v_step.up(V))
                    v.tensor_tensor(nxt[:, sh:S], cur[:, sh:S], cur[:, 0:S - sh], ADD).then_inc(v_step.sem, v_step.up(V))
                    V.eng.wait_ge(v_step.sem, v_step.last(V))
                    cur, sh, k = nxt, 2 * sh, k + 1
                d = pd[:, g4, :]
                v.scalar_tensor_tensor(d[:, 16:S], cur[:, 16:S], 1.0 / w, x[:, 16:S], MUL, SUB).then_inc(v_step.sem, v_step.up(V))
                v.tensor_tensor(cur[:, 0:16], cur[:, 0:16], konst[:, K_CNT + 16 * g4:K_CNT + 16 * g4 + 16], MUL).then_inc(v_step.sem, v_step.up(V))
                V.eng.wait_ge(v_step.sem, v_step.last(V))
                v.tensor_tensor(d[:, 0:16], cur[:, 0:16], x[:, 0:16], SUB).then_inc(pool_d.sem, pool_d.up(V))
                V.eng.wait_ge(pool_d.sem, pool_d.last(V))

            for g4 in range(4):
                pool(g4)
            for r in range(8):
                rope(r)
            for r in range(8, 12):
                rope(r)
            rope(12)
            V.eng.wait_ge(iw_tr.sem, iw_tr.at(V, 1))
            v.tensor_scalar(flat(iwc), bank[7][:, 0:NT * AH], AH ** -0.5, None, MUL).then_inc(iw_ev.sem, iw_ev.up(V))
            V.eng.wait_ge(iw_ev.sem, iw_ev.last(V))
            for g4 in range(4):
                V.eng.wait_ge(pool_dh.sem, pool_dh.at(V, g4 + 1))
                v.tensor_tensor(b_lo[:, g4, :], pd[:, g4, :], b_hi[:, g4, :].bitcast(F32), SUB).then_inc(pool_dl.sem, pool_dl.up(V))
            for g4 in range(4):
                V.eng.wait_ge(pool_hi.sem, pool_hi.at(V, g4 + 1))
                v.scalar_tensor_tensor(b_lo[:, g4, :], bank[g4][:], col(P_SC + g4), b_hi[:, g4, :].bitcast(F32), MUL, SUB).then_inc(pool_lo.sem, pool_lo.up(V))
            v.memset(mask_of[0], 0.0).then_inc(v_step.sem, v_step.up(V))
            V.eng.wait_ge(v_step.sem, v_step.last(V))
            v.memset(mask_of[0][0:64, 64:P], HIDE).then_inc(v_step.sem, v_step.up(V))
            V.eng.wait_ge(v_step.sem, v_step.last(V))
            for n in range(3 * AH):
                i, hh = 1 + n // AH, n % AH
                acc, w = mask_of[i], iwc[:, i, hh:hh + 1]
                V.eng.wait_ge(ix_rel.sem, ix_rel.at(V, n + 1))
                if hh == 0:
                    v.tensor_scalar(acc, rel[n % 2][:, 0:i * P + P], w, None, MUL).then_inc(ix_use.sem, ix_use.up(V))
                    V.eng.wait_ge(ix_use.sem, ix_use.last(V))
                else:
                    v.scalar_tensor_tensor(acc, rel[n % 2][:, 0:i * P + P], w, acc, MUL, ADD).then_inc(ix_use.sem, ix_use.up(V))
                    V.eng.wait_ge(ix_use.sem, ix_use.last(V))
                if hh == AH - 1:
                    v.memset(acc[0:64, i * P + 64:i * P + P], OUT_OF).then_inc(v_step.sem, v_step.up(V))

            def ranks():
                for x in range(3):
                    V.eng.wait_ge(v_step.sem, V.alone(v_step.last(V, 2)))
                    v.max(st8[x], mask_of[1 + x]).then_inc(v_step.sem, v_step.up(V))
                for x in range(3):
                    V.eng.wait_ge(v_step.sem, V.alone(v_step.last(V, 2)))
                    v.match_replace(mask_of[1 + x], st8[x], mask_of[1 + x], TAKEN).then_inc(v_step.sem, v_step.up(V))

            for n in range(19):
                if n < NSEL // 8:
                    ranks()
                if n < 16:
                    V.eng.wait_ge(m_s.sem, m_s.at(V, n + 1))
                    v.tensor_reduce(mmx2[:, n:n + 1], bank[n % 2][:, 0:NM], AX.X, MAX).then_inc(v_step.sem, v_step.up(V))
                    V.eng.wait_ge(v_step.sem, v_step.last(V))
                    v.tensor_scalar(mmx2[:, n:n + 1], mmx2[:, n:n + 1], -(MHD ** -0.5), None, MUL).then_inc(m_mx.sem, m_mx.up(V))
                if n >= 5 and (n - 5) % 4 == 0 and (n - 5) // 4 < 3 or n == 18:
                    i = (n - 5) // 4 if n < 18 else 3
                    V.eng.wait_ge(m_o.sem, m_o.at(V, 4 * i + 4))
                    v.reciprocal(mrc[:, 0:4], msm2[:, 4 * i:4 * i + 4]).then_inc(v_step.sem, v_step.up(V))
                    V.eng.wait_ge(v_step.sem, v_step.last(V))
                    v.tensor_tensor(om[:, i, :].rearrange("p (g n) -> p g n", g=4), bank[4 + i % 2][:].rearrange("p (g n) -> p g n", g=4),
                                           over(mrc[:, 0:4].unsqueeze(2), [P, 4, P]), MUL).then_inc(m_or.sem, m_or.up(V))
                    V.eng.wait_ge(m_or.sem, m_or.last(V))
            V.eng.wait_ge(v_step.sem, v_step.last(V))
            for i in range(1, NT):
                v.tensor_scalar(mask_of[i], mask_of[i], -2e38, HIDE, ALU.is_gt, MUL).then_inc(v_step.sem, v_step.up(V))
            V.eng.wait_ge(v_step.sem, v_step.last(V))
            for s in range(NT * AH + 4):
                if s < NT * AH:
                    i, nk = s // AH, (s // AH + 1) * P
                    V.eng.wait_ge(at_s.sem, at_s.at(V, s + 1))
                    if s >= 4:
                        V.eng.wait_ge(at_t.sem, at_t.at(V, s - 3))
                    v.scalar_tensor_tensor(sc[s % 4][:, 0:nk], bank[s % 4][:, 0:nk], HD ** -0.5, mask_of[i], MUL, ADD).then_inc(a_sc.sem, a_sc.up(V))
                    V.eng.wait_ge(a_sc.sem, a_sc.last(V))
                    v.tensor_reduce(amx[:, s:s + 1], sc[s % 4][:, 0:nk], AX.X, MAX).then_inc(v_step.sem, v_step.up(V))
                    V.eng.wait_ge(v_step.sem, v_step.last(V))
                    v.tensor_scalar(amx[:, s:s + 1], amx[:, s:s + 1], -1.0, None, MUL).then_inc(at_mx.sem, at_mx.up(V))
                if s >= 2 and (s - 2) % AH == AH - 1:
                    i = (s - 2) // AH
                    V.eng.wait_ge(at_o.sem, at_o.at(V, AH * (i + 1)))
                    v.reciprocal(ars, asum[:, AH * i:AH * i + AH]).then_inc(v_step.sem, v_step.up(V))
                    V.eng.wait_ge(v_step.sem, v_step.last(V))
                    v.tensor_tensor(otok[:].rearrange("p (g n) -> p g n", g=AH), bank[6 + i % 2][:].rearrange("p (g n) -> p g n", g=AH),
                                           over(ars.unsqueeze(2), [P, AH, HD]), MUL).then_inc(a_or.sem, a_or.up(V))
                if s >= 4 and (s - 4) % AH == AH - 1:
                    i = (s - 4) // AH
                    V.eng.wait_ge(a_oh.sem, a_oh.at(V, i + 1))
                    v.tensor_tensor(b_lo[:, 4:8, i * P:i * P + P], bank[6 + i % 2][:].rearrange("p (c n) -> p c n", c=4),
                                           b_hi[:, 4:8, i * P:i * P + P].bitcast(F32), SUB).then_inc(a_ol.sem, a_ol.up(V))
            for i in range(NT):
                V.eng.wait_ge(m_oh.sem, m_oh.at(V, i + 1))
                v.tensor_tensor(bm_lo[:, :, i * P:i * P + P], bank[6 + i % 2][:].rearrange("p (c n) -> p c n", c=4),
                                       b_hi[:, 8:12, i * P:i * P + P].bitcast(F32), SUB).then_inc(m_ol.sem, m_ol.up(V))
            V.eng.wait_ge(m_ol.sem, V.alone(m_ol.last(V)))
            with v.Fori(0, 4) as i:
                V.loop("v_gates", i)
                for u6 in range(6):
                    n, dd = u6 % 3, u6 // 3
                    m = qk[:, bass.ds(i * 2 + dd, 1), :]
                    V.eng.wait_ge(gt_sig.sem, gt_sig.at(V, i * 6 + (u6 + 1)))
                    V.eng.wait_ge(ring.done, ring.products(V, U2_G + 2 * u6 + 1, turn=i, size=12))
                    br = bank[2 * (u6 % 2) + 1][:].unsqueeze(1)
                    if n == 0:
                        v.tensor_tensor(m, sg[u6 % 2][:].unsqueeze(1), br, MUL).then_inc(gt_use.sem, gt_use.up(V))
                        V.eng.wait_ge(gt_use.sem, gt_use.last(V))
                    else:
                        v.tensor_tensor(gt[:].unsqueeze(1), sg[u6 % 2][:].unsqueeze(1), br, MUL).then_inc(v_step.sem, v_step.up(V))
                        V.eng.wait_ge(v_step.sem, v_step.last(V))
                        v.tensor_tensor(m, m, gt[:].unsqueeze(1), ADD).then_inc(gt_use.sem, gt_use.up(V))
                        V.eng.wait_ge(gt_use.sem, gt_use.last(V))
                V.loop_end(4)
            for k in range(KC):
                V.eng.wait_ge(mg_hi.sem, mg_hi.at(V, k + 1))
                v.tensor_tensor(xT_lo[:, k, :], qk[:, k, :], xT_hi[:, k, :].bitcast(F32), SUB).then_inc(mg_lo.sem, mg_lo.up(V))
            norm_v(V, 0, U2_OUT + KC - 1)
            V.eng.wait_ge(rt_tr.sem, rt_tr.at(V, 1))
            v.tensor_copy(flat(rsc[:]), bank[2][:, 0:NT * NE]).then_inc(v_step.sem, v_step.up(V))
            V.eng.wait_ge(v_step.sem, v_step.last(V))
            V.eng.wait_ge(rb_ld.sem, rb_ld.at(V, 2))
            v.tensor_tensor(rbi[:], rsc[:], over(rbias[:].unsqueeze(1), [P, NT, NE]), ADD).then_inc(v_step.sem, v_step.up(V))
            V.eng.wait_ge(v_step.sem, v_step.last(V))
            b4 = flat(rbi[:]).rearrange("p (g x) -> p g x", x=4)
            tm = rtm[:].rearrange("p i g x -> p (i g) x")
            e = lambda k: b4[:, :, k:k + 1]
            f = lambda k: tm[:, :, k:k + 1]
            for o, a, b, op in ((0, e(0), e(1), MAX), (1, e(0), e(1), MIN), (2, e(2), e(3), MAX), (3, e(2), e(3), MIN)):
                v.tensor_tensor(f(o), a, b, op).then_inc(v_step.sem, v_step.up(V))
            V.eng.wait_ge(v_step.sem, v_step.last(V))
            v.tensor_tensor(f(4), f(0), f(2), MAX).then_inc(v_step.sem, v_step.up(V))
            v.tensor_tensor(f(5), f(0), f(2), MIN).then_inc(v_step.sem, v_step.up(V))
            v.tensor_tensor(f(6), f(1), f(3), MAX).then_inc(v_step.sem, v_step.up(V))
            V.eng.wait_ge(v_step.sem, v_step.last(V))
            v.tensor_tensor(f(5), f(5), f(6), MAX).then_inc(v_step.sem, v_step.up(V))
            V.eng.wait_ge(v_step.sem, v_step.last(V))
            v.tensor_tensor(rgs[:], rtm[:, :, :, 4], rtm[:, :, :, 5], ADD).then_inc(v_step.sem, v_step.up(V))
            V.eng.wait_ge(v_step.sem, v_step.last(V))

            def first_best(hot, src, n):
                v.tensor_reduce(rbest[:, :, 0:1], src, AX.X, MAX).then_inc(v_step.sem, v_step.up(V))
                V.eng.wait_ge(v_step.sem, v_step.last(V))
                v.tensor_tensor(hot, src, over(rbest[:, :, 0:1], [P, NT, n]), ALU.is_equal).then_inc(v_step.sem, v_step.up(V))
                V.eng.wait_ge(v_step.sem, v_step.last(V))
                v.tensor_tensor(hot, hot, over(konst[:, K_REV:K_REV + n].unsqueeze(1), [P, NT, n]), MUL).then_inc(v_step.sem, v_step.up(V))
                V.eng.wait_ge(v_step.sem, v_step.last(V))
                v.tensor_reduce(rbest[:, :, 0:1], hot, AX.X, MAX).then_inc(v_step.sem, v_step.up(V))
                V.eng.wait_ge(v_step.sem, v_step.last(V))
                v.tensor_tensor(hot, hot, over(rbest[:, :, 0:1], [P, NT, n]), ALU.is_equal).then_inc(v_step.sem, v_step.up(V))
                V.eng.wait_ge(v_step.sem, v_step.last(V))

            first_best(ghot[:], rgs[:], NG)
            v.tensor_scalar(rgs[:], ghot[:], 1.0, -HIDE, SUB, MUL).then_inc(v_step.sem, v_step.up(V))
            V.eng.wait_ge(v_step.sem, v_step.last(V))
            x4 = lambda a: a.rearrange("p i (g x) -> p i g x", x=4)
            v.tensor_tensor(x4(rbi[:]), x4(rbi[:]), over(ghot[:].unsqueeze(3), [P, NT, NG, 4]), MUL).then_inc(v_step.sem, v_step.up(V))
            V.eng.wait_ge(v_step.sem, v_step.last(V))
            v.tensor_tensor(x4(rbi[:]), x4(rbi[:]), over(rgs[:].unsqueeze(3), [P, NT, NG, 4]), ADD).then_inc(v_step.sem, v_step.up(V))
            V.eng.wait_ge(v_step.sem, v_step.last(V))
            first_best(oh[:, 0, :, :], rbi[:], NE)
            v.scalar_tensor_tensor(rbi[:], oh[:, 0, :, :], 2 * HIDE, rbi[:], MUL, ADD).then_inc(v_step.sem, v_step.up(V))
            V.eng.wait_ge(v_step.sem, v_step.last(V))
            first_best(oh[:, 1, :, :], rbi[:], NE)
            v.tensor_tensor(oh[:, 2, :, :], oh[:, 0, :, :], oh[:, 1, :, :], ADD).then_inc(rt_oh.sem, rt_oh.up(V))
            V.eng.wait_ge(rt_oh.sem, rt_oh.last(V))
            for a in range(2):
                v.tensor_tensor(rtmp[:], rsc[:], oh[:, a, :, :], MUL).then_inc(v_step.sem, v_step.up(V))
                V.eng.wait_ge(v_step.sem, v_step.last(V))
                v.tensor_reduce(gw[:, :, a:a + 1], rtmp[:], AX.X, ADD).then_inc(v_step.sem, v_step.up(V))
                V.eng.wait_ge(v_step.sem, v_step.last(V))
            v.tensor_tensor(gw[:, :, 2:3], gw[:, :, 0:1], gw[:, :, 1:2], ADD).then_inc(v_step.sem, v_step.up(V))
            V.eng.wait_ge(v_step.sem, v_step.last(V))
            v.reciprocal(gw[:, :, 2:3], gw[:, :, 2:3]).then_inc(v_step.sem, v_step.up(V))
            V.eng.wait_ge(v_step.sem, v_step.last(V))
            v.tensor_tensor(gw[:, :, 0:2], gw[:, :, 0:2], over(gw[:, :, 2:3], [P, NT, 2]), MUL).then_inc(v_step.sem, v_step.up(V))
            V.eng.wait_ge(v_step.sem, v_step.last(V))
            V.eng.wait_ge(rt_rank.sem, rt_rank.at(V, 1))
            rank = bank[1][:, 0:NT * NE].rearrange("p (i e) -> p i e", i=NT)
            v.tensor_copy(rbi[:], bank[1][:, NT * NE:2 * NT * NE].rearrange("p (i e) -> p i e", i=NT)).then_inc(v_step.sem, v_step.up(V))
            V.eng.wait_ge(v_step.sem, v_step.last(V))
            for i in range(1, NT):
                v.tensor_tensor(rbi[:, i, :], rbi[:, i, :], rbi[:, i - 1, :], ADD).then_inc(v_step.sem, v_step.up(V))
                V.eng.wait_ge(v_step.sem, v_step.last(V))
            cnt = rbi[:, NT - 1, :]
            v.tensor_scalar(nblk[:], cnt, 0.5, None, ALU.is_gt).then_inc(v_step.sem, v_step.up(V))
            V.eng.wait_ge(v_step.sem, v_step.last(V))
            for k in range(1, NT):
                v.scalar_tensor_tensor(nblk[:], cnt, P * k + 0.5, nblk[:], ALU.is_gt, ADD).then_inc(v_step.sem, v_step.up(V))
                V.eng.wait_ge(v_step.sem, v_step.last(V))
            v.tensor_tensor_scan(pend[:], ones[:, 0:NE], nblk[:], 0.0, MUL, ADD).then_inc(v_step.sem, v_step.up(V))
            V.eng.wait_ge(v_step.sem, v_step.last(V))
            v.tensor_copy(pace[:, 0:1], pace[:, 1:2]).then_inc(v_step.sem, v_step.up(V))
            v.tensor_scalar(used[:], konst[:, K_BNO:K_BNO + NB:2], pend[:, NE - 1:NE], None, ALU.is_lt).then_inc(v_step.sem, v_step.up(V))
            v.tensor_tensor(bst[:], pend[:], nblk[:], SUB).then_inc(v_step.sem, v_step.up(V))
            V.eng.wait_ge(v_step.sem, v_step.last(V))
            v.tensor_reduce(turns[:], used[:], AX.X, ADD).then_inc(v_step.sem, v_step.up(V))
            V.eng.wait_ge(v_step.sem, v_step.last(V))
            v.tensor_copy(pace[:, 1:2], turns[:]).then_inc(v_step.sem, v_step.up(V))
            V.eng.wait_ge(v_step.sem, v_step.last(V))
            v.tensor_tensor(bcmp[:], over(pend[:].unsqueeze(1), [P, NB + 1, NE]),
                                   over(konst[:, K_BNO:K_BNO + NB + 1].unsqueeze(2), [P, NB + 1, NE]), ALU.is_le).then_inc(v_step.sem, v_step.up(V))
            V.eng.wait_ge(v_step.sem, v_step.last(V))
            v.tensor_reduce(bef[:], bcmp[:], AX.X, ADD).then_inc(v_step.sem, v_step.up(V))
            V.eng.wait_ge(v_step.sem, v_step.last(V))
            v.tensor_scalar(bei[:], bef[:], NE - 1.0, None, MIN).then_inc(be_ok.sem, be_ok.up(V))
            V.eng.wait_ge(be_ok.sem, be_ok.last(V))
            v.tensor_scalar(bst[:], bst[:], float(P), -1.0, MUL, ADD).then_inc(v_step.sem, v_step.up(V))
            V.eng.wait_ge(v_step.sem, v_step.last(V))
            v.tensor_tensor(rtmp[:], rank, over(bst[:].unsqueeze(1), [P, NT, NE]), ADD).then_inc(v_step.sem, v_step.up(V))
            V.eng.wait_ge(v_step.sem, v_step.last(V))
            v.tensor_tensor(rtmp[:, 1:NT, :], rtmp[:, 1:NT, :], rbi[:, 0:NT - 1, :], ADD).then_inc(v_step.sem, v_step.up(V))
            V.eng.wait_ge(v_step.sem, v_step.last(V))
            for a in range(2):
                v.tensor_tensor(hot2[:], rtmp[:], oh[:, a, :, :], MUL).then_inc(v_step.sem, v_step.up(V))
                V.eng.wait_ge(v_step.sem, v_step.last(V))
                v.tensor_reduce(dest[:, a, :], hot2[:], AX.X, ADD).then_inc(v_step.sem, v_step.up(V))
                V.eng.wait_ge(v_step.sem, v_step.last(V))
            v.tensor_copy(desti[:], dest[:]).then_inc(v_step.sem, v_step.up(V))
            d8 = dest[:].rearrange("p a i -> p (a i)")
            v.tensor_scalar(d128[:], d8, 1.0 / P, None, MUL).then_inc(v_step.sem, v_step.up(V))
            V.eng.wait_ge(v_step.sem, v_step.last(V))
            v.tensor_tensor(slot_ge[:], over(d128[:].unsqueeze(2), [P, 2 * NT, NB + 2]),
                                   over(row128[:, 0:NB + 2].unsqueeze(1), [P, 2 * NT, NB + 2]), ALU.is_ge).then_inc(v_step.sem, v_step.up(V))
            V.eng.wait_ge(v_step.sem, v_step.last(V))
            v.tensor_tensor(slot_b[:], slot_ge[:, :, 0:NB + 1], slot_ge[:, :, 1:NB + 2], SUB).then_inc(v_step.sem, v_step.up(V))
            v.tensor_reduce(d128[:], slot_ge[:], AX.X, ADD).then_inc(v_step.sem, v_step.up(V))
            V.eng.wait_ge(v_step.sem, v_step.last(V))
            v.tensor_scalar(d128[:], d128[:], -float(P), float(P), MUL, ADD).then_inc(v_step.sem, v_step.up(V))
            V.eng.wait_ge(v_step.sem, v_step.last(V))
            v.tensor_tensor(d128[:], d128[:], d8, ADD).then_inc(v_step.sem, v_step.up(V))
            V.eng.wait_ge(v_step.sem, v_step.last(V))
            for a in range(2):
                v.tensor_tensor(slot_b[:, NT * a:NT * a + NT, :], slot_b[:, NT * a:NT * a + NT, :],
                                       over(konst[:, K_TOK:K_TOK + NT].unsqueeze(2), [P, NT, NB + 1]), MUL).then_inc(v_step.sem, v_step.up(V))
            v.tensor_tensor(slot_p[:], over(d128[:].unsqueeze(2), [P, 2 * NT, P]),
                                   over(row128[:].unsqueeze(1), [P, 2 * NT, P]), ALU.is_equal).then_inc(slot_oh.sem, slot_oh.up(V))
            V.eng.wait_ge(slot_oh.sem, slot_oh.last(V))
            V.eng.wait_ge(slot_mm.sem, slot_mm.at(V, 1))
            v.tensor_copy(slots[:], bank[3][:, 0:NB + 1]).then_inc(rt_dest.sem, rt_dest.up(V))
            V.eng.wait_ge(rt_dest.sem, V.alone(rt_dest.last(V)))
            V.pace(pace)
            with v.Fori(0, NB // 2) as bb:
                V.loop("v_moe", bb)
                with V.eng.If(bb < V.turns):
                    for q in range(2):
                        V.eng.wait_ge(act_h.sem, act_h.at(V, bb * 2 + (q + 1)))
                        V.eng.wait_ge(wt_done.sem, wt_done.at(V, bb * 12 + (6 * q + 4)))
                        v.tensor_tensor(hs[:], hs[:], bank[3][:], MUL).then_inc(h_val.sem, h_val.up(V))
                        V.eng.wait_ge(h_val.sem, h_val.last(V))
                        V.eng.wait_ge(y_free.sem, y_free.at(V, bb * 2 + (q - 1)))
                        V.eng.wait_ge(wt_done.sem, wt_done.at(V, bb * 12 + (6 * q + 6)))
                        for x in range(2):
                            v.tensor_copy(yb[q][:, x * S:x * S + S], bank[5 + x][:]).then_inc(y_ev.sem, y_ev.up(V))
                V.loop_end(NB // 2)
            def experts_added(i):
                a, b = yg[(2 * i) % 4], yg[(2 * i + 1) % 4]
                V.eng.wait_ge(ygl[(2 * i) % 4].sem, ygl[(2 * i) % 4].at(V, i // 2 + 1))
                V.eng.wait_ge(ygl[(2 * i + 1) % 4].sem, ygl[(2 * i + 1) % 4].at(V, i // 2 + 1))
                v.tensor_scalar(a[:], a[:], gw[:, i, 0:1], None, MUL).then_inc(v_step.sem, v_step.up(V))
                V.eng.wait_ge(v_step.sem, v_step.last(V))
                v.scalar_tensor_tensor(a[:], b[:], gw[:, i, 1:2], a[:], MUL, ADD).then_inc(yg_use.sem, yg_use.up(V))
                V.eng.wait_ge(yg_use.sem, yg_use.last(V))
                v.scalar_tensor_tensor(h[:, i, :], h[:, i, :], ALPHA, a[:], MUL, ADD).then_inc(yg_use.sem, yg_use.up(V))
                V.eng.wait_ge(yg_use.sem, yg_use.last(V))

            norm_v(V, 1, None, experts_added)

        def finish(E):
            for n in range(NT):
                E.eng.wait_ge(norm_z.sem, norm_z.at(E, NT + n + 1))
                E.eng.dma_start(out[0, n * P:n * P + P, :], h[:, n, :]).then_inc(stored, 16)
            E.eng.wait_ge(stored, 16 * NT)
            E.eng.wait_ge(h_st.sem, h_st.at(E, NT))

        TWO_PI = 6.283185307179586
        C1, C2, C3 = 6.28125, 0.0019350051879882812, 3.019916050501e-07
        MAGIC = 12582912.0
        HALF_PI, PI_BELOW = TWO_PI / 4, 3.1415925
        x_rows = t["x"].rearrange("o (i p) d -> (o p) i d", p=P)

        def loads0(E):
            sp = E.eng
            sp.dma_start(konst[:], t["konst"][:, 0:K_END]).then_inc(ld.sem, ld.up(E))
            for k, name in enumerate(("positions", "positions_2")):
                sp.dma_start(proj[:, k, :].bitcast(I32), over(t[name], [P, S])).then_inc(ld.sem, ld.up(E))
            for i in range(NT):
                sp.dma_start(h[:, i, :], x_rows[:, i, :]).then_inc(ld.sem, ld.up(E))

        def gpsimd0(G):
            g = G.eng
            g.nop().then_inc(began, 1)
            g.memset(small[:, 0:1], EPS).then_inc(set_up.sem, set_up.up(G))
            g.memset(small[:, 1:2], 1.0).then_inc(set_up.sem, set_up.up(G))
            g.memset(mean_of[:], 1.0 / W).then_inc(set_up.sem, set_up.up(G))
            g.memset(ones[:], 1.0).then_inc(set_up.sem, set_up.up(G))
            g.memset(pace[:], 0).then_inc(set_up.sem, set_up.up(G))
            g.memset(gaup[:], 0.0).then_inc(set_up.sem, set_up.up(G))
            g.memset(zeros[:], 0.0).then_inc(set_up.sem, set_up.up(G))
            G.eng.wait_ge(set_up.sem, set_up.last(G))
            ring.prime(g, None)
            for _ in range(2):
                g.nop().then_inc(y_free.sem, y_free.up(G))

        def tensor0(T):
            ring.prime(None, T.eng)
            for free in [wt_done] * 6 + [x_tr, h_tr]:
                T.eng.nop().then_inc(free.sem, free.up(T))
            T.eng.wait_ge(ld.sem, ld.at(T, 7))
            T.eng.wait_ge(set_up.sem, set_up.at(T, 7))
            norm_pe(T, 0)

        def scalar0(A):
            load_gb(A, t["ln_in_g"].rearrange("(o n) -> o n", o=1), t["ln_in_b"].rearrange("(o n) -> o n", o=1))
            A.eng.wait_ge(set_up.sem, set_up.at(A, 7))
            norm_a(A, 0)
            for n, tab in enumerate((sinA, cosA, sinB, cosB)):
                A.eng.wait_ge(tab_arg.sem, tab_arg.at(A, n + 1))
                A.eng.activation(tab[:], tab[:], ACT.Sin).then_inc(tab_sin.sem, tab_sin.up(A))
                A.eng.wait_ge(tab_sin.sem, tab_sin.last(A))

        def vector0(V):
            v = V.eng
            for free in (y_ev, gt_use, gt_use):
                v.nop().then_inc(free.sem, free.up(V))
            V.eng.wait_ge(ld.sem, ld.at(V, 7))
            V.eng.wait_ge(set_up.sem, set_up.at(V, 7))
            norm_v(V, 0, None)
            for k, (sin, cos) in enumerate(((sinA, cosA), (sinB, cosB))):
                ang, cyc, posi = proj[:, 4, :], proj[:, 5, :], proj[:, k, :].bitcast(I32)
                v.tensor_copy(ang, posi).then_inc(v_step.sem, v_step.up(V))
                V.eng.wait_ge(v_step.sem, v_step.last(V))
                v.tensor_scalar(ang, ang, konst[:, K_FREQ + 2 * k:K_FREQ + 2 * k + 1], None, MUL).then_inc(v_step.sem, v_step.up(V))
                V.eng.wait_ge(v_step.sem, v_step.last(V))
                for tab, quarter in ((sin, 0.0), (cos, 0.25)):
                    v.tensor_scalar(cyc, ang, 1.0 / TWO_PI, quarter, MUL, ADD).then_inc(v_step.sem, v_step.up(V))
                    V.eng.wait_ge(v_step.sem, v_step.last(V))
                    v.tensor_scalar(cyc, cyc, MAGIC, MAGIC, ADD, SUB).then_inc(v_step.sem, v_step.up(V))
                    V.eng.wait_ge(v_step.sem, v_step.last(V))
                    v.scalar_tensor_tensor(tab[:], cyc, -C1, ang, MUL, ADD).then_inc(v_step.sem, v_step.up(V))
                    V.eng.wait_ge(v_step.sem, v_step.last(V))
                    v.scalar_tensor_tensor(tab[:], cyc, -C2, tab[:], MUL, ADD).then_inc(v_step.sem, v_step.up(V))
                    V.eng.wait_ge(v_step.sem, v_step.last(V))
                    v.scalar_tensor_tensor(tab[:], cyc, -C3, tab[:], MUL, ADD).then_inc(v_step.sem, v_step.up(V))
                    V.eng.wait_ge(v_step.sem, v_step.last(V))
                    v.tensor_scalar(tab[:], tab[:], HALF_PI if quarter else 0.0, PI_BELOW, ADD, MIN).then_inc(v_step.sem, v_step.up(V))
                    V.eng.wait_ge(v_step.sem, v_step.last(V))
                    v.tensor_scalar(tab[:], tab[:], -PI_BELOW, None, MAX).then_inc(tab_arg.sem, tab_arg.up(V))
                    V.eng.wait_ge(tab_arg.sem, tab_arg.last(V))
            for k, sin in enumerate((sinA, sinB)):
                V.eng.wait_ge(tab_sin.sem, tab_sin.at(V, 2 * k + 1))
                v.tensor_scalar(sin[:], sin[:], konst[:, K_FREQ + 2 * k + 1:K_FREQ + 2 * k + 2], None, MUL).then_inc(v_step.sem, v_step.up(V))
                V.eng.wait_ge(v_step.sem, v_step.last(V))
            V.eng.wait_ge(tab_sin.sem, tab_sin.at(V, 4))

        stages = {
            "sync": (loads0, loads1, loads2), "gpsimd": (gpsimd0, splits1, splits2),
            "tensor": (tensor0, tensor1, tensor2), "scalar": (scalar0, scalar1, scalar2),
            "vector": (vector0, vector1, vector2),
        }

        def program(E, name):
            before, block1, block2 = stages[name]
            before(E)
            E.leave()
            for number, body in ((1, block1), (2, block2)):
                if body is None:
                    continue
                with E.eng.Fori(0, L) as l:
                    E.enter(number, l)
                    body(E)
                    E.leave()
            E.enter(2, L - 1)

        @block.sync
        def _(sp):
            E = Lane(sp, began)
            program(E, "sync")
            finish(E)

        @block.gpsimd
        def _(pool):
            program(Lane(pool, began), "gpsimd")

        @block.tensor
        def _(pe):
            program(Lane(pe, began), "tensor")

        @block.scalar
        def _(act):
            program(Lane(act, began), "scalar")

        @block.vector
        def _(dve):
            program(Lane(dve, began), "vector")


INPUTS = [
    "x", "positions", "ln_in_g", "ln_in_b", "w_in", "w_sc_conv", "w_gla_a_up", "b_gla_a", "g_gla_head", "g_mla_q",
    "w_mla_uq", "g_mla_kv", "w_mla_ukv", "w_cfm_dw", "g_cfm_ln", "b_cfm_ln", "g_branch", "w_out", "ln1_g", "ln1_b",
    "w_ffn_up", "w_ffn_dw", "w_ffn_down", "ln2_g", "ln2_b", "mem_2", "positions_2", "w_in_2", "b_in_2", "pool_w_2",
    "pool_scale_2", "w_mem_kv_2", "w_br_2", "w_out_2", "ln1_g_2", "ln1_b_2", "w_router_2", "router_bias_2",
    "w1_2", "w3_2", "w2_2", "ln2_g_2", "ln2_b_2",
]


def kernel(**inputs):
    import numpy as np
    import concourse.bacc as bacc
    from concourse.bass_utils import run_bass_kernel_spmd

    nc = bacc.Bacc("TRN2", target_bir_lowering=False, num_devices=1)
    arrays, t = {}, {}
    for name in INPUTS + ["konst"]:
        a = shape_constants() if name == "konst" else np.ascontiguousarray(inputs[name])
        arrays[f"in_{name}"] = a
        t[name] = nc.dram_tensor(f"in_{name}", a.shape, mybir.dt.from_np(a.dtype), kind="ExternalInput").ap()
    out = nc.dram_tensor("out_h", (1, S, D), F32, kind="ExternalOutput").ap()
    build(nc, t, out)
    r = run_bass_kernel_spmd(nc, [arrays], core_ids=[0])
    return r.results[0]["out_h"]
```
